# Optimizing a Trainium2 kernel written in Bass

```python
import math
import jax, jax.numpy as jnp
from jax import lax
import numpy as np

D_MODEL = 1024
BATCH = 1
SEQ = 256
DEPTH = 1
DEC_BATCH = 8
DEC_SEQ = 1
PAST_LEN = 1024
PAGE_SIZE = 128

GDN_HEADS = 8
GDN_DK = 64
GDN_DV = 64
GDN_CONV = 4
GDN_CHUNK = 64
GDN_QKV = 2 * GDN_HEADS * GDN_DK + GDN_HEADS * GDN_DV
DSA_HEADS = 8
DSA_KV_HEADS = 4
DSA_DH = 64
IDX_HEADS = 4
IDX_DIM = 64
TOPK_MAX = 256
Q_BLOCK = 128
MEM_LEN = 256
MEM_HEADS = 4
MEM_DH = 128
N_BRANCH = 3
BRANCH_W = 512
N_EXPERTS = 32
TOP_K = 4
D_FF = 1024
SWIGLU_LIMIT = 7.0
SWIGLU_ALPHA = 1.702
MOE_BLOCK = 128
EPS = 1e-6

SPLITS = (GDN_QKV, GDN_HEADS * GDN_DV, GDN_HEADS, GDN_HEADS,
          DSA_HEADS * DSA_DH, DSA_KV_HEADS * DSA_DH, DSA_KV_HEADS * DSA_DH,
          IDX_HEADS * IDX_DIM, IDX_DIM, IDX_HEADS,
          MEM_HEADS * MEM_DH, N_BRANCH * D_MODEL)
D_IN = sum(SPLITS)

kernel_name = "hybrid_gdn_dsa_mem_moe_step"

F32 = jnp.float32

def rms_norm(x, g):
    xf = x.astype(F32)
    y = xf * lax.rsqrt(jnp.mean(xf * xf, axis=-1, keepdims=True) + EPS)
    return (y * g.astype(F32)).astype(x.dtype)

def l2_norm(x):
    xf = x.astype(F32)
    return xf * lax.rsqrt(jnp.sum(xf * xf, axis=-1, keepdims=True) + EPS)

def heads(a, n, d):
    return a.reshape(*a.shape[:-1], n, d)

def in_proj(x, norm_g, w_in):
    h = rms_norm(x, norm_g)
    cuts = [int(c) for c in np.cumsum(SPLITS)[:-1]]
    return jnp.split(h @ w_in, cuts, axis=-1)

def causal_conv(x, conv_state, w):
    T = x.shape[1]
    xc = jnp.concatenate([conv_state.astype(x.dtype), x], axis=1)
    y = sum(w[i] * xc[:, i:i + T] for i in range(GDN_CONV))
    return jax.nn.silu(y), xc[:, T:]

def gdn_chunked(q, k, v, beta, g):
    B, T, H, DK = q.shape
    DV = v.shape[-1]
    C = GDN_CHUNK
    N = T // C

    def chunks(a):
        a = a.reshape(B, N, C, H, *a.shape[3:])
        return jnp.moveaxis(a, (1, 3), (0, 2))

    q, k, v, beta, g = chunks(q), chunks(k), chunks(v), chunks(beta), chunks(g)
    G = jnp.cumsum(g, axis=-1)
    incl = jnp.tril(jnp.ones((C, C), bool))
    strict = jnp.tril(jnp.ones((C, C), bool), -1)
    gamma = jnp.exp(jnp.where(incl, G[..., :, None] - G[..., None, :], -jnp.inf))
    kb = k * beta[..., None]
    m = jnp.where(strict, jnp.einsum('nbhcd,nbhed->nbhce', kb, k) * gamma, 0.0)
    a_mat = m + jnp.eye(C, dtype=m.dtype)
    rhs = jnp.concatenate([v * beta[..., None], kb * jnp.exp(G)[..., None]], axis=-1)
    sol = lax.linalg.triangular_solve(a_mat, rhs, left_side=True, lower=True, unit_diagonal=True)
    u, w = sol[..., :DV], sol[..., DV:]
    qk = jnp.einsum('nbhcd,nbhed->nbhce', q, k) * gamma
    qg = q * jnp.exp(G)[..., None]
    kd = k * jnp.exp(G[..., -1:] - G)[..., None]
    decay_last = jnp.exp(G[..., -1])

    def step(S, xs):
        qg_c, kd_c, u_c, w_c, qk_c, d_c = xs
        vn = u_c - jnp.einsum('bhck,bhkv->bhcv', w_c, S)
        o = jnp.einsum('bhck,bhkv->bhcv', qg_c, S) + jnp.einsum('bhce,bhev->bhcv', qk_c, vn)
        S = S * d_c[..., None, None] + jnp.einsum('bhck,bhcv->bhkv', kd_c, vn)
        return S, o

    S0 = jnp.zeros((B, H, DK, DV), F32)
    S, o = lax.scan(step, S0, (qg, kd, u, w, qk, decay_last))
    o = jnp.moveaxis(o, (0, 2), (1, 3)).reshape(B, T, H, DV)
    return o, S

def gdn_recurrent(q, k, v, beta, g, S0):
    def step(S, xs):
        qt, kt, vt, bt, gt = xs
        S = S * jnp.exp(gt)[..., None, None]
        vn = bt[..., None] * (vt - jnp.einsum('bhk,bhkv->bhv', kt, S))
        S = S + jnp.einsum('bhk,bhv->bhkv', kt, vn)
        return S, jnp.einsum('bhk,bhkv->bhv', qt, S)

    xs = tuple(jnp.moveaxis(a, 1, 0) for a in (q, k, v, beta, g))
    S, o = lax.scan(step, S0.astype(F32), xs)
    return jnp.moveaxis(o, 0, 1), S

def gdn_branch(qkv, z, b, a, conv_state, ssm_state, conv_w, a_log, dt_bias, norm_w):
    B, T, _ = qkv.shape
    y, new_conv = causal_conv(qkv, conv_state, conv_w)
    q, k, v = jnp.split(y, [GDN_HEADS * GDN_DK, 2 * GDN_HEADS * GDN_DK], axis=-1)
    q = l2_norm(heads(q, GDN_HEADS, GDN_DK)) * GDN_DK ** -0.5
    k = l2_norm(heads(k, GDN_HEADS, GDN_DK))
    v = heads(v, GDN_HEADS, GDN_DV).astype(F32)
    beta = jax.nn.sigmoid(b.astype(F32))
    g = -jnp.exp(a_log.astype(F32)) * jax.nn.softplus(a.astype(F32) + dt_bias.astype(F32))
    if ssm_state is None:
        o, S = gdn_chunked(q, k, v, beta, g)
    else:
        o, S = gdn_recurrent(q, k, v, beta, g, ssm_state)
    o = rms_norm(o, norm_w) * jax.nn.silu(heads(z, GDN_HEADS, GDN_DV).astype(F32))
    return o.reshape(B, T, -1).astype(qkv.dtype), new_conv, S

def index_scores(qi, ki, wi):
    s = jnp.einsum('bthd,bld->bthl', qi.astype(F32), ki.astype(F32))
    wt = wi.astype(F32) * (IDX_HEADS ** -0.5 * IDX_DIM ** -0.5)
    return jnp.einsum('bthl,bth->btl', jax.nn.relu(s), wt)

def sparse_attend(q, ksel, vsel, valid):
    B, T = q.shape[:2]
    qg = q.reshape(B, T, DSA_KV_HEADS, DSA_HEADS // DSA_KV_HEADS, DSA_DH)
    s = jnp.einsum('btkgd,btnkd->btkgn', qg, ksel).astype(F32) * DSA_DH ** -0.5
    s = jnp.where(valid[:, :, None, None, :], s, -jnp.inf)
    p = jax.nn.softmax(s, axis=-1).astype(vsel.dtype)
    o = jnp.einsum('btkgn,btnkd->btkgd', p, vsel)
    return o.reshape(B, T, DSA_HEADS * DSA_DH)

def _rows(a, i):
    return a[i]

gather_rows = jax.vmap(_rows)

def dsa_prompt(q, k, v, qi, ki, wi):
    B, S = q.shape[:2]
    n_sel = min(TOPK_MAX, S // 4)
    spos = jnp.arange(S)

    def block(t0):
        qb = lax.dynamic_slice_in_dim(q, t0, Q_BLOCK, axis=1)
        qib = lax.dynamic_slice_in_dim(qi, t0, Q_BLOCK, axis=1)
        wib = lax.dynamic_slice_in_dim(wi, t0, Q_BLOCK, axis=1)
        tpos = t0 + jnp.arange(Q_BLOCK)
        sc = index_scores(qib, ki, wib)
        sc = jnp.where(spos[None, None, :] <= tpos[None, :, None], sc, -jnp.inf)
        _, idx = lax.top_k(sc, n_sel)
        valid = idx <= tpos[None, :, None]
        return sparse_attend(qb, gather_rows(k, idx), gather_rows(v, idx), valid)

    out = lax.map(block, jnp.arange(S // Q_BLOCK) * Q_BLOCK)
    return jnp.moveaxis(out, 0, 1).reshape(B, S, -1)

def dsa_sample(q, k, v, qi, ki, wi, cache_k, cache_v, cache_ki, page_table, layer):
    Bd, T = q.shape[:2]
    n_pages = page_table.shape[1]
    past = n_pages * PAGE_SIZE
    L = past + T
    n_sel = min(TOPK_MAX, L // 4)
    ki_past = cache_ki[layer, page_table].reshape(Bd, past, IDX_DIM)
    ki_all = jnp.concatenate([ki_past.astype(ki.dtype), ki], axis=1)
    tpos = past + jnp.arange(T)
    sc = index_scores(qi, ki_all, wi)
    sc = jnp.where(jnp.arange(L)[None, None, :] <= tpos[None, :, None], sc, -jnp.inf)
    _, idx = lax.top_k(sc, n_sel)
    valid = idx <= tpos[None, :, None]
    in_past = (idx < past)[..., None, None]
    pidx = jnp.minimum(idx, past - 1)
    phys = page_table[jnp.arange(Bd)[:, None, None], pidx // PAGE_SIZE]
    off = pidx % PAGE_SIZE
    nidx = jnp.clip(idx - past, 0, T - 1)
    ksel = jnp.where(in_past, cache_k[layer, phys, off].astype(k.dtype), gather_rows(k, nidx))
    vsel = jnp.where(in_past, cache_v[layer, phys, off].astype(v.dtype), gather_rows(v, nidx))
    return sparse_attend(q, ksel, vsel, valid)

def mem_kv(mem, norm_g, w_kv):
    B, M = mem.shape[:2]
    kv = rms_norm(mem, norm_g) @ w_kv
    mk, mv = jnp.split(kv, 2, axis=-1)
    return heads(mk, MEM_HEADS, MEM_DH), heads(mv, MEM_HEADS, MEM_DH)

def mem_attend(q, mk, mv):
    B, T = q.shape[:2]
    qh = heads(q, MEM_HEADS, MEM_DH)
    s = jnp.einsum('bthd,bmhd->bthm', qh, mk.astype(q.dtype)).astype(F32) * MEM_DH ** -0.5
    p = jax.nn.softmax(s, axis=-1).astype(q.dtype)
    return jnp.einsum('bthm,bmhd->bthd', p, mv.astype(q.dtype)).reshape(B, T, -1)

def merge_out(x, o_gdn, o_dsa, o_mem, gates, w_branch, w_out):
    B, T, _ = x.shape
    br = jnp.einsum('nbtc,ncd->nbtd', jnp.stack([o_gdn, o_dsa, o_mem]), w_branch)
    gt = jax.nn.sigmoid(gates.reshape(B, T, N_BRANCH, D_MODEL).astype(F32)).astype(x.dtype)
    merged = jnp.einsum('btnd,nbtd->btd', gt, br)
    return x + merged @ w_out

def moe(h, w_router, b_router, w_gu, b_gu, w_dn, b_dn):
    shp = h.shape
    x = h.reshape(-1, D_MODEL)
    N = x.shape[0]
    NK = N * TOP_K
    logits = (x @ w_router + b_router).astype(F32)
    top_val, top_e = lax.top_k(logits, TOP_K)
    probs = jax.nn.softmax(top_val, axis=-1)
    flat_e = top_e.reshape(-1)
    order = jnp.argsort(flat_e)
    e_sorted = flat_e[order]
    tok_sorted = order // TOP_K
    p_sorted = probs.reshape(-1)[order]
    counts = jnp.bincount(flat_e, length=N_EXPERTS)
    padded = (counts + MOE_BLOCK - 1) // MOE_BLOCK * MOE_BLOCK
    pad_end = jnp.cumsum(padded)
    pad_start = pad_end - padded
    start = jnp.cumsum(counts) - counts
    dest = pad_start[e_sorted] + jnp.arange(NK) - start[e_sorted]
    n_blocks = -(-NK // MOE_BLOCK) + N_EXPERTS
    slot_tok = jnp.zeros(n_blocks * MOE_BLOCK, jnp.int32).at[dest].set(tok_sorted.astype(jnp.int32))
    block_e = jnp.minimum(jnp.searchsorted(pad_end, jnp.arange(n_blocks) * MOE_BLOCK, side='right'), N_EXPERTS - 1)
    xb = x[slot_tok].reshape(n_blocks, MOE_BLOCK, D_MODEL)

    def expert(args):
        xe, e = args
        gu = xe @ w_gu[e] + b_gu[e]
        gate, up = jnp.split(gu, 2, axis=-1)
        gate = jnp.minimum(gate, SWIGLU_LIMIT)
        up = jnp.clip(up, -SWIGLU_LIMIT, SWIGLU_LIMIT)
        glu = gate * jax.nn.sigmoid(SWIGLU_ALPHA * gate)
        return ((up + 1.0) * glu) @ w_dn[e] + b_dn[e]

    yb = lax.map(expert, (xb, block_e)).reshape(n_blocks * MOE_BLOCK, D_MODEL)
    y = jnp.zeros_like(x).at[tok_sorted].add(yb[dest] * p_sorted[:, None].astype(x.dtype))
    return y.reshape(shp)

def setup_inputs(seed: int = 0) -> dict:
    key = jax.random.key(seed)
    ks = iter(jax.random.split(key, 32))

    def nrm(shape, scale=1.0):
        return jax.random.normal(next(ks), shape, F32) * scale

    n_pages = PAST_LEN // PAGE_SIZE
    n_used = DEC_BATCH * n_pages
    n_pool = n_used + (n_used + 3) // 4
    x_prompt = nrm((BATCH, SEQ, D_MODEL))
    x_sample = nrm((DEC_BATCH, DEC_SEQ, D_MODEL))
    cache_k = nrm((DEPTH, n_pool, PAGE_SIZE, DSA_KV_HEADS, DSA_DH))
    cache_v = nrm((DEPTH, n_pool, PAGE_SIZE, DSA_KV_HEADS, DSA_DH))
    cache_k_idx = nrm((DEPTH, n_pool, PAGE_SIZE, IDX_DIM))
    cache_mem_k = nrm((DEPTH, DEC_BATCH, MEM_LEN, MEM_HEADS, MEM_DH))
    cache_mem_v = nrm((DEPTH, DEC_BATCH, MEM_LEN, MEM_HEADS, MEM_DH))
    state_gdn = nrm((DEPTH, DEC_BATCH, GDN_HEADS, GDN_DK, GDN_DV), 0.3)
    state_conv = nrm((DEPTH, DEC_BATCH, GDN_CONV - 1, GDN_QKV))
    page_table = jax.random.permutation(next(ks), n_pool)[:n_used].reshape(DEC_BATCH, n_pages).astype(jnp.int32)
    mem_prompt = nrm((BATCH, MEM_LEN, D_MODEL))
    norm_attn = 1.0 + nrm((DEPTH, D_MODEL), 0.02)
    w_in = nrm((DEPTH, D_MODEL, D_IN), D_MODEL ** -0.5)
    conv_w = nrm((DEPTH, GDN_CONV, GDN_QKV), 0.5)
    gdn_a_log = jnp.log(jax.random.uniform(next(ks), (DEPTH, GDN_HEADS), F32, 1.0, 16.0))
    dt = jnp.exp(jax.random.uniform(next(ks), (DEPTH, GDN_HEADS), F32, math.log(1e-3), math.log(1e-1)))
    gdn_dt_bias = dt + jnp.log(-jnp.expm1(-dt))
    gdn_norm = 1.0 + nrm((DEPTH, GDN_DV), 0.02)
    norm_mem = 1.0 + nrm((DEPTH, D_MODEL), 0.02)
    w_mem_kv = nrm((DEPTH, D_MODEL, 2 * MEM_HEADS * MEM_DH), D_MODEL ** -0.5)
    w_branch = nrm((DEPTH, N_BRANCH, BRANCH_W, D_MODEL), BRANCH_W ** -0.5)
    w_out = nrm((DEPTH, D_MODEL, D_MODEL), D_MODEL ** -0.5)
    norm_ffn = 1.0 + nrm((DEPTH, D_MODEL), 0.02)
    w_router = nrm((DEPTH, D_MODEL, N_EXPERTS), D_MODEL ** -0.5)
    b_router = nrm((DEPTH, N_EXPERTS), 0.01)
    w_gate_up = nrm((DEPTH, N_EXPERTS, D_MODEL, 2 * D_FF), D_MODEL ** -0.5)
    b_gate_up = nrm((DEPTH, N_EXPERTS, 2 * D_FF), 0.01)
    w_down = nrm((DEPTH, N_EXPERTS, D_FF, D_MODEL), D_FF ** -0.5)
    b_down = nrm((DEPTH, N_EXPERTS, D_MODEL), 0.01)
    norm_final = 1.0 + nrm((D_MODEL,), 0.02)
    return {"x_prompt": x_prompt, "x_sample": x_sample, "cache_k": cache_k, "cache_v": cache_v,
            "cache_k_idx": cache_k_idx, "cache_mem_k": cache_mem_k, "cache_mem_v": cache_mem_v,
            "state_gdn": state_gdn, "state_conv": state_conv, "page_table": page_table,
            "mem_prompt": mem_prompt, "norm_attn": norm_attn, "w_in": w_in, "conv_w": conv_w,
            "gdn_a_log": gdn_a_log, "gdn_dt_bias": gdn_dt_bias, "gdn_norm": gdn_norm,
            "norm_mem": norm_mem, "w_mem_kv": w_mem_kv, "w_branch": w_branch, "w_out": w_out,
            "norm_ffn": norm_ffn, "w_router": w_router, "b_router": b_router,
            "w_gate_up": w_gate_up, "b_gate_up": b_gate_up, "w_down": w_down, "b_down": b_down,
            "norm_final": norm_final}

def reference(x_prompt, x_sample, cache_k, cache_v, cache_k_idx, cache_mem_k, cache_mem_v,
              state_gdn, state_conv, page_table, mem_prompt, norm_attn, w_in, conv_w,
              gdn_a_log, gdn_dt_bias, gdn_norm, norm_mem, w_mem_kv, w_branch, w_out,
              norm_ffn, w_router, b_router, w_gate_up, b_gate_up, w_down, b_down, norm_final):
    xp, xs = x_prompt, x_sample
    B = xp.shape[0]
    kp, vp, ip, mkp, mvp, sp, cp = [], [], [], [], [], [], []
    ksl, vsl, isl, ssl, csl = [], [], [], [], []
    for l in range(DEPTH):
        (g_qkv, g_z, g_b, g_a, d_q, d_k, d_v, i_q, i_k, i_w, m_q, gates) = in_proj(xp, norm_attn[l], w_in[l])
        conv0 = jnp.zeros((B, GDN_CONV - 1, GDN_QKV), xp.dtype)
        o_g, conv_new, ssm_new = gdn_branch(g_qkv, g_z, g_b, g_a, conv0, None, conv_w[l],
                                            gdn_a_log[l], gdn_dt_bias[l], gdn_norm[l])
        k_h = heads(d_k, DSA_KV_HEADS, DSA_DH)
        v_h = heads(d_v, DSA_KV_HEADS, DSA_DH)
        o_d = dsa_prompt(heads(d_q, DSA_HEADS, DSA_DH), k_h, v_h, heads(i_q, IDX_HEADS, IDX_DIM), i_k, i_w)
        mk, mv = mem_kv(mem_prompt, norm_mem[l], w_mem_kv[l])
        o_m = mem_attend(m_q, mk, mv)
        xp = merge_out(xp, o_g, o_d, o_m, gates, w_branch[l], w_out[l])
        xp = xp + moe(rms_norm(xp, norm_ffn[l]), w_router[l], b_router[l], w_gate_up[l], b_gate_up[l], w_down[l], b_down[l])
        kp.append(k_h); vp.append(v_h); ip.append(i_k); mkp.append(mk); mvp.append(mv)
        sp.append(ssm_new); cp.append(conv_new)
        (g_qkv, g_z, g_b, g_a, d_q, d_k, d_v, i_q, i_k, i_w, m_q, gates) = in_proj(xs, norm_attn[l], w_in[l])
        o_g, conv_new, ssm_new = gdn_branch(g_qkv, g_z, g_b, g_a, state_conv[l], state_gdn[l], conv_w[l],
                                            gdn_a_log[l], gdn_dt_bias[l], gdn_norm[l])
        k_h = heads(d_k, DSA_KV_HEADS, DSA_DH)
        v_h = heads(d_v, DSA_KV_HEADS, DSA_DH)
        o_d = dsa_sample(heads(d_q, DSA_HEADS, DSA_DH), k_h, v_h, heads(i_q, IDX_HEADS, IDX_DIM), i_k, i_w,
                         cache_k, cache_v, cache_k_idx, page_table, l)
        o_m = mem_attend(m_q, cache_mem_k[l], cache_mem_v[l])
        xs = merge_out(xs, o_g, o_d, o_m, gates, w_branch[l], w_out[l])
        xs = xs + moe(rms_norm(xs, norm_ffn[l]), w_router[l], b_router[l], w_gate_up[l], b_gate_up[l], w_down[l], b_down[l])
        ksl.append(k_h); vsl.append(v_h); isl.append(i_k); ssl.append(ssm_new); csl.append(conv_new)
    y_prompt = rms_norm(xp, norm_final)
    y_sample = rms_norm(xs, norm_final)
    k_prompt, v_prompt, kidx_prompt = jnp.stack(kp), jnp.stack(vp), jnp.stack(ip)
    memk_prompt, memv_prompt = jnp.stack(mkp), jnp.stack(mvp)
    ssm_prompt, conv_prompt = jnp.stack(sp), jnp.stack(cp)
    k_sample, v_sample, kidx_sample = jnp.stack(ksl), jnp.stack(vsl), jnp.stack(isl)
    ssm_sample, conv_sample = jnp.stack(ssl), jnp.stack(csl)
    return (y_prompt, y_sample, k_prompt, v_prompt, kidx_prompt, memk_prompt, memv_prompt,
            ssm_prompt, conv_prompt, k_sample, v_sample, kidx_sample, ssm_sample, conv_sample)


_drawn_inputs = setup_inputs


def setup_inputs(seed=0):
    import zlib

    import numpy as np

    out = dict(_drawn_inputs(seed))
    spreads = {}
    factors = {'norm_mem': 2.875, 'b_gate_up': 8.0, 'b_down': 8.0, 'norm_final': 2.74}
    for name, (base, spread) in spreads.items():
        noise = np.random.default_rng([zlib.crc32(name.encode()), seed]).standard_normal(out[name].shape)
        drawn = base * np.exp(spread * noise) if base else spread * noise
        out[name] = __import__('jax').numpy.asarray(drawn.astype(out[name].dtype))
    for name, factor in factors.items():
        out[name] = (out[name] * factor).astype(out[name].dtype)
    return out
```

```python
from contextlib import ExitStack

import concourse.bass as bass
from concourse import mybir

F32 = mybir.dt.float32
I32 = mybir.dt.int32
ALU = mybir.AluOpType
ACT = mybir.ActivationFunctionType
AX = mybir.AxisListType.X

P = 128
D = 1024
KD = D // P
NP, NS = 256, 8
NT = NP + NS
TOK = [(0, P), (P, P), (NP, NS)]
PAST, PAGE, NPAGES, NPOOL = 1024, 128, 8, 80
L = PAST + 1
NEG = -1e30
TAKEN = -3e38
EPS = 1e-6
NE, TOPK, FF = 32, 4, 1024
SLOTS = 64
PAIRS = NE // 2
CHUNKS = 12
LIMIT, ALPHA = 7.0, 1.702
TOP_PROMPT, TOP_SAMPLE = 64, 256
MAX_PASSES = -(-NT // SLOTS)

C_QKV, C_Z, C_B, C_A, C_DQ, C_DK, C_IQ, C_IK, C_IW, C_MQ, C_G = (
    0, 1536, 2048, 2056, 2064, 2576, 3088, 3344, 3408, 3412, 3924)

IQ, IK, IW, DK, DV, DQ, GQ, GK, GV, GZ, BE, AA, MQ = 0, 2, 3, 4, 6, 8, 12, 16, 20, 24, 28, 29, 30
NTILES = 34

SLOT_W = 528 * KD
RING_SLOTS = 4
KV0 = RING_SLOTS * SLOT_W
KT0 = KV0 + 3 * 2048
RING_END = CHUNKS * 2048
PT0 = RING_END
HT0 = PT0 + NTILES * NT
OT0 = HT0 + KD * NT
Z0 = OT0 + 12 * NT
ARENA = Z0 + 12064
assert KT0 + 1536 <= RING_END


ORDERS = {
    "te_steps": [
        ("sv_ps", 1), ("xT_ps", 8), ("memT_ps", 8), ("sidx_scores", 1), ("iw_ps", 1), ("sc8_ps", 1),
        ("iscore_ps", 2), ("mkT_ps", 4), ("tok_ps", 3), ("PTm_ps", 1), ("smv_step", 8),
        ("s64_ps", 1), ("PT64_ps", 1), ("sv_step", 8), ("cstate_ps", 1), ("crow_ps", 1),
        ("qksum_ps", 8), ("bg_ps", 1), ("G_ps", 1), ("GT_ps", 1), ("EG_ps", 4), ("BEs_ps", 1),
        ("row_ps", 4), ("kk_ps", 2), ("kvtok_ps", 2), ("ksr_ps", 1), ("uw_ps", 2), ("kS_ps", 1),
        ("vnr_ps", 1), ("outer_ps", 4), ("so_ps", 1), ("osum_ps", 4), ("h2T_ps", 8),
        ("logit_ps", 3), ("bgu_ps", 1), ("rank_ps", 1), ("probT_ps", 1), ("bd_ps", 6),
    ],
    "act_steps": [
        ("root_ready", 1), ("relu32_ready", 3), ("mkT_ready", 4), ("tok_ready", 3),
        ("smk_ready", 16), ("sm_exp", 1), ("sk_ready", 32), ("sa_exp", 1), ("csig_ready", 12),
        ("softplus_ready", 1), ("qksq_ready", 8), ("qkroot_ready", 8), ("eG_ready", 1),
        ("EG_ready", 4), ("gam_ready", 2), ("osq_ready", 4), ("oroot_ready", 4), ("root2_ready", 3),
        ("h2T_ready", 8), ("pexp_ready", 3), ("root3_ready", 3),
    ],
    "ve_steps": [
        ("sv_ready", 1), ("x_normed", 5), ("hT_ready", 8), ("memT_ready", 8), ("Qdi_ready", 8),
        ("kiT_ready", 8), ("wmix_ready", 1), ("iwtok_ready", 1), ("sc8_read", 3),
        ("ibias_ready", 2), ("bias8_ready", 1), ("Qm_ready", 1), ("QdT_ready", 1), ("sm_nmax", 1),
        ("sm_p", 1), ("PTm_ready", 1), ("sa_nmax", 1), ("sa_p", 1), ("PT64_ready", 2),
        ("so_read", 3), ("crow_ready", 1), ("conv_ready", 24), ("silu_ready", 12), ("dtx_ready", 1),
        ("gT_ready", 1), ("qk_ready", 8), ("bg_ready", 2), ("G_ready", 1), ("GL_ready", 1),
        ("GT_ready", 1), ("BEs_ready", 1), ("kk_read", 2), ("kv_tok", 8), ("uw_ready", 4), ("qg_ready", 4),
        ("state0", 1), ("o_read", 1), ("vnT_ready", 1), ("go_ready", 4), ("og_ready", 4), ("x1_ready", 6),
        ("h2_ready", 3), ("passes_known", 1), ("probT_ready", 1), ("bd_added", 6), ("acc_final", 1),
        ("y_ready", 3),
    ],
}
SHARED = {}
for _group, _names in ORDERS.items():
    _base = 0
    for _name, _count in _names:
        SHARED[_name] = (_group, _base)
        _base += _count


def program(nc, x_prompt, x_sample, cache_k, cache_v, cache_k_idx, cache_mem_k, cache_mem_v,
            state_gdn, state_conv, page_table, mem_prompt, norm_attn, w_in, conv_w, gdn_a_log,
            gdn_dt_bias, gdn_norm, norm_mem, w_mem_kv, w_branch, w_out, norm_ffn, w_router,
            b_router, w_gate_up, b_gate_up, w_down, b_down, norm_final,
            y_prompt, y_sample, k_prompt, v_prompt, kidx_prompt, memk_prompt, memv_prompt,
            ssm_prompt, conv_prompt, k_sample, v_sample, kidx_sample, ssm_sample, conv_sample):
    ctx = ExitStack()
    with ctx:
        A = ctx.enter_context(nc.sbuf_tensor("arena", [P, ARENA], F32))

        def sb(name, cols, dt=F32):
            return ctx.enter_context(nc.sbuf_tensor(name, [P, cols], dt))

        sems = {}

        def S(name):
            if name in SHARED:
                name = SHARED[name][0]
            if name not in sems:
                sems[name] = ctx.enter_context(nc.semaphore(name))
            return sems[name]

        def after(name, count):
            return S(name), SHARED[name][1] + count

        def area(at, *shape):
            n = 1
            for s in shape:
                n *= s
            v = A[:, at:at + n]
            if len(shape) == 2:
                v = v.rearrange("p (a b) -> p a b", a=shape[0])
            if len(shape) == 3:
                v = v.rearrange("p (a b c) -> p a b c", a=shape[0], b=shape[1])
            return v

        bank = [ctx.enter_context(nc.psum_tensor(f"bank{i}", [P, 512], F32)) for i in range(8)]

        ident = sb("ident", P)
        blockones = sb("blockones", P)
        ones = sb("ones", P)
        before = sb("before", P)
        cumul = sb("cumul", P)
        diag64 = sb("diag64", 64)
        incl = sb("incl", 64)
        strict = sb("strict", 64)
        level = sb("level", 6 * 64)
        headsel = sb("headsel", 512)
        seq64 = sb("seq64", 64)
        seq64t = sb("seq64t", 8)
        head32 = sb("head32", 32)
        seq32t = sb("seq32t", 8)
        iota_slot = sb("iota_slot", SLOTS)
        eps = sb("eps", 1)
        xc_i, ec_i, lv_i, slot_i = (area(KT0 + 128 + 64 * i, 64).bitcast(I32) for i in range(4))

        ptab = sb("ptab", 64, I32)
        svec = area(KT0, P)
        svT = sb("svT", 64)
        gnorm = sb("gnorm", 1)
        alog = sb("alog", 2)
        ssq = sb("ssq", 8)
        rinv = sb("rinv", 8)
        iwtok = sb("iwtok", 8)
        wmix = sb("wmix", 8)
        top8 = sb("top8", 8)
        mx = sb("mx", 2)
        nmx = sb("nmx", 2)
        sm = sb("sm", 2)
        rs = sb("rs", 2)
        mx1 = sb("mx1", 4)
        becols = sb("becols", 16)
        gcols = sb("gcols", 16)
        Gcols = sb("Gcols", 16)
        eG = sb("eG", 16)
        eGl = sb("eGl", 16)
        beG = sb("beG", 16)

        slot = [area(s * SLOT_W, SLOT_W) for s in range(RING_SLOTS)]
        kvbuf = [area(KV0 + 2048 * i, 2048) for i in range(3)]
        ktbuf = [area(KT0 + 512 * i, 512) for i in range(3)]
        xraw = area(KV0, 3, 1024)
        memraw = area(KV0 + 3072, 2, 1024)
        sqs = area(KV0 + 5120, 1024)
        proj = area(PT0, NTILES, NT)
        hT = area(HT0, KD, NT)
        oT = area(OT0, 12, NT)

        memT = area(Z0, KD, NP)
        vtok = area(Z0, 3, 256)
        ktok = area(Z0 + 768, 3, 256)
        iktok = area(Z0 + 1536, 3, 64)
        idxc = area(Z0 + 2048, 32, 128)
        smx = area(Z0 + 2048, 2, 256)
        smt = smx[:, 0, :]
        pts = area(Z0 + 2560, 2, 256)
        QdT = area(Z0 + 3072, 16, 64)
        Qm = area(Z0 + 4096, 32, 32)
        S32 = area(Z0 + 5120, 256)
        PT64 = area(Z0 + 5376, 8, 64)
        PTm = area(Z0 + 5888, 2, 32)
        pnew = area(Z0 + 5952, 8)
        pnewT = area(Z0 + 5960, 64)
        mk = area(Z0 + 6144, 2, 512)
        mv = area(Z0 + 7168, 2, 512)
        mkT = area(Z0 + 8192, 4, 256)
        Qdi = area(Z0 + 9216, 8, 32)
        relu32 = area(Z0 + 9472, L)
        S64 = area(Z0 + 9472, L)
        sc8 = area(Z0 + 10504, L)
        biasP = area(Z0 + 11536, 2, 256)

        conv = area(PT0, 12, NT)
        vb = area(Z0 + 1024, 2, 512)
        kbG = area(Z0 + 2048, 2, 512)
        kd = area(Z0 + 3072, 2, 512)
        gamT = area(Z0 + 4096, 2, 512)
        MT = area(Z0 + 5120, 2, 512)
        qkT = area(Z0 + 6144, 2, 512)
        X = area(Z0 + 7168, 2, 512)
        XT = area(Z0 + 8192, 2, 512)
        T1 = area(Z0 + 9216, 2, 512)
        EG = area(Z0 + 10240, 4, NT)
        St = area(Z0 + 11296, 4, 64)
        vn = area(Z0 + 11552, 512)
        usol = gamT
        wT = area(Z0 + 5120, 4, 256)
        nrm = area(PT0 + GQ * NT, 12, NT)
        sS = area(KV0, 8, 4, 64)
        ksr = area(KV0 + 2048, 512)
        Lm = area(KV0 + 2560, 2, 512)
        vnx = area(KV0 + 2560, 2, 8 * 64)
        vnT = area(KV0 + 3584, 4, 8)
        vnr = area(KV0 + 3616, 512)
        BEs = area(KV0 + 4128, 4, 8)
        srow = area(KV0 + 4160, 1536)
        xst = area(KT0, 12, 8, 4)
        dg = area(KT0 + 384, 512)
        conv_rows = area(KV0 + 4160, 1536)

        mergedT = area(Z0, KD, NT)
        acc = area(Z0 + 2112, 3, 1024)
        sgate = area(Z0 + 5184, 2, NT)
        gmul = area(Z0 + 5712, 2, NT)
        M0 = PT0
        h2 = area(M0, 3, 1024)
        h2T = area(M0 + 3072, KD, NT)
        xg = area(M0 + 5184, KD, 128)
        actT = area(M0 + 6208, 8, 64)
        gb = area(M0 + 6720, 8, 64)
        sg = area(M0 + 7232, 8, 64)
        ub = area(M0 + 7744, 8, 64)
        yT = area(M0 + 8256, KD, 128)
        yr = area(M0 + 9280, 1024)
        Sg = area(M0 + 10304, 3, 2, 64)
        Sw = area(M0 + 10688, 3, 2, 64)
        SwT = area(M0 + 11072, NT)
        gffn = area(Z0 + 10540, 1024)
        gfin = area(M0 + 12368, 1024)
        assert M0 + 13392 <= Z0, (M0 + 13392, Z0)
        bdn = area(Z0 + 6400, 1024)
        bgr = area(Z0 + 7424, 4, 128)
        bguT = area(Z0 + 7936, 512)
        wr = area(Z0 + 8448, KD, NE)
        brt = area(Z0 + 8704, NE)
        logit = area(Z0 + 8736, 3, NE)
        prob = area(Z0 + 8832, 3, NE)
        sel = area(Z0 + 8928, 3, NE)
        slotcol = area(Z0 + 9024, 3, NE)
        probT = area(Z0 + 9120, NT)
        rt = area(Z0 + 9384, 4, NE)
        sqs2 = area(Z0 + 9512, 1024)
        npass = sb("npass", 4, I32)
        cntf = sb("cntf", 8)

        ring = area(0, CHUNKS, 2048)
        block = ctx.enter_context(nc.Block())

        def w_cols(w, c0, n):
            return w.rearrange("(k p) n -> p k n", p=P)[:, :, c0:c0 + n]

        pieces = [("idx", w_cols(w_in[0], C_IQ, 324), 324), ("dkv", w_cols(w_in[0], C_DK, 512), 512),
                  ("dq", w_cols(w_in[0], C_DQ, 512), 512), ("mq", w_cols(w_in[0], C_MQ, 512), 512),
                  ("mkw", w_cols(w_mem_kv[0], 0, 512), 512), ("mvw", w_cols(w_mem_kv[0], 512, 512), 512),
                  ("q", w_cols(w_in[0], 0, 512), 512), ("k", w_cols(w_in[0], 512, 512), 512),
                  ("v", w_cols(w_in[0], 1024, 512), 512), ("z", w_cols(w_in[0], C_Z, 528), 528)]
        for n in range(3):
            gate = [(f"g{n}{hf}", w_cols(w_in[0], C_G + n * D + hf * 512, 512), 512) for hf in range(2)]
            pieces += [gate[0], (f"br{n}", None, None), gate[1]]
        pieces += [("wo0", w_cols(w_out[0], 0, 512), 512), ("wo1", w_cols(w_out[0], 512, 512), 512)]
        index = {name: i for i, (name, _, _) in enumerate(pieces)}

        def piece_view(name):
            i = index[name]
            w = pieces[i][2]
            if w is None:
                return slot[i % RING_SLOTS][:, 0:4096].rearrange("p (k n) -> p k n", k=4)
            return slot[i % RING_SLOTS][:, 0:KD * w].rearrange("p (k n) -> p k n", k=KD)

        def wait_piece(eng, name):
            i = index[name]
            eng.wait_ge(S(f"slot{i % RING_SLOTS}_loaded"), 16 * (i // RING_SLOTS + 1))

        units = [("mk", i) for i in range(4)] + [("k", b) for b in range(8)] + \
                [("mv", i) for i in range(4)] + [("v", b) for b in range(8)]

        def wait_unit_used(eng, u):
            kind, i = units[u]
            if kind == "mk":
                eng.wait_ge(S("smk_ps"), 4 * (i + 1))
            elif kind == "k":
                eng.wait_ge(S("sk_ps"), 4 * (i + 1))
            elif kind == "mv":
                eng.wait_ge(*after("smv_step", 2 * (i + 1)))
            else:
                eng.wait_ge(*after("sv_step", i + 1))

        def wait_unit(eng, n):
            per = 16 * NPAGES
            got = sum(32 if units[m][0][0] == "m" else per for m in range(n % 3, n + 1, 3))
            eng.wait_ge(S(f"kv{n % 3}_loaded"), got)

        tiles = [("idx", 0, 128, IQ), ("idx", 128, 128, IQ + 1), ("idx", 256, 64, IK), ("idx", 320, 4, IW),
                 ("dkv", 0, 128, DK), ("dkv", 128, 128, DK + 1), ("dkv", 256, 128, DV), ("dkv", 384, 128, DV + 1)]
        tiles += [("dq", 128 * i, 128, DQ) for i in range(4)]
        tiles += [("mq", 128 * i, 128, MQ + i) for i in range(4)]
        tiles += [("mkw", a, 0, None) for a in range(2)] + [("mvw", a, 0, None) for a in range(2)]
        tiles += [("q", 128 * i, 128, GQ + i) for i in range(4)]
        tiles += [("k", 128 * i, 128, GK + i) for i in range(4)]
        tiles += [("v", 128 * i, 128, GV + i) for i in range(4)]
        tiles += [("z", 128 * i, 128, GZ + i) for i in range(4)]
        tiles += [("z", 512, 8, BE), ("z", 520, 8, AA)]
        n_proj = {}
        for i, (nm, _, _, _) in enumerate(tiles):
            n_proj[nm] = i + 1
        NPROJ = 3

        heads_it = [("mem", a, h) for a in range(2) for h in range(4)] + \
                   [("dsa", a, h) for a in range(2) for h in range(8)]

        def width(it):
            return P if (it[0] == "dsa" and it[1] == 0) else NP

        CONST = 14

        @block.sync
        def _(sp):
            sp.dma_start(xraw[:, 0:2, :], x_prompt[0].rearrange("(a p) d -> p a d", p=P)).then_inc(S("x_loaded"), 16)
            sp.dma_start(xraw[0:NS, 2, :], x_sample.rearrange("b o d -> (b o) d")).then_inc(S("x_loaded"), 16)
            sp.dma_start(memraw, mem_prompt[0].rearrange("(a p) d -> p a d", p=P)).then_inc(S("x_loaded"), 16)
            for i, (name, src, w) in enumerate(pieces):
                if i >= RING_SLOTS:
                    old = pieces[i - RING_SLOTS][0]
                    if old in n_proj:
                        sp.wait_ge(S("proj_done"), n_proj[old])
                    else:
                        sp.wait_ge(S("br_ps"), 8 * int(old[-2 if old[0] == "g" else -1]) + (4 if old[0] == "g" and old[-1] == "0" else 8))
                done = S(f"slot{i % RING_SLOTS}_loaded")
                if name[0:2] == "br":
                    src = w_branch[0, int(name[2])]
                    if name != "br1":
                        sp.dma_start(piece_view(name), src.rearrange("(c p) n -> p c n", p=P)).then_inc(done, 16)
                    else:
                        rows = src.rearrange("(t u j d) n -> u d t j n", t=2, u=2, j=2)
                        for u in range(2):
                            for t in range(2):
                                ins = sp.dma_start(piece_view(name)[u * 64:u * 64 + 64, 2 * t:2 * t + 2, :], rows[u][:, t])
                                ins.then_inc(S("br1_part") if (u, t) != (1, 1) else done, 16)
                else:
                    sp.dma_start(piece_view(name), src).then_inc(done, 16)
            sp.wait_ge(S("x1_ps"), 6)
            sp.sem_inc(S("ring_free"), CHUNKS)
            sp.wait_ge(*after("passes_known", 1))
            passes = sp.value_load(npass[0:1, 0:1], min_val=1, max_val=MAX_PASSES)
            with sp.Fori(0, passes) as q:
                with sp.Fori(0, PAIRS) as p:
                    for half in range(2):
                        e = sp.snap(p * 2 + half)
                        for j in range(CHUNKS):
                            sp.wait_ge(S("ring_free"), (q * NE + p * 2 + half) * CHUNKS + j + 1)
                            if j < KD:
                                sp.dma_start(ring[:, j, :], w_gate_up[0, bass.DynSlice(e, 1), j * P:(j + 1) * P, :]
                                             .rearrange("o p n -> (o p) n")).then_inc(S(f"chunk{j}_loaded"), 16)
                            else:
                                r0 = (j - KD) * 2 * P
                                sp.dma_start(ring[:, j, :].rearrange("p (c n) -> p c n", c=2),
                                             w_down[0, bass.DynSlice(e, 1), r0:r0 + 2 * P, :]
                                             .rearrange("o (c p) n -> p (o c) n", p=P)).then_inc(S(f"chunk{j}_loaded"), 16)
            sp.wait_ge(*after("y_ready", 3))
            sp.dma_start(y_prompt[0].rearrange("(a p) d -> p a d", p=P), acc[:, 0:2, :]).then_inc(S("out_written"), 16)
            sp.dma_start(y_sample.rearrange("b o d -> (b o) d"), acc[0:NS, 2, :]).then_inc(S("out_written"), 16)
            sp.wait_ge(S("out_written"), 32)

        @block.gpsimd
        def _(pool):
            n = [0]

            def link(ins):
                n[0] += 1
                ins.then_inc(S("pool_done"), 1)
                pool.wait_ge(S("pool_done"), n[0])

            pool.dma_start(ptab[0:1, :], page_table.rearrange("(o b) n -> o (b n)", o=1)).then_inc(S("ptab_loaded"), 16)
            pool.dma_start(svec[0:8, :], norm_attn.rearrange("o (r c) -> (o r) c", c=P)).then_inc(S("small_loaded"), 16)
            pool.dma_start(svec[8:16, :], norm_mem.rearrange("o (r c) -> (o r) c", c=P)).then_inc(S("small_loaded"), 16)
            pool.dma_start(svec[16:64, :], conv_w[0].rearrange("i (r c) -> (i r) c", c=P)).then_inc(S("small_loaded"), 16)
            pool.dma_start(gnorm[0:64, :], gdn_norm.rearrange("o v -> v o")).then_inc(S("small_loaded"), 16)
            pool.dma_start(gnorm[64:128, :], gdn_norm.rearrange("o v -> v o")).then_inc(S("small_loaded"), 16)
            pool.dma_start(alog[0:8, 0:1], gdn_a_log.rearrange("o v -> v o")).then_inc(S("small_loaded"), 16)
            pool.dma_start(alog[0:8, 1:2], gdn_dt_bias.rearrange("o v -> v o")).then_inc(S("small_loaded"), 16)

            def select(t, op, base, pattern, cm, fill):
                link(pool.affine_select(out=t, in_=t, compare_op=op, fill=fill, base=base, pattern=pattern,
                                        channel_multiplier=cm))

            link(pool.memset(ident[:, :], 0.0))
            select(ident[:, :], ALU.not_equal, 0, [[-1, P]], 1, 1.0)
            pool.wait_ge(S("pool_done"), n[0])
            link(pool.memset(eps[:, :], EPS))
            link(pool.memset(ones[:, :], 1.0))
            pool.sem_inc(S("ident_ready"), 1)
            pool.wait_ge(S("ptab_loaded"), 16)
            with pool.Fori(0, NS) as b:
                for j in range(NPAGES):
                    page = pool.value_load(ptab[0:1, bass.DynSlice(b * NPAGES + j, 1)], min_val=0, max_val=NPOOL - 1)
                    pos = (j % 4) * 2 + j // 4
                    pool.dma_start(A[:, bass.DynSlice(Z0 + 2048 + b * 512 + pos * 64, 64)],
                                   cache_k_idx[0, bass.DynSlice(page, 1)].rearrange("o p n -> (o p) n"))\
                        .then_inc(S("idx_loaded"), 16)
            link(pool.memset(before[:, :], 1.0))
            select(before[:, :], ALU.is_gt, 0, [[1, P]], -1, 0.0)
            link(pool.memset(blockones[:, :], 0.0))
            link(pool.memset(blockones[0:64, 0:64], 1.0))
            link(pool.memset(blockones[64:128, 64:128], 1.0))
            link(pool.tensor_copy(cumul[:, :], blockones[:, :]))
            select(cumul[:, :], ALU.is_ge, 0, [[1, P]], -1, 0.0)
            link(pool.tensor_copy(diag64[0:64, :], ident[0:64, 0:64]))
            link(pool.tensor_copy(diag64[64:128, :], ident[64:128, 64:128]))
            link(pool.memset(incl[:, :], 0.0))
            link(pool.memset(strict[:, :], 1.0))
            for h0 in (0, 64):
                select(incl[h0:h0 + 64, :], ALU.is_ge, 0, [[1, 64]], -1, NEG)
                select(strict[h0:h0 + 64, :], ALU.is_gt, 0, [[1, 64]], -1, 0.0)
            link(pool.memset(headsel[0:8, :], 0.0))
            select(headsel[0:8, :], ALU.not_equal, 0, [[-1, 8], [0, 64]], 1, 1.0)
            link(pool.memset(seq64[0:8, :], 0.0))
            select(seq64[0:8, :], ALU.not_equal, 0, [[-1, 8], [0, 8]], 1, 1.0)
            link(pool.memset(head32[0:4, :], 0.0))
            select(head32[0:4, :], ALU.not_equal, 0, [[0, 8], [-1, 4]], 1, 1.0)
            link(pool.memset(seq64t[0:64, :], 1.0))
            select(seq64t[0:64, :], ALU.is_ge, 0, [[-8, 8]], 1, 0.0)
            select(seq64t[0:64, :], ALU.is_ge, 7, [[8, 8]], -1, 0.0)
            link(pool.memset(seq32t[0:32, :], 1.0))
            select(seq32t[0:32, :], ALU.is_ge, 0, [[-4, 8]], 1, 0.0)
            select(seq32t[0:32, :], ALU.is_ge, 3, [[4, 8]], -1, 0.0)
            link(pool.iota(xc_i[:, :], pattern=[[1, 64]], base=0, channel_multiplier=0))
            link(pool.iota(slot_i[:, :], pattern=[[1, 64]], base=0, channel_multiplier=0))
            link(pool.iota(ec_i[:, :], pattern=[[0, 64]], base=0, channel_multiplier=1))
            pool.sem_inc(S("consts_ready"), 1)
            pool.wait_ge(*after("memT_ready", KD))
            for u, (kind, b) in enumerate(units):
                if u >= 3:
                    wait_unit_used(pool, u - 3)
                buf, done = kvbuf[u % 3], S(f"kv{u % 3}_loaded")
                if kind[0] == "m":
                    src = cache_mem_k if kind == "mk" else cache_mem_v
                    for i in range(2):
                        pool.dma_start(buf[:, i * 1024:(i + 1) * 1024].rearrange("p (a n) -> p a n", a=2),
                                       src[0, 2 * b + i].rearrange("(a p) h d -> p a (h d)", p=P)).then_inc(done, 16)
                else:
                    src = cache_k if kind == "k" else cache_v
                    for j in range(NPAGES):
                        page = pool.value_load(ptab[0:1, b * NPAGES + j:b * NPAGES + j + 1], min_val=0, max_val=NPOOL - 1)
                        pool.dma_start(buf[:, j * 256:(j + 1) * 256],
                                       src[0, bass.DynSlice(page, 1)]
                                       .rearrange("o p h d -> (o p) (h d)")).then_inc(done, 16)
                if u == 2:
                    for a in range(2):
                        pool.wait_ge(S("iscore_ready"), a + 1)
                        pool.affine_select(out=biasP[:, a, :], in_=biasP[:, a, :], compare_op=ALU.is_ge, fill=NEG,
                                           base=a * P, pattern=[[-1, 256]], channel_multiplier=1)\
                            .then_inc(S("iscore_masked"), 1)
                    for a in range(2):
                        pool.wait_ge(*after("ibias_ready", a + 1))
                        pool.affine_select(out=biasP[:, a, :], in_=biasP[:, a, :], compare_op=ALU.is_ge, fill=NEG,
                                           base=a * P, pattern=[[-1, 256]], channel_multiplier=1)\
                            .then_inc(S("ibias_masked"), 1)

            pool.wait_ge(*after("sv_step", NS))
            pool.dma_start(srow[0:24, :], state_conv[0].rearrange("b i c -> (b i) c")).then_inc(S("state_rows"), 16)
            for hh in range(2):
                pool.dma_start(sS[hh * 64:hh * 64 + 64, :, :, :].rearrange("p b h v -> p (b h) v"),
                               state_gdn[0].rearrange("b (h e) k v -> e k (b h) v", e=2)[hh]).then_inc(S("sstate_loaded"), 16)
            pool.dma_start(conv_sample[0, :, 0:2, :], state_conv[0, :, 1:3, :]).then_inc(S("pool_stored"), 16)
            pool.wait_ge(*after("crow_ready", 1))
            pool.dma_start(conv_prompt[0, 0], conv_rows[32:35, :]).then_inc(S("pool_stored"), 16)
            pool.dma_start(conv_sample[0, :, 2, :], conv_rows[35:43, :]).then_inc(S("pool_stored"), 16)
            pool.wait_ge(S("state_ready"), 4)
            for hh in range(2):
                pool.dma_start(ssm_prompt[0, 0].rearrange("(h e) k v -> e k h v", e=2)[hh], St[hh * 64:hh * 64 + 64, :, :])\
                    .then_inc(S("pool_stored"), 16)
            pool.wait_ge(S("sS_ready"), 4)
            for hh in range(2):
                pool.dma_start(ssm_sample[0].rearrange("b (h e) k v -> e k (b h) v", e=2)[hh],
                               sS[hh * 64:hh * 64 + 64, :, :, :].rearrange("p b h v -> p (b h) v")).then_inc(S("pool_stored"), 16)
            pool.wait_ge(*after("og_ready", 4))
            pool.wait_ge(S("pool_stored"), 16 * 7)
            pool.dma_start(acc[:, 0:2, :], x_prompt[0].rearrange("(a p) d -> p a d", p=P)).then_inc(S("xagain_loaded"), 16)
            pool.dma_start(acc[0:NS, 2, :], x_sample.rearrange("b o d -> (b o) d")).then_inc(S("xagain_loaded"), 16)
            pool.dma_start(gffn, norm_ffn[0].partition_broadcast(P)).then_inc(S("moe_small"), 16)
            pool.dma_start(brt, b_router[0].partition_broadcast(P)).then_inc(S("moe_small"), 16)
            pool.dma_start(wr, w_router[0].rearrange("(k p) n -> p k n", p=P)).then_inc(S("moe_small"), 16)
            pool.dma_start(bdn[0:NE, :], b_down[0]).then_inc(S("moe_small"), 16)
            pool.dma_start(bgr, b_gate_up[0].rearrange("e (m c) -> (e m) c", c=P).rearrange("(g r) c -> r g c", r=P))\
                .then_inc(S("moe_small"), 16)
            pool.wait_ge(S("x1_ps"), 6)
            pool.dma_start(gfin, norm_final.partition_broadcast(P)).then_inc(S("gfin_loaded"), 16)

        @block.scalar
        def _(act):
            n = [0]

            def link(ins):
                n[0] += 1
                ins.then_inc(S("act_done"), 1)
                act.wait_ge(S("act_done"), n[0])

            def signal(ins, name):
                ins.then_inc(S(name), 1)

            act.wait_ge(S("x_loaded"), 48)
            act.wait_ge(S("ident_ready"), 1)
            for j, (t, m) in enumerate([(xraw[:, 0, :], P), (xraw[:, 1, :], P), (xraw[:, 2, :], NS),
                                        (memraw[:, 0, :], P), (memraw[:, 1, :], P)]):
                link(act.activation(sqs[0:m, :], t[0:m, :], ACT.Square, accum_out=ssq[0:m, j:j + 1]))
            for j, m in enumerate([P, P, NS, P, P]):
                link(act.activation(rinv[0:m, j:j + 1], ssq[0:m, j:j + 1], ACT.Sqrt, bias=eps[0:m, :], scale=1.0 / D))
            act.sem_inc(S("root_ready"), 1)

            def evac(i):
                nm, c, m, dst = tiles[i]
                b = bank[i % NPROJ]
                act.wait_ge(S("proj_done"), i + 1)
                if nm == "mkw" or nm == "mvw":
                    signal(act.activation((mk if nm == "mkw" else mv)[:, c, :], b[:, :], ACT.Copy), "proj_evac")
                elif nm == "idx" and dst == IK:
                    link(act.activation(proj[64:128, IK, :], b[0:64, 0:NT], ACT.Copy))
                    signal(act.activation(proj[0:64, IK, :], b[0:64, 0:NT], ACT.Copy), "proj_evac")
                elif nm == "dq":
                    kv = c // 128
                    t, u = kv // 2, kv % 2
                    link(act.activation(proj[u * 64:u * 64 + 64, DQ + 2 * t, :], b[0:64, 0:NT], ACT.Copy))
                    signal(act.activation(proj[u * 64:u * 64 + 64, DQ + 2 * t + 1, :], b[64:128, 0:NT], ACT.Copy), "proj_evac")
                else:
                    signal(act.activation(proj[0:m, dst, :], b[0:m, 0:NT], ACT.Copy), "proj_evac")

            for i in range(n_proj["dq"]):
                evac(i)
            act.wait_ge(*after("sidx_scores", 1))
            act.activation(relu32[0:32, 0:512], bank[6][0:32, :], ACT.Relu).then_inc(S("relu32_ready"), 1)
            act.activation(relu32[0:32, 512:1024], bank[7][0:32, :], ACT.Relu).then_inc(S("relu32_ready"), 1)
            act.activation(relu32[0:32, 1024:1025], bank[3][0:32, 0:1], ACT.Relu).then_inc(S("relu32_ready"), 1)
            for i in range(n_proj["dq"], n_proj["z"]):
                evac(i)
            act.wait_ge(S("proj_evac"), n_proj["z"])
            act.dma_start(memk_prompt[0, 0].rearrange("(a p) h d -> p a (h d)", p=P), mk).then_inc(S("act_stored"), 16)
            act.dma_start(memv_prompt[0, 0].rearrange("(a p) h d -> p a (h d)", p=P), mv).then_inc(S("act_stored"), 16)
            for h in range(4):
                act.wait_ge(*after("mkT_ps", h + 1))
                signal(act.activation(mkT[:, h, :], bank[h % 2][:, 0:256], ACT.Copy), "mkT_ready")
            for a, (c0, w) in enumerate(TOK):
                act.wait_ge(*after("tok_ps", a + 1))
                link(act.activation(ktok[0:w, a, :], bank[6][0:w, 0:256], ACT.Copy))
                link(act.activation(vtok[0:w, a, :], bank[6][0:w, 256:512], ACT.Copy))
                signal(act.activation(iktok[0:w, a, :], bank[7][0:w, 0:64], ACT.Copy), "tok_ready")
            act.wait_ge(*after("tok_ready", 3))
            for dst_p, dst_s, t in ((k_prompt, k_sample, ktok), (v_prompt, v_sample, vtok)):
                act.dma_start(dst_p[0, 0].rearrange("(a p) h d -> p a (h d)", p=P), t[:, 0:2, :]).then_inc(S("act_stored"), 16)
                act.dma_start(dst_s[0].rearrange("b o h d -> (b o) (h d)"), t[0:NS, 2, :]).then_inc(S("act_stored"), 16)
            act.dma_start(kidx_prompt[0, 0].rearrange("(a p) d -> p a d", p=P), iktok[:, 0:2, :]).then_inc(S("act_stored"), 16)
            act.dma_start(kidx_sample[0].rearrange("b o d -> (b o) d"), iktok[0:NS, 2, :]).then_inc(S("act_stored"), 16)

            def exp_it(i):
                act.wait_ge(S("att_nmax"), i + 1)
                w = width(heads_it[i])
                signal(act.activation(smx[:, i % 2, 0:w], smx[:, i % 2, 0:w], ACT.Exp, bias=nmx[:, i % 2:i % 2 + 1],
                                      accum_out=sm[:, i % 2:i % 2 + 1]), "att_exp")

            def out_it(i):
                kind, a, h = heads_it[i]
                act.wait_ge(S("att_o"), i + 1)
                ob = bank[2 + i % 2]
                if kind == "mem":
                    dst, src = oT[:, 8 + h, a * P:(a + 1) * P], ob[:, 0:P]
                else:
                    t, u, j = h // 4, (h // 2) % 2, h % 2
                    dst = oT[u * 64:u * 64 + 64, 4 + 2 * t + j, a * P:(a + 1) * P]
                    src = ob[u * 64:u * 64 + 64, 0:P]
                signal(act.activation(dst, src, ACT.Copy), "att_out")

            for i in range(len(heads_it)):
                exp_it(i)
                if i >= 1:
                    out_it(i - 1)
            out_it(len(heads_it) - 1)

            for m in range(16):
                act.wait_ge(S("smk_ps"), m + 1)
                signal(act.activation(ktbuf[m % 3], bank[m % 2][:, :], ACT.Copy), "smk_ready")
            act.wait_ge(*after("sm_nmax", 1))
            signal(act.activation(S32[0:32, :], S32[0:32, :], ACT.Exp, bias=mx1[0:32, 1:2], accum_out=mx1[0:32, 2:3]), "sm_exp")
            for m in range(32):
                act.wait_ge(S("sk_ps"), m + 1)
                signal(act.activation(ktbuf[(16 + m) % 3], bank[m % 2][:, :], ACT.Copy), "sk_ready")
            act.wait_ge(*after("sa_nmax", 1))
            signal(act.activation(S64[0:64, :], S64[0:64, :], ACT.Exp, bias=mx1[0:64, 1:2], accum_out=mx1[0:64, 2:3]), "sa_exp")

            act.wait_ge(*after("conv_ready", 24))
            sigs = [t for t in range(12)]
            for t in sigs:
                signal(act.activation(nrm[:, t, :], conv[:, t, :], ACT.Sigmoid), "csig_ready")
            act.wait_ge(S("small_loaded"), 112)
            link(act.activation(proj[0:8, BE, :], proj[0:8, BE, :], ACT.Sigmoid))
            act.wait_ge(*after("dtx_ready", 1))
            link(act.activation(proj[0:8, MQ, :], proj[0:8, MQ, :], ACT.Exp, scale=-1.0))
            link(act.activation(proj[0:8, MQ, :], proj[0:8, MQ, :], ACT.Ln, bias=1.0))
            signal(act.activation(alog[0:8, 0:1], alog[0:8, 0:1], ACT.Exp), "softplus_ready")
            for t in range(8):
                act.wait_ge(*after("silu_ready", t + 1))
                signal(act.activation(nrm[:, t, :], conv[:, t, :], ACT.Square), "qksq_ready")
            for t in range(8):
                act.wait_ge(*after("qksum_ps", t + 1))
                signal(act.activation(nrm[:, t, :], bank[t % 4][:, 0:NT], ACT.Sqrt, bias=eps[:, :]), "qkroot_ready")
            act.wait_ge(*after("G_ready", 1))
            act.wait_ge(*after("GL_ready", 1))
            link(act.activation(eG[:, :], Gcols[:, :], ACT.Exp))
            signal(act.activation(eGl[:, :], eGl[:, :], ACT.Exp), "eG_ready")
            for hp in range(4):
                act.wait_ge(*after("EG_ps", hp + 1))
                signal(act.activation(EG[:, hp, :], bank[4 + hp % 2][:, 0:NT], ACT.Exp), "EG_ready")
            for a in range(2):
                act.wait_ge(S("gdiff_ready"), a + 1)
                signal(act.activation(gamT[:, a, :], gamT[:, a, :], ACT.Exp), "gam_ready")
            for t in range(4):
                act.wait_ge(*after("go_ready", t + 1))
                link(act.activation(nrm[:, 8 + t, :], oT[:, t, :], ACT.Square))
                signal(act.activation(nrm[:, 4 + t, :], proj[:, GZ + t, :], ACT.Sigmoid), "osq_ready")
            for t in range(4):
                act.wait_ge(*after("osum_ps", t + 1))
                signal(act.activation(nrm[:, 8 + t, :], bank[t][:, 0:NT], ACT.Sqrt, bias=eps[:, :], scale=1.0 / 64), "oroot_ready")

            for i in range(24):
                act.wait_ge(S("gate_ps"), i + 1)
                if i >= 2:
                    act.wait_ge(S("merge_step"), i - 1)
                signal(act.activation(sgate[:, i % 2, :], bank[i % 2][:, 0:NT], ACT.Sigmoid), "sgate_ready")

            for j, (c0, w) in enumerate(TOK):
                act.wait_ge(*after("x1_ready", 2 * (j + 1)))
                link(act.activation(sqs2[0:w, :], acc[0:w, j, :], ACT.Square, accum_out=ssq[0:w, j:j + 1]))
                signal(act.activation(rinv[0:w, j:j + 1], ssq[0:w, j:j + 1], ACT.Sqrt, bias=eps[0:w, :], scale=1.0 / D), "root2_ready")
            for k in range(KD):
                act.wait_ge(*after("h2T_ps", k + 1))
                signal(act.activation(h2T[:, k, :], bank[k % 4][:, 0:NT], ACT.Copy), "h2T_ready")
            for j, (c0, w) in enumerate(TOK):
                act.wait_ge(S("lmax_ready"), j + 1)
                signal(act.activation(prob[0:w, j, :], logit[0:w, j, :], ACT.Exp, bias=cntf[0:w, j:j + 1]), "pexp_ready")
            act.wait_ge(*after("passes_known", 1))
            passes = act.value_load(npass[0:1, 0:1], min_val=1, max_val=MAX_PASSES)
            act.sem_inc(S("yr_ready"), 1)
            act.sem_inc(S("yT_ready"), 1)
            with act.Fori(0, passes) as q:
                with act.Fori(0, PAIRS) as p:
                    it = q * PAIRS + p
                    act.wait_ge(S("xg_ps"), it + 1)
                    for j in range(2):
                        act.activation(xg[:, 4 * j:4 * j + 4, :], bank[j][:, :].rearrange("p (a b) -> p a b", a=4), ACT.Copy)\
                            .then_inc(S("xg_ready"), 1)
                    for half in range(2):
                        act.wait_ge(S("gate_clipped"), it * 2 + half + 1)
                        act.activation(sg, gb, ACT.Sigmoid, scale=ALPHA).then_inc(S("moe_sig"), 1)
                        act.wait_ge(S("ring_free"), (it * 2 + half + 2) * CHUNKS)
                        act.activation(yT[:, :, half * 64:half * 64 + 64],
                                       bank[4][:, :].rearrange("p (a b) -> p a b", a=8), ACT.Copy).then_inc(S("yT_ready"), 1)
                    act.wait_ge(S("y_ps"), it + 1)
                    for j in range(2):
                        act.activation(yr[:, j * 512:(j + 1) * 512], bank[j][:, :], ACT.Copy).then_inc(S("yr_ready"), 1)
            for j, (c0, w) in enumerate(TOK):
                act.wait_ge(*after("acc_final", 1))
                link(act.activation(sqs2[0:w, :], acc[0:w, j, :], ACT.Square, accum_out=ssq[0:w, j:j + 1]))
                signal(act.activation(rinv[0:w, j:j + 1], ssq[0:w, j:j + 1], ACT.Sqrt, bias=eps[0:w, :], scale=1.0 / D), "root3_ready")
            act.wait_ge(S("act_stored"), 16 * 8)

        @block.tensor
        def _(pe):
            def mm(out, lhsT, rhs, start=True, stop=True, **kw):
                return pe.matmul(out, lhsT, rhs, start=start, stop=stop, **kw)

            def tr(out, in_, m):
                return pe.transpose(out, in_, ident[0:m, 0:m])

            pe.wait_ge(S("ident_ready"), 1)
            pe.wait_ge(S("small_loaded"), 112)
            tr(bank[7][:, 0:64], svec[0:64, :], 64).then_inc(S("sv_ps"), 1)
            pe.wait_ge(*after("x_normed", 5))
            pe.wait_ge(*after("sv_ready", 1))
            for k in range(KD):
                for j, (c0, w) in enumerate(TOK):
                    last = tr(bank[k][:, c0:c0 + w], xraw[0:w, j, k * P:(k + 1) * P], w)
                last.then_inc(S("xT_ps"), 1)
            for k in range(KD):
                pe.wait_ge(*after("hT_ready", k + 1))
                for j in range(2):
                    last = tr(bank[k][:, j * P:(j + 1) * P], memraw[:, j, k * P:(k + 1) * P], P)
                last.then_inc(S("memT_ps"), 1)
            pe.wait_ge(*after("memT_ready", KD))

            def project(i):
                nm, c, m, dst = tiles[i]
                if i == 0 or tiles[i - 1][0] != nm:
                    wait_piece(pe, nm)
                if i >= NPROJ:
                    pe.wait_ge(S("proj_evac"), i - NPROJ + 1)
                w = piece_view(nm)
                for k in range(KD):
                    if nm in ("mkw", "mvw"):
                        last = mm(bank[i % NPROJ][:, :], memT[:, k, c * P:(c + 1) * P], w[:, k, :], k == 0, k == KD - 1)
                    else:
                        last = mm(bank[i % NPROJ][0:m, 0:NT], w[:, k, c:c + m], hT[:, k, :], k == 0, k == KD - 1)
                last.then_inc(S("proj_done"), 1)

            for i in range(n_proj["dq"]):
                project(i)
            pe.wait_ge(*after("Qdi_ready", 8))
            pe.wait_ge(S("idx_loaded"), 16 * 64)
            pe.wait_ge(S("consts_ready"), 1)
            pe.wait_ge(S("proj_evac"), n_proj["idx"])
            for b in range(NS):
                if b >= 2:
                    pe.wait_ge(*after("kiT_ready", b - 1))
                for g in range(4):
                    last = tr(bank[4 + b % 2][:, g * P:(g + 1) * P], idxc[:, b * 4 + g, :], P)
                last.then_inc(S("kiT_ps"), 1)
                if b >= 1:
                    _score = b - 1
                    pe.wait_ge(*after("kiT_ready", b))
                    for h in range(2):
                        last = mm(bank[6 + h][0:32, :], Qdi[h * 64:h * 64 + 64, _score, :],
                                  ktbuf[_score % 2][h * 64:h * 64 + 64, :], _score == 0, False)
                    mm(bank[3][0:32, 0:1], Qdi[0:64, _score, :], proj[0:64, IK, NP + _score:NP + _score + 1],
                       _score == 0, False).then_inc(S("sidx_step"), 1)
            pe.wait_ge(*after("kiT_ready", 8))
            for h in range(2):
                mm(bank[6 + h][0:32, :], Qdi[h * 64:h * 64 + 64, 7, :], ktbuf[1][h * 64:h * 64 + 64, :], False, True)
            mm(bank[3][0:32, 0:1], Qdi[0:64, 7, :], proj[0:64, IK, NP + 7:NP + 8], False, True).then_inc(S("sidx_scores"), 1)
            mm(bank[4][0:32, 0:8], head32[0:4, :], proj[0:4, IW, NP:NT])
            for a in range(2):
                last = tr(bank[5][:, 4 * a:4 * a + 4], proj[0:4, IW, a * P:(a + 1) * P], 4)
            last.then_inc(S("iw_ps"), 1)
            pe.wait_ge(*after("relu32_ready", 3))
            pe.wait_ge(*after("iwtok_ready", 1))
            pe.wait_ge(*after("wmix_ready", 1))
            mm(bank[6][0:8, :], wmix[0:32, :], relu32[0:32, 0:512])
            mm(bank[7][0:8, :], wmix[0:32, :], relu32[0:32, 512:1024])
            mm(bank[3][0:8, 0:1], wmix[0:32, :], relu32[0:32, 1024:1025]).then_inc(S("sc8_ps"), 1)
            for a in range(2):
                if a:
                    pe.wait_ge(S("iscore_read"), a)
                for i in range(4):
                    h0 = (i % 2) * 64
                    last = mm(bank[4 + i % 2][:, (i // 2) * 256:(i // 2) * 256 + 256],
                              proj[h0:h0 + 64, IQ + i // 2, a * P:(a + 1) * P], proj[h0:h0 + 64, IK, 0:NP])
                last.then_inc(S("iscore_ps"), 1)
            for i in range(n_proj["dq"], n_proj["z"]):
                project(i)
            pe.wait_ge(S("proj_evac"), n_proj["z"])
            for h in range(4):
                if h >= 2:
                    pe.wait_ge(*after("mkT_ready", h - 1))
                for j in range(2):
                    last = tr(bank[h % 2][:, j * P:(j + 1) * P], mk[:, j, h * P:(h + 1) * P], P)
                last.then_inc(S("mkT_ps"), 1)
            pe.wait_ge(*after("sc8_read", 3))
            for a, (c0, w) in enumerate(TOK):
                if a:
                    pe.wait_ge(*after("tok_ready", a))
                for t in range(2):
                    tr(bank[6][0:w, t * P:(t + 1) * P], proj[:, DK + t, c0:c0 + w], P)
                    tr(bank[6][0:w, 256 + t * P:256 + (t + 1) * P], proj[:, DV + t, c0:c0 + w], P)
                tr(bank[7][0:w, 0:64], proj[0:64, IK, c0:c0 + w], 64).then_inc(S("tok_ps"), 1)

            def scores(i):
                kind, a, h = heads_it[i]
                if i >= 2:
                    pe.wait_ge(S("att_scaled"), i - 1)
                out = bank[4 + i % 2][:, 0:width(heads_it[i])]
                if kind == "mem":
                    m = mm(out, proj[:, MQ + h, a * P:(a + 1) * P], mkT[:, h, :])
                else:
                    t, u, j = h // 4, (h // 2) % 2, h % 2
                    r = slice(u * 64, u * 64 + 64)
                    m = mm(out, proj[r, DQ + 2 * t + j, a * P:(a + 1) * P], proj[r, DK + t, 0:width(heads_it[i])])
                m.then_inc(S("att_s"), 1)

            pe.wait_ge(*after("mkT_ready", 4))
            pe.wait_ge(*after("tok_ready", 3))
            pe.wait_ge(S("iscore_read"), 2)
            scores(0)
            for i, (kind, a, h) in enumerate(heads_it):
                if i + 1 < len(heads_it):
                    scores(i + 1)
                nk = width(heads_it[i]) // P
                pe.wait_ge(S("att_p"), i + 1)
                if i >= 2:
                    pe.wait_ge(S("att_pT"), i - 1)
                for c in range(nk):
                    last = tr(bank[6 + i % 2][:, c * P:(c + 1) * P], smx[:, i % 2, c * P:(c + 1) * P], P)
                last.then_inc(S("att_pT_ps"), 1)
                pe.wait_ge(S("att_pT"), i + 1)
                if i >= 2:
                    pe.wait_ge(S("att_out"), i - 1)
                for c in range(nk):
                    if kind == "mem":
                        last = mm(bank[2 + i % 2][:, 0:P], mv[:, c, h * P:(h + 1) * P], pts[:, i % 2, c * P:(c + 1) * P],
                                  c == 0, c == nk - 1)
                    else:
                        u, kv = (h // 2) % 2, h // 2
                        last = mm(bank[2 + i % 2][u * 64:u * 64 + 64, 0:P], vtok[:, c, kv * 64:kv * 64 + 64],
                                  pts[:, i % 2, c * P:(c + 1) * P], c == 0, c == nk - 1)
                last.then_inc(S("att_o"), 1)

            pe.wait_ge(S("att_out"), len(heads_it))
            pe.wait_ge(*after("Qm_ready", 1))

            def mem_scores(m):
                pe.wait_ge(*after("smk_ready", m + 1))
                for j in range(2):
                    h = 2 * (m % 2) + j
                    r = (m // 2) * 4 + h
                    last = mm(bank[4][0:32, 0:256], Qm[:, r, :], ktbuf[m % 3][:, j * 256:(j + 1) * 256],
                              r == 0, r == 31)
                last.then_inc(S("smk_used"), 1)

            for m in range(16):
                b = m // 2
                if m % 4 == 0:
                    wait_unit(pe, m // 4)
                if m >= 2:
                    pe.wait_ge(*after("smk_ready", m - 1))
                src = kvbuf[(m // 4) % 3][:, (b % 2) * 1024:(b % 2) * 1024 + 1024]
                for j in range(2):
                    h = 2 * (m % 2) + j
                    for c in range(2):
                        last = tr(bank[m % 2][:, j * 256 + c * P:j * 256 + (c + 1) * P],
                                  src[:, c * 512 + h * P:c * 512 + (h + 1) * P], P)
                last.then_inc(S("smk_ps"), 1)
                if m >= 1:
                    mem_scores(m - 1)
            mem_scores(15)

            pe.wait_ge(*after("QdT_ready", 1))

            def key_scores(m):
                b, t, hf = m // 4, (m // 2) % 2, m % 2
                pe.wait_ge(*after("sk_ready", m + 1))
                if hf == 0:
                    mm(bank[3][0:64, 0:1], QdT[:, b * 2 + t, :], proj[:, DK + t, NP + b:NP + b + 1], m == 0, False)
                mm(bank[6 + hf][0:64, :], QdT[:, b * 2 + t, :], ktbuf[(16 + m) % 3], m < 2, False).then_inc(S("sk_used"), 1)

            for m in range(32):
                b, t, hf = m // 4, (m // 2) % 2, m % 2
                u = 4 + b
                if m % 4 == 0:
                    wait_unit(pe, u)
                if m >= 2:
                    pe.wait_ge(*after("sk_ready", m - 1))
                for g in range(4):
                    pg = hf * 4 + g
                    last = tr(bank[m % 2][:, g * P:(g + 1) * P], kvbuf[u % 3][:, pg * 256 + t * P:pg * 256 + (t + 1) * P], P)
                last.then_inc(S("sk_ps"), 1)
                if m >= 1:
                    key_scores(m - 1)
            key_scores(31)
            pe.wait_ge(*after("sm_p", 1))
            for c in range(2):
                last = tr(bank[0][:, c * 32:(c + 1) * 32], S32[0:32, c * P:(c + 1) * P], 32)
            last.then_inc(S("PTm_ps"), 1)
            pe.wait_ge(*after("PTm_ready", 1))
            for b in range(NS):
                u = 12 + b // 2
                if b % 2 == 0:
                    wait_unit(pe, u)
                src = kvbuf[u % 3][:, (b % 2) * 1024:(b % 2) * 1024 + 1024]
                for h in range(4):
                    for c in range(2):
                        last = mm(bank[5][:, h * 8 + b:h * 8 + b + 1], src[:, c * 512 + h * P:c * 512 + (h + 1) * P],
                                  PTm[:, c, b * 4 + h:b * 4 + h + 1], c == 0, c == 1)
                last.then_inc(S("smv_step"), 1)
            pe.wait_ge(*after("bias8_ready", 1))
            mm(bank[6][0:64, :], seq64[0:8, :], sc8[0:8, 0:512], False, True)
            mm(bank[7][0:64, :], seq64[0:8, :], sc8[0:8, 512:1024], False, True)
            mm(bank[3][0:64, 0:1], seq64[0:8, :], sc8[0:8, 1024:1025], False, True).then_inc(S("s64_ps"), 1)
            pe.wait_ge(*after("sa_p", 1))
            for g in range(8):
                tr(bank[0][:, g * 64:(g + 1) * 64], S64[0:64, g * P:(g + 1) * P], 64)
            tr(bank[1][0:8, 0:64], pnew[0:64, :], 64).then_inc(S("PT64_ps"), 1)
            pe.wait_ge(*after("PT64_ready", 2))
            for t in range(2):
                mm(bank[3][:, t * 64:(t + 1) * 64], vtok[0:8, 2, t * P:(t + 1) * P], pnewT[0:8, :])
            for b in range(NS):
                u = 16 + b
                wait_unit(pe, u)
                for t in range(2):
                    for pg in range(NPAGES):
                        last = mm(bank[2][:, t * 32 + b * 4:t * 32 + b * 4 + 4],
                                  kvbuf[u % 3][:, pg * 256 + t * P:pg * 256 + (t + 1) * P],
                                  PT64[:, pg, b * 8 + 4 * t:b * 8 + 4 * t + 4], pg == 0, pg == 7)
                last.then_inc(S("sv_step"), 1)

            pe.wait_ge(*after("so_read", 3))
            pe.wait_ge(S("state_rows"), 16)
            for t in range(12):
                last = tr(bank[4][:, t * 24:(t + 1) * 24], srow[0:24, t * P:(t + 1) * P], 24)
            last.then_inc(S("cstate_ps"), 1)
            for t in range(12):
                last = tr(bank[5 + t // 4][0:11, (t % 4) * P:(t % 4 + 1) * P], proj[:, GQ + t, NP - 3:NT], P)
            last.then_inc(S("crow_ps"), 1)
            pe.wait_ge(*after("crow_ready", 1))
            for t in range(8):
                pe.wait_ge(*after("qksq_ready", t + 1))
                if t >= 4:
                    pe.wait_ge(*after("qkroot_ready", t - 3))
                mm(bank[t % 4][:, 0:NT], blockones[:, :], nrm[:, t, :]).then_inc(S("qksum_ps"), 1)
            pe.wait_ge(*after("gT_ready", 1))
            for a in range(2):
                tr(bank[4][:, 8 * a:8 * a + 8], proj[0:8, BE, a * P:(a + 1) * P], 8)
                last = tr(bank[4][:, 16 + 8 * a:24 + 8 * a], proj[0:8, AA, a * P:(a + 1) * P], 8)
            last.then_inc(S("bg_ps"), 1)
            pe.wait_ge(*after("bg_ready", 2))
            mm(bank[5][:, 0:16], cumul[:, :], gcols[:, :])
            mm(bank[5][:, 16:32], blockones[:, :], gcols[:, :]).then_inc(S("G_ps"), 1)
            pe.wait_ge(*after("G_ready", 1))
            for a in range(2):
                last = tr(bank[6][0:8, a * P:(a + 1) * P], Gcols[:, 8 * a:8 * a + 8], P)
            last.then_inc(S("GT_ps"), 1)
            pe.wait_ge(*after("GT_ready", 1))
            for hp in range(4):
                if hp >= 2:
                    pe.wait_ge(*after("EG_ready", hp - 1))
                mm(bank[4 + hp % 2][:, 0:NT], headsel[0:8, hp * P:(hp + 1) * P], proj[0:8, AA, :]).then_inc(S("EG_ps"), 1)
            for hp in range(4):
                last = mm(bank[7][:, hp * 8:hp * 8 + 8], headsel[0:8, hp * P:(hp + 1) * P], proj[0:8, BE, NP:NT])
            last.then_inc(S("BEs_ps"), 1)
            for a in range(2):
                for w, name in ((0, "G"), (1, "B")):
                    pe.wait_ge(S("diag_ready"), 2 * a + w + 1)
                    mm(bank[6][:, :], blockones[:, :], dg).then_inc(S("row_ps"), 1)
                    pe.wait_ge(S("row_read"), 2 * a + w + 1)
            pe.wait_ge(*after("EG_ready", 4))
            pe.wait_ge(*after("qk_ready", 8))
            for a in range(2):
                for h in range(8):
                    r = slice((h % 2) * 64, (h % 2) * 64 + 64)
                    for nn in range(2):
                        cs = slice(a * P + nn * 64, a * P + nn * 64 + 64)
                        o = slice(nn * 64, nn * 64 + 64)
                        half = slice((h // 2) * 64, (h // 2) * 64 + 64)
                        mm(bank[4 * a + h % 2][o, half], conv[r, 4 + h // 2, cs], conv[r, 4 + h // 2, cs])
                        last = mm(bank[4 * a + 2 + h % 2][o, half], conv[r, 4 + h // 2, cs], conv[r, h // 2, cs])
                last.then_inc(S("kk_ps"), 1)
            pe.wait_ge(*after("kk_read", 2))
            for a in range(2):
                if a:
                    pe.wait_ge(*after("kv_tok", 4 * a))
                for t in range(4):
                    tr(bank[4][:, t * P:(t + 1) * P], conv[:, 4 + t, a * P:(a + 1) * P], P)
                    last = tr(bank[5][:, t * P:(t + 1) * P], conv[:, 8 + t, a * P:(a + 1) * P], P)
                last.then_inc(S("kvtok_ps"), 1)
            pe.wait_ge(*after("BEs_ready", 1))
            for t in range(4):
                last = tr(bank[7][0:8, t * P:(t + 1) * P], conv[:, 4 + t, NP:NT], P)
            last.then_inc(S("ksr_ps"), 1)
            for l in range(6):
                for a in range(2):
                    pe.wait_ge(S("lvl_ready"), 2 * l + a + 1)
                    if l:
                        pe.wait_ge(S("XT_ready"), 2 * (l - 1) + a + 1)
                    else:
                        pe.wait_ge(*after("kv_tok", 8))
                    for h in range(8):
                        for nn in range(2):
                            o = slice(nn * 64, nn * 64 + 64)
                            hs = slice(h * 64, (h + 1) * 64)
                            last = mm(bank[4 + a][o, hs], Lm[o, a, hs], X[o, a, hs])
                    last.then_inc(S("T1_ps"), 1)
                for a in range(2):
                    pe.wait_ge(S("T1_ready"), 2 * l + a + 1)
                    for h in range(8):
                        for nn in range(2):
                            o = slice(nn * 64, nn * 64 + 64)
                            hs = slice(h * 64, (h + 1) * 64)
                            mm(bank[0 + a][o, hs], XT[o, a, hs], T1[o, a, hs])
                            last = mm(bank[2 + a][o, hs], T1[o, a, hs], XT[o, a, hs])
                    last.then_inc(S("T2_ps"), 1)
            pe.wait_ge(S("XT_ready"), 12)
            for a in range(2):
                for h in range(8):
                    for nn in range(2):
                        o = slice(nn * 64, nn * 64 + 64)
                        hs = slice(h * 64, (h + 1) * 64)
                        r = slice((h % 2) * 64, (h % 2) * 64 + 64)
                        mm(bank[4 + a][o, hs], XT[o, a, hs], vb[o, a, hs])
                        last = mm(bank[6 + nn][r, (h // 2) * P + a * 64:(h // 2) * P + a * 64 + 64], kbG[o, a, hs], XT[o, a, hs])
                last.then_inc(S("uw_ps"), 1)
            for c in range(4):
                a, nn = c // 2, c % 2
                o = slice(nn * 64, nn * 64 + 64)
                cs = slice(c * 64, c * 64 + 64)
                if c == 0:
                    pe.wait_ge(*after("uw_ready", 4))
                    pe.wait_ge(*after("qg_ready", 4))
                    pe.wait_ge(*after("state0", 1))
                else:
                    pe.wait_ge(S("state_ready"), c)
                for h in range(8):
                    r = slice((h % 2) * 64, (h % 2) * 64 + 64)
                    last = mm(bank[4 + h % 2][o, (h // 2) * 64:(h // 2) * 64 + 64], wT[r, h // 2, cs], St[r, h // 2, :])
                last.then_inc(S("wS_ps"), 1)
                pe.wait_ge(S("vn_ready"), 2 * c + 2)
                for h in range(8):
                    r = slice((h % 2) * 64, (h % 2) * 64 + 64)
                    hs = slice(h * 64, (h + 1) * 64)
                    oc = slice(((h // 2) % 2) * 256 + c * 64, ((h // 2) % 2) * 256 + c * 64 + 64)
                    mm(bank[h // 4][r, oc], St[r, h // 2, :], conv[r, h // 2, cs])
                    mm(bank[2 + h // 4][r, oc], vn[o, hs], qkT[o, a, hs])
                    last = mm(bank[6][r, (h // 2) * 64:(h // 2) * 64 + 64], kd[o, a, hs], vn[o, hs])
                last.then_inc(S("dS_ps"), 1)
            pe.wait_ge(*after("o_read", 1))
            pe.wait_ge(S("sstate_loaded"), 32)
            pe.wait_ge(*after("qk_ready", 8))
            for b in range(NS):
                for h in range(8):
                    r = slice((h % 2) * 64, (h % 2) * 64 + 64)
                    last = mm(bank[2][r, (h // 2) * 8 + b:(h // 2) * 8 + b + 1], sS[r, b, h // 2, :],
                              conv[r, 4 + h // 2, NP + b:NP + b + 1])
            last.then_inc(S("kS_ps"), 1)
            pe.wait_ge(*after("vnT_ready", 1))
            for t in range(4):
                last = tr(bank[3][0:8, t * P:(t + 1) * P], vnT[:, t, :], P)
            last.then_inc(S("vnr_ps"), 1)
            for hp in range(4):
                pe.wait_ge(S("vnx_ready"), hp + 1)
                for hh in range(2):
                    h = 2 * hp + hh
                    last = mm(bank[6 + hp % 2][hh * 64:hh * 64 + 64, :], ksr[0:8, h * 64:(h + 1) * 64], vnx[0:8, hh, :])
                last.then_inc(S("outer_ps"), 1)
                pe.wait_ge(S("sS_ready"), hp + 1)
            for b in range(NS):
                for h in range(8):
                    r = slice((h % 2) * 64, (h % 2) * 64 + 64)
                    last = mm(bank[2][r, (h // 2) * 8 + b:(h // 2) * 8 + b + 1], sS[r, b, h // 2, :],
                              conv[r, h // 2, NP + b:NP + b + 1])
            last.then_inc(S("so_ps"), 1)
            pe.wait_ge(*after("go_ready", 4))
            for t in range(4):
                pe.wait_ge(*after("osq_ready", t + 1))
                mm(bank[t][:, 0:NT], blockones[:, :], nrm[:, 8 + t, :]).then_inc(S("osum_ps"), 1)
            pe.wait_ge(*after("og_ready", 4))

            i = 0
            for nb in range(3):
                wait_piece(pe, f"br{nb}")
                wb = piece_view(f"br{nb}")
                for d in range(KD):
                    hf = d // 4
                    if d % 4 == 0:
                        wait_piece(pe, f"g{nb}{hf}")
                    wg = piece_view(f"g{nb}{hf}")
                    if i >= 2:
                        pe.wait_ge(S("sgate_ready"), i - 1)
                    for k in range(KD):
                        last = mm(bank[i % 2][:, 0:NT], wg[:, k, (d % 4) * P:(d % 4 + 1) * P], hT[:, k, :], k == 0, k == KD - 1)
                    last.then_inc(S("gate_ps"), 1)
                    if i >= 2:
                        pe.wait_ge(S("merge_step"), i - 1)
                    for c in range(4):
                        last = mm(bank[2 + i % 2][:, 0:NT], wb[:, c, d * P:(d + 1) * P], oT[:, 4 * nb + c, :], c == 0, c == 3)
                    last.then_inc(S("br_ps"), 1)
                    i += 1
            pe.wait_ge(S("merge_step"), 24)
            for hf in range(2):
                wait_piece(pe, f"wo{hf}")
                w = piece_view(f"wo{hf}")
                for j, (c0, m) in enumerate(TOK):
                    for k in range(KD):
                        last = mm(bank[hf * 3 + j][0:m, :], mergedT[:, k, c0:c0 + m], w[:, k, :], k == 0, k == KD - 1)
                    last.then_inc(S("x1_ps"), 1)
            pe.wait_ge(*after("h2_ready", 3))
            pe.wait_ge(*after("x1_ready", 6))
            for k in range(KD):
                if k >= 4:
                    pe.wait_ge(*after("h2T_ready", k - 3))
                for j, (c0, w) in enumerate(TOK):
                    last = tr(bank[k % 4][:, c0:c0 + w], h2[0:w, j, k * P:(k + 1) * P], w)
                last.then_inc(S("h2T_ps"), 1)
            pe.wait_ge(*after("h2T_ready", KD))
            pe.wait_ge(S("moe_small"), 16 * 5)
            for j, (c0, w) in enumerate(TOK):
                for k in range(KD):
                    last = mm(bank[4][0:w, j * NE:(j + 1) * NE], h2T[:, k, c0:c0 + w], wr[:, k, :], k == 0, k == KD - 1)
                last.then_inc(S("logit_ps"), 1)
            for g in range(4):
                last = tr(bank[5][:, g * P:(g + 1) * P], bgr[:, g, :], P)
            last.then_inc(S("bgu_ps"), 1)
            pe.wait_ge(S("sel_ready"), 3)
            mm(bank[6][:, 0:NE], before[:, :], sel[:, 0, :])
            mm(bank[6][:, NE:2 * NE], before[:, :], sel[:, 1, :], True, False)
            mm(bank[6][:, NE:2 * NE], ones[:, :], sel[:, 0, :], False, True)
            mm(bank[6][0:NS, 2 * NE:3 * NE], before[0:NS, 0:NS], sel[0:NS, 2, :], True, False)
            mm(bank[6][0:NS, 2 * NE:3 * NE], ones[:, 0:NS], sel[:, 0, :], False, False)
            mm(bank[6][0:NS, 2 * NE:3 * NE], ones[:, 0:NS], sel[:, 1, :], False, True)
            mm(bank[6][0:1, 3 * NE:4 * NE], ones[:, 0:1], sel[:, 0, :], True, False)
            mm(bank[6][0:1, 3 * NE:4 * NE], ones[:, 0:1], sel[:, 1, :], False, False)
            mm(bank[6][0:1, 3 * NE:4 * NE], ones[0:NS, 0:1], sel[0:NS, 2, :], False, True).then_inc(S("rank_ps"), 1)
            pe.wait_ge(S("prob_ready"), 3)
            for j, (c0, w) in enumerate(TOK):
                last = tr(bank[7][0:NE, c0:c0 + w], prob[0:w, j, :], w)
            last.then_inc(S("probT_ps"), 1)
            pe.wait_ge(*after("probT_ready", 1))
            i = 0
            for j, (c0, w) in enumerate(TOK):
                for hf in range(2):
                    if i >= 2:
                        pe.wait_ge(*after("bd_added", i - 1))
                    mm(bank[i % 2][0:w, :], probT[0:NE, c0:c0 + w], bdn[0:NE, hf * 512:(hf + 1) * 512]).then_inc(S("bd_ps"), 1)
                    i += 1
            pe.wait_ge(*after("bd_added", 6))
            pe.wait_ge(*after("passes_known", 1))
            passes = pe.value_load(npass[0:1, 0:1], min_val=1, max_val=MAX_PASSES)
            pe.sem_inc(S("SwT_ps"), 1)
            pe.sem_inc(S("add_ps"), 1)
            with pe.Fori(0, passes) as q:
                with pe.Fori(0, PAIRS) as p:
                    it = pe.snap(q * PAIRS + p)
                    pe.wait_ge(S("slots_built"), it + 1)
                    pe.wait_ge(S("yr_ready"), it * 2 + 1)
                    for d in range(KD):
                        for j, (c0, w) in enumerate(TOK):
                            last = mm(bank[d // 4][:, (d % 4) * P:(d % 4 + 1) * P], h2[0:w, j, d * P:(d + 1) * P],
                                      Sg[0:w, j, :, :].rearrange("p a b -> p (a b)"), j == 0, j == 2)
                    last.then_inc(S("xg_ps"), 1)
                    pe.wait_ge(S("SwT_ready"), it + 1)
                    for j, (c0, w) in enumerate(TOK):
                        last = tr(bank[5][:, c0:c0 + w], Sw[0:w, j, :, :].rearrange("p a b -> p (a b)"), w)
                    last.then_inc(S("SwT_ps"), 1)
                    pe.wait_ge(S("xg_ready"), it * 2 + 2)
                    for half in range(2):
                        loaded = pe.snap((it * 2 + half + 1) * 16)
                        pe.wait_ge(S("act_ready"), it * 2 + half + 1)
                        for k in range(KD):
                            pe.wait_ge(S(f"chunk{k}_loaded"), loaded)
                            for m in range(16):
                                last = mm(bank[2 + m // 8][:, (m % 8) * 64:(m % 8) * 64 + 64],
                                          ring[:, k, m * P:(m + 1) * P], xg[:, k, half * 64:half * 64 + 64],
                                          k == 0 and m % 8 == 0, k == KD - 1, skip_group_check=True)
                            last.then_inc(S("ring_free"), 1)
                        pe.wait_ge(S("act_ready"), it * 2 + half + 1 + 1)
                        pe.wait_ge(S("yT_ready"), it * 2 + half + 1)
                        for m in range(8):
                            if m % 2 == 0:
                                pe.wait_ge(S(f"chunk{KD + m // 2}_loaded"), loaded)
                            for d in range(KD):
                                last = mm(bank[4][:, d * 64:(d + 1) * 64],
                                          ring[:, KD + m // 2, (m % 2) * D + d * P:(m % 2) * D + (d + 1) * P],
                                          actT[:, m, :], m == 0 and d == 0, m == 7, skip_group_check=True)
                            if m % 2 == 1:
                                last.then_inc(S("ring_free"), 1)
                    pe.wait_ge(S("yT_ready"), it * 2 + 2 + 1)
                    for d in range(KD):
                        last = tr(bank[d // 4][:, (d % 4) * P:(d % 4 + 1) * P], yT[:, d, :], P)
                    last.then_inc(S("y_ps"), 1)
                    pe.wait_ge(S("yr_ready"), it * 2 + 2 + 1)
                    pe.wait_ge(S("SwT_ready"), it + 1 + 1)
                    i = 0
                    for j, (c0, w) in enumerate(TOK):
                        for hf in range(2):
                            pe.wait_ge(S("y_added"), it * 6 + max(i - 1, 0) + 1)
                            mm(bank[6 + i % 2][0:w, :], SwT[:, c0:c0 + w], yr[:, hf * 512:(hf + 1) * 512]).then_inc(S("add_ps"), 1)
                            i += 1

        @block.vector
        def _(ve):
            n = [0]

            def link(ins):
                n[0] += 1
                ins.then_inc(S("ve_done"), 1)
                ve.wait_ge(S("ve_done"), n[0])

            def signal(ins, name):
                ins.then_inc(S(name), 1)

            def bc(ap, *shape):
                return ap.to_broadcast(list(shape))

            ve.wait_ge(*after("sv_ps", 1))
            signal(ve.tensor_copy(svT[:, :], bank[7][:, 0:64]), "sv_ready")
            ve.wait_ge(*after("root_ready", 1))
            for j, m in enumerate([P, P, NS, P, P]):
                link(ve.reciprocal(rinv[0:m, j:j + 1], rinv[0:m, j:j + 1]))
            for j, (t, m) in enumerate([(xraw[:, 0, :], P), (xraw[:, 1, :], P), (xraw[:, 2, :], NS),
                                        (memraw[:, 0, :], P), (memraw[:, 1, :], P)]):
                signal(ve.tensor_scalar(t[0:m, :], t[0:m, :], rinv[0:m, j:j + 1], None, ALU.mult), "x_normed")
            ve.wait_ge(*after("sv_ready", 1))
            for k in range(KD):
                ve.wait_ge(*after("xT_ps", k + 1))
                signal(ve.tensor_scalar(hT[:, k, :], bank[k][:, 0:NT], svT[:, k:k + 1], None, ALU.mult), "hT_ready")
            for k in range(KD):
                ve.wait_ge(*after("memT_ps", k + 1))
                signal(ve.tensor_scalar(memT[:, k, :], bank[k][:, 0:NP], svT[:, 8 + k:9 + k], None, ALU.mult), "memT_ready")
            ve.wait_ge(S("consts_ready"), 1)
            link(ve.tensor_copy(iota_slot[:, :], slot_i[:, :]))
            ve.wait_ge(S("consts_ready"), 1)
            link(ve.tensor_scalar(ec_i[:, :], ec_i[:, :], 63, None, ALU.bitwise_and))
            link(ve.tensor_tensor(xc_i[:, :], xc_i[:, :], ec_i[:, :], ALU.bitwise_xor))
            for l in range(6):
                link(ve.tensor_scalar(lv_i[:, :], xc_i[:, :], l, None, ALU.logical_shift_right))
                link(ve.tensor_scalar(level[:, l * 64:(l + 1) * 64], lv_i[:, :], 1, None, ALU.is_equal))
                link(ve.tensor_tensor(level[:, l * 64:(l + 1) * 64], level[:, l * 64:(l + 1) * 64], strict[:, :], ALU.mult))
            link(ve.memset(Qdi, 0.0))
            ve.wait_ge(S("proj_evac"), 2)
            for i in range(4):
                s0 = (i % 2) * 64
                for h in range(2):
                    at = Z0 + 9216 + i
                    dst = A[h * 64:h * 64 + 64, at:at + 7 * 36 + 1:36]
                    signal(ve.tensor_copy(dst, proj[s0:s0 + 64, IQ + i // 2, NP:NT]), "Qdi_ready")
            for b in range(NS):
                ve.wait_ge(S("kiT_ps"), b + 1)
                if b >= 2:
                    ve.wait_ge(S("sidx_step"), b - 1)
                signal(ve.tensor_copy(ktbuf[b % 2], bank[4 + b % 2][:, :]), "kiT_ready")
            ve.wait_ge(*after("iw_ps", 1))
            signal(ve.scalar_tensor_tensor(out=wmix[0:32, :], in0=bank[4][0:32, 0:8], scalar=0.0625,
                                           in1=seq32t[0:32, :], op0=ALU.mult, op1=ALU.mult), "wmix_ready")
            signal(ve.tensor_scalar(iwtok[:, :], bank[5][:, 0:8], 0.0625, None, ALU.mult), "iwtok_ready")
            ve.wait_ge(*after("sc8_ps", 1))
            signal(ve.tensor_scalar(sc8[0:8, 0:512], bank[6][0:8, :], 0.0, None, ALU.add), "sc8_read")
            signal(ve.tensor_scalar(sc8[0:8, 512:1024], bank[7][0:8, :], 0.0, None, ALU.add), "sc8_read")
            signal(ve.tensor_scalar(sc8[0:8, 1024:1025], bank[3][0:8, 0:1], 0.0, None, ALU.add), "sc8_read")
            for a in range(2):
                ve.wait_ge(*after("iscore_ps", a + 1))
                for i in range(4):
                    src = bank[4 + i % 2][:, (i // 2) * 256:(i // 2) * 256 + 256]
                    dst = biasP[:, a, :] if i == 0 else smt
                    link(ve.tensor_scalar(dst, src, 0.0, iwtok[:, 4 * a + i:4 * a + i + 1], ALU.max, ALU.mult))
                    if i in (1, 2):
                        link(ve.tensor_tensor(biasP[:, a, :], biasP[:, a, :], smt, ALU.add))
                    if i == 3:
                        ve.sem_inc(S("iscore_read"), 1)
                        link(ve.tensor_tensor(biasP[:, a, :], biasP[:, a, :], smt, ALU.add))
                        signal(ve.tensor_scalar(biasP[:, a, :], biasP[:, a, :], 0.0, None, ALU.add), "iscore_ready")
            for a in range(2):
                ve.wait_ge(S("iscore_masked"), a + 1)
                for r in range(TOP_PROMPT // 8):
                    link(ve.max(top8[:, :], biasP[:, a, :]))
                    link(ve.match_replace(biasP[:, a, :], top8[:, :], biasP[:, a, :], TAKEN))
                signal(ve.tensor_scalar(biasP[:, a, :], biasP[:, a, :], -2.9e38, NEG, ALU.is_gt, ALU.mult), "ibias_ready")
            ve.wait_ge(*after("sc8_read", 3))
            for r in range(TOP_SAMPLE // 8):
                link(ve.max(top8[0:8, :], sc8[0:8, :]))
                link(ve.match_replace(sc8[0:8, :], top8[0:8, :], sc8[0:8, :], TAKEN))
            signal(ve.tensor_scalar(sc8[0:8, :], sc8[0:8, :], -2.9e38, NEG, ALU.is_gt, ALU.mult), "bias8_ready")

            ve.wait_ge(S("ibias_masked"), 2)

            def scale(i):
                kind, a, h = heads_it[i]
                w = width(heads_it[i])
                ve.wait_ge(S("att_s"), i + 1)
                if i >= 2:
                    ve.wait_ge(S("att_pT_ps"), i - 1)
                src = bank[4 + i % 2][:, 0:w]
                if kind == "mem":
                    signal(ve.tensor_scalar(smx[:, i % 2, :], src, P ** -0.5, None, ALU.mult), "att_scaled")
                else:
                    signal(ve.scalar_tensor_tensor(out=smx[:, i % 2, 0:w], in0=src, scalar=64 ** -0.5, in1=biasP[:, a, 0:w],
                                                   op0=ALU.mult, op1=ALU.add), "att_scaled")
                ve.wait_ge(S("att_scaled"), i + 1)
                link(ve.reduce_max(mx[:, i % 2:i % 2 + 1], smx[:, i % 2, 0:w], AX))
                signal(ve.tensor_scalar(nmx[:, i % 2:i % 2 + 1], mx[:, i % 2:i % 2 + 1], -1.0, None, ALU.mult), "att_nmax")

            def norm(i):
                w = width(heads_it[i])
                ve.wait_ge(S("att_exp"), i + 1)
                link(ve.reciprocal(rs[:, i % 2:i % 2 + 1], sm[:, i % 2:i % 2 + 1]))
                signal(ve.tensor_scalar(smx[:, i % 2, 0:w], smx[:, i % 2, 0:w], rs[:, i % 2:i % 2 + 1], None, ALU.mult), "att_p")

            def ptout(i):
                w = width(heads_it[i])
                ve.wait_ge(S("att_pT_ps"), i + 1)
                if i >= 2:
                    ve.wait_ge(S("att_o"), i - 1)
                signal(ve.tensor_copy(pts[:, i % 2, 0:w], bank[6 + i % 2][:, 0:w]), "att_pT")

            scale(0)
            for i in range(len(heads_it)):
                if i + 1 < len(heads_it):
                    scale(i + 1)
                norm(i)
                ptout(i)

            link(ve.memset(Qm, 0.0))
            for h in range(4):
                at = Z0 + 4096 + h * 33
                ins = ve.tensor_copy(A[:, at:at + 7 * 132 + 1:132], proj[:, MQ + h, NP:NT])
                if h < 3:
                    link(ins)
                else:
                    signal(ins, "Qm_ready")
            link(ve.memset(QdT, 0.0))
            for t in range(2):
                for u in range(2):
                    for j in range(2):
                        at = Z0 + 3072 + t * 64 + 4 * t + 2 * u + j
                        ins = ve.tensor_copy(A[u * 64:u * 64 + 64, at:at + 7 * 136 + 1:136],
                                             proj[u * 64:u * 64 + 64, DQ + 2 * t + j, NP:NT])
                        if (t, u, j) == (1, 1, 1):
                            signal(ins, "QdT_ready")
                        else:
                            link(ins)

            def softmax_rows(rows, dst, wait, nmax, expd, m):
                link(ve.reduce_max(mx1[0:rows, 0:1], dst, AX))
                signal(ve.tensor_scalar(mx1[0:rows, 1:2], mx1[0:rows, 0:1], -1.0, None, ALU.mult), nmax)
                ve.wait_ge(*after(expd, 1))
                link(ve.reciprocal(mx1[0:rows, 3:4], mx1[0:rows, 2:3]))
                ins = ve.tensor_scalar(dst, dst, mx1[0:rows, 3:4], None, ALU.mult)
                return ins

            ve.wait_ge(S("smk_used"), 16)
            link(ve.tensor_scalar(S32[0:32, :], bank[4][0:32, 0:256], P ** -0.5, None, ALU.mult))
            signal(softmax_rows(32, S32[0:32, :], None, "sm_nmax", "sm_exp", 0), "sm_p")
            ve.wait_ge(*after("PTm_ps", 1))
            signal(ve.tensor_copy(PTm, bank[0][:, 0:64].rearrange("p (a b) -> p a b", a=2)), "PTm_ready")
            ve.wait_ge(*after("smv_step", 8))
            for h in range(4):
                link(ve.tensor_copy(oT[:, 8 + h, NP:NT], bank[5][:, h * 8:h * 8 + 8]))
            ve.wait_ge(*after("s64_ps", 1))
            link(ve.tensor_scalar(S64[0:64, 0:512], bank[6][0:64, :], 0.125, None, ALU.mult))
            link(ve.tensor_scalar(S64[0:64, 512:1024], bank[7][0:64, :], 0.125, None, ALU.mult))
            link(ve.tensor_scalar(S64[0:64, 1024:1025], bank[3][0:64, 0:1], 0.125, None, ALU.mult))
            link(softmax_rows(64, S64[0:64, :], None, "sa_nmax", "sa_exp", 1))
            signal(ve.tensor_scalar(pnew[0:64, :], seq64t[0:64, :], S64[0:64, 1024:1025], None, ALU.mult), "sa_p")
            ve.wait_ge(*after("PT64_ps", 1))
            signal(ve.tensor_copy(PT64, bank[0][:, :].rearrange("p (a b) -> p a b", a=8)), "PT64_ready")
            signal(ve.tensor_copy(pnewT[0:8, :], bank[1][0:8, 0:64]), "PT64_ready")
            ve.wait_ge(*after("sv_step", 8))
            for t in range(2):
                for u in range(2):
                    r = slice(u * 64, u * 64 + 64)
                    for j in range(2):
                        c2 = t * 32 + 2 * u + j
                        c3 = t * 64 + 4 * t + 2 * u + j
                        dst = oT[r, 4 + 2 * t + j, NP:NT]
                        link(ve.tensor_copy(dst, bank[2][r, c2:c2 + 29:4]))
                        link(ve.tensor_tensor(dst, dst, bank[3][r, c3:c3 + 57:8], ALU.add))
            ve.sem_inc(S("so_read"), 3)

            ve.wait_ge(S("act_stored"), 16 * 8)
            ve.wait_ge(*after("cstate_ps", 1))
            link(ve.tensor_copy(xst[:, :, :, 0:3], bank[4][:, 0:288].rearrange("p (t b i) -> p t b i", t=12, b=8)))
            for t in range(12):
                link(ve.tensor_copy(xst[:, t, :, 3], proj[:, GQ + t, NP:NT]))
            ve.wait_ge(*after("crow_ps", 1))
            for g in range(3):
                link(ve.tensor_copy(conv_rows[32:43, g * 512:(g + 1) * 512], bank[5 + g][0:11, :]))
            ve.sem_inc(S("crow_ready"), 1)
            for t in range(12):
                w = [svT[:, 16 + i * 12 + t:17 + i * 12 + t] for i in range(4)]
                x = proj[:, GQ + t, 0:NP]
                y = conv[:, t, 0:NP]
                link(ve.tensor_scalar(y, x, w[3], None, ALU.mult))
                for i in range(3):
                    s = 3 - i
                    ins = ve.scalar_tensor_tensor(out=y[:, s:NP], in0=x[:, 0:NP - s], scalar=w[i], in1=y[:, s:NP],
                                                  op0=ALU.mult, op1=ALU.add)
                    if i < 2:
                        link(ins)
                    else:
                        signal(ins, "conv_ready")
                ys = conv[:, t, NP:NT]
                link(ve.tensor_scalar(ys, xst[:, t, :, 3], w[3], None, ALU.mult))
                for i in range(3):
                    ins = ve.scalar_tensor_tensor(out=ys, in0=xst[:, t, :, i], scalar=w[i], in1=ys, op0=ALU.mult, op1=ALU.add)
                    if i < 2:
                        link(ins)
                    else:
                        signal(ins, "conv_ready")
            ve.wait_ge(*after("conv_ready", 24))
            for t in range(12):
                ve.wait_ge(*after("csig_ready", t + 1))
                signal(ve.tensor_tensor(conv[:, t, :], conv[:, t, :], nrm[:, t, :], ALU.mult), "silu_ready")
            ve.wait_ge(S("small_loaded"), 112)
            link(ve.tensor_scalar(proj[0:8, AA, :], proj[0:8, AA, :], alog[0:8, 1:2], None, ALU.add))
            link(ve.tensor_scalar(proj[0:8, MQ + 1, :], proj[0:8, AA, :], -1.0, None, ALU.mult))
            signal(ve.tensor_tensor(proj[0:8, MQ, :], proj[0:8, MQ + 1, :], proj[0:8, AA, :], ALU.max), "dtx_ready")
            link(ve.tensor_scalar(proj[0:8, AA, :], proj[0:8, AA, :], 0.0, None, ALU.max))
            ve.wait_ge(*after("softplus_ready", 1))
            link(ve.tensor_tensor(proj[0:8, AA, :], proj[0:8, AA, :], proj[0:8, MQ, :], ALU.add))
            signal(ve.tensor_scalar(proj[0:8, AA, :], proj[0:8, AA, :], alog[0:8, 0:1], -1.0, ALU.mult, ALU.mult), "gT_ready")
            for t in range(8):
                ve.wait_ge(*after("qkroot_ready", t + 1))
                link(ve.reciprocal(nrm[:, t, :], nrm[:, t, :]))
                signal(ve.scalar_tensor_tensor(out=conv[:, t, :], in0=conv[:, t, :], scalar=0.125 if t < 4 else 1.0,
                                               in1=nrm[:, t, :], op0=ALU.mult, op1=ALU.mult), "qk_ready")
            ve.wait_ge(*after("bg_ps", 1))
            signal(ve.tensor_copy(becols[:, :], bank[4][:, 0:16]), "bg_ready")
            signal(ve.tensor_copy(gcols[:, :], bank[4][:, 16:32]), "bg_ready")
            ve.wait_ge(*after("G_ps", 1))
            signal(ve.tensor_copy(Gcols[:, :], bank[5][:, 0:16]), "G_ready")
            ve.wait_ge(*after("G_ready", 1))
            signal(ve.tensor_tensor(eGl[:, :], bank[5][:, 16:32], Gcols[:, :], ALU.subtract), "GL_ready")
            ve.wait_ge(*after("GT_ps", 1))
            signal(ve.tensor_copy(proj[0:8, AA, 0:NP], bank[6][0:8, 0:NP]), "GT_ready")
            ve.wait_ge(*after("BEs_ps", 1))
            signal(ve.tensor_copy(BEs, bank[7][:, 0:32].rearrange("p (a b) -> p a b", a=4)), "BEs_ready")
            dg3 = dg.rearrange("p (h c) -> p h c", h=8)
            d64 = diag64[:, :].unsqueeze(1).to_broadcast([P, 8, 64])
            for a in range(2):
                for w, cols in ((0, Gcols), (1, becols)):
                    if a or w:
                        ve.wait_ge(*after("row_ps", 2 * a + w))
                    signal(ve.tensor_tensor(dg3, d64, bc(cols[:, 8 * a:8 * a + 8].unsqueeze(2), P, 8, 64), ALU.mult), "diag_ready")
                    ve.wait_ge(*after("row_ps", 2 * a + w + 1))
                    if w == 0:
                        g3 = gamT[:, a, :].rearrange("p (h c) -> p h c", h=8)
                        link(ve.tensor_tensor(g3, bank[6][:, :].rearrange("p (h c) -> p h c", h=8),
                                              bc(Gcols[:, 8 * a:8 * a + 8].unsqueeze(2), P, 8, 64), ALU.subtract))
                        ve.sem_inc(S("row_read"), 1)
                        signal(ve.tensor_tensor(g3, g3, incl[:, :].unsqueeze(1).to_broadcast([P, 8, 64]), ALU.add), "gdiff_ready")
                    else:
                        m3 = MT[:, a, :].rearrange("p (h c) -> p h c", h=8)
                        link(ve.tensor_tensor(m3, bank[6][:, :].rearrange("p (h c) -> p h c", h=8),
                                              strict[:, :].unsqueeze(1).to_broadcast([P, 8, 64]), ALU.mult))
                        ve.sem_inc(S("row_read"), 1)
            ve.wait_ge(*after("eG_ready", 1))
            link(ve.tensor_tensor(beG[:, :], becols[:, :], eG[:, :], ALU.mult))
            for a in range(2):
                ve.wait_ge(*after("kk_ps", a + 1))
                ve.wait_ge(*after("gam_ready", a + 1))
                link(ve.tensor_tensor(MT[:, a, :], MT[:, a, :], gamT[:, a, :], ALU.mult))
                for e in range(2):
                    mt, qk, gm = (x[:, a, :].rearrange("p (h e c) -> p h e c", h=4, e=2)[:, :, e, :] for x in (MT, qkT, gamT))
                    kkb, qkb = (bank[4 * a + 2 * m + e][:, 0:256].rearrange("p (h c) -> p h c", h=4) for m in range(2))
                    link(ve.tensor_tensor(mt, mt, kkb, ALU.mult))
                    ins = ve.tensor_tensor(qk, gm, qkb, ALU.mult)
                    if e == 0:
                        link(ins)
                    else:
                        signal(ins, "kk_read")
            for a in range(2):
                ve.wait_ge(*after("kvtok_ps", a + 1))
                k3, v3 = (b[:, :].rearrange("p (h c) -> p h c", h=8) for b in (bank[4], bank[5]))
                for dst, src, cols in ((kbG, k3, beG), (kd, k3, eGl), (vb, v3, becols)):
                    signal(ve.tensor_tensor(dst[:, a, :].rearrange("p (h c) -> p h c", h=8), src,
                                            bc(cols[:, 8 * a:8 * a + 8].unsqueeze(2), P, 8, 64), ALU.mult), "kv_tok")
                signal(ve.tensor_copy(X[:, a, :].rearrange("p (h c) -> p h c", h=8), d64), "kv_tok")
                link(ve.tensor_copy(XT[:, a, :].rearrange("p (h c) -> p h c", h=8), d64))
            ve.wait_ge(*after("ksr_ps", 1))
            link(ve.tensor_copy(ksr[0:8, :], bank[7][0:8, :]))
            for l in range(6):
                for a in range(2):
                    if l:
                        ve.wait_ge(S("T1_ps"), 2 * (l - 1) + a + 1)
                    signal(ve.tensor_tensor(Lm[:, a, :].rearrange("p (h c) -> p h c", h=8), MT[:, a, :].rearrange("p (h c) -> p h c", h=8),
                                            level[:, l * 64:(l + 1) * 64].unsqueeze(1).to_broadcast([P, 8, 64]), ALU.mult), "lvl_ready")
                for a in range(2):
                    ve.wait_ge(S("T1_ps"), 2 * l + a + 1)
                    if l:
                        ve.wait_ge(S("T2_ps"), 2 * (l - 1) + a + 1)
                    signal(ve.tensor_copy(T1[:, a, :], bank[4 + a][:, :]), "T1_ready")
                for a in range(2):
                    ve.wait_ge(S("T2_ps"), 2 * l + a + 1)
                    link(ve.tensor_tensor(X[:, a, :], X[:, a, :], bank[0 + a][:, :], ALU.subtract))
                    signal(ve.tensor_tensor(XT[:, a, :], XT[:, a, :], bank[2 + a][:, :], ALU.subtract), "XT_ready")
            for a in range(2):
                ve.wait_ge(*after("uw_ps", a + 1))
                signal(ve.tensor_copy(usol[:, a, :], bank[4 + a][:, :]), "uw_ready")
            for nn in range(2):
                signal(ve.tensor_copy(wT.rearrange("p h (a n c) -> p h a n c", a=2, n=2)[:, :, :, nn, :],
                                      bank[6 + nn][:, :].rearrange("p (h a c) -> p h a c", h=4, a=2)), "uw_ready")
            ve.wait_ge(*after("EG_ready", 4))
            ve.wait_ge(*after("kk_ps", 2))
            for t in range(4):
                signal(ve.tensor_tensor(conv[:, t, 0:NP], conv[:, t, 0:NP], EG[:, t, 0:NP], ALU.mult), "qg_ready")
            signal(ve.memset(St, 0.0), "state0")
            for c in range(4):
                a, nn = c // 2, c % 2
                o = slice(nn * 64, nn * 64 + 64)
                ve.wait_ge(S("wS_ps"), c + 1)
                if c:
                    ve.wait_ge(S("dS_ps"), c)
                for e in range(2):
                    v3, u3 = (x.rearrange("p (h e c) -> p h e c", h=4, e=2)[o, :, e, :] for x in (vn, usol[:, a, :]))
                    signal(ve.tensor_tensor(v3, u3, bank[4 + e][o, 0:256].rearrange("p (h c) -> p h c", h=4), ALU.subtract), "vn_ready")
                ve.wait_ge(S("dS_ps"), c + 1)
                link(ve.tensor_tensor(St, St, bc(EG[:, :, c * 64 + 63:c * 64 + 64], P, 4, 64), ALU.mult))
                signal(ve.tensor_tensor(St, St, bank[6][:, 0:256].rearrange("p (a b) -> p a b", a=4), ALU.add), "state_ready")
            for t in range(4):
                cs = slice((t % 2) * 256, (t % 2) * 256 + 256)
                link(ve.tensor_copy(oT[:, t, 0:NP], bank[t // 2][:, cs]))
                ins = ve.tensor_tensor(oT[:, t, 0:NP], oT[:, t, 0:NP], bank[2 + t // 2][:, cs], ALU.add)
                if t < 3:
                    link(ins)
                else:
                    signal(ins, "o_read")
            ve.wait_ge(*after("kS_ps", 1))
            link(ve.tensor_tensor(vnT, bank[2][:, 0:32].rearrange("p (a b) -> p a b", a=4), EG[:, :, NP:NT], ALU.mult))
            link(ve.tensor_tensor(vnT, conv[:, 8:12, NP:NT], vnT, ALU.subtract))
            signal(ve.tensor_tensor(vnT, vnT, BEs, ALU.mult), "vnT_ready")
            ve.wait_ge(*after("vnr_ps", 1))
            link(ve.tensor_copy(vnr[0:8, :], bank[3][0:8, :]))
            for hp in range(4):
                if hp:
                    ve.wait_ge(*after("outer_ps", hp))
                for hh in range(2):
                    h = 2 * hp + hh
                    ins = ve.tensor_tensor(vnx[0:8, hh, :].rearrange("p (b v) -> p b v", b=8),
                                           bc(ident[0:8, 0:8].unsqueeze(2), 8, 8, 64),
                                           bc(vnr[0:8, h * 64:(h + 1) * 64].unsqueeze(1), 8, 8, 64), ALU.mult)
                    if hh:
                        signal(ins, "vnx_ready")
                    else:
                        link(ins)
                link(ve.tensor_tensor(sS[:, :, hp, :], sS[:, :, hp, :], bc(EG[:, hp, NP:NT].unsqueeze(2), P, 8, 64), ALU.mult))
                ve.wait_ge(*after("outer_ps", hp + 1))
                signal(ve.tensor_tensor(sS[:, :, hp, :], sS[:, :, hp, :], bank[6 + hp % 2][:, :].rearrange("p (b v) -> p b v", b=8), ALU.add), "sS_ready")
            ve.wait_ge(*after("so_ps", 1))
            for t in range(4):
                signal(ve.tensor_copy(oT[:, t, NP:NT], bank[2][:, t * 8:t * 8 + 8]), "go_ready")
            for t in range(4):
                ve.wait_ge(*after("oroot_ready", t + 1))
                link(ve.reciprocal(nrm[:, 8 + t, :], nrm[:, 8 + t, :]))
                link(ve.tensor_tensor(proj[:, GZ + t, :], proj[:, GZ + t, :], nrm[:, 4 + t, :], ALU.mult))
                link(ve.scalar_tensor_tensor(out=oT[:, t, :], in0=oT[:, t, :], scalar=gnorm[:, 0:1], in1=nrm[:, 8 + t, :],
                                             op0=ALU.mult, op1=ALU.mult))
                signal(ve.tensor_tensor(oT[:, t, :], oT[:, t, :], proj[:, GZ + t, :], ALU.mult), "og_ready")

            i = 0
            for nb in range(3):
                for d in range(KD):
                    ve.wait_ge(S("sgate_ready"), i + 1)
                    ve.wait_ge(S("br_ps"), i + 1)
                    if nb == 0:
                        signal(ve.tensor_tensor(mergedT[:, d, :], sgate[:, i % 2, :], bank[2 + i % 2][:, 0:NT], ALU.mult), "merge_step")
                    else:
                        link(ve.tensor_tensor(gmul[:, i % 2, :], sgate[:, i % 2, :], bank[2 + i % 2][:, 0:NT], ALU.mult))
                        signal(ve.tensor_tensor(mergedT[:, d, :], mergedT[:, d, :], gmul[:, i % 2, :], ALU.add), "merge_step")
                    i += 1
            ve.wait_ge(S("xagain_loaded"), 32)
            for hf in range(2):
                for j, (c0, w) in enumerate(TOK):
                    ve.wait_ge(S("x1_ps"), hf * 3 + j + 1)
                    link(ve.tensor_tensor(acc[0:w, j, hf * 512:(hf + 1) * 512], acc[0:w, j, hf * 512:(hf + 1) * 512],
                                          bank[hf * 3 + j][0:w, :], ALU.add))
            ve.sem_inc(S("x1_ready"), 6)
            for j, (c0, w) in enumerate(TOK):
                ve.wait_ge(*after("root2_ready", j + 1))
                link(ve.reciprocal(rinv[0:w, j:j + 1], rinv[0:w, j:j + 1]))
                ve.wait_ge(S("moe_small"), 16 * 5)
                signal(ve.scalar_tensor_tensor(out=h2[0:w, j, :], in0=acc[0:w, j, :], scalar=rinv[0:w, j:j + 1], in1=gffn[0:w, :],
                                               op0=ALU.mult, op1=ALU.mult), "h2_ready")
            for j, (c0, w) in enumerate(TOK):
                ve.wait_ge(*after("logit_ps", 3))
                lg = logit[0:w, j, :]
                link(ve.tensor_tensor(lg, bank[4][0:w, j * NE:(j + 1) * NE], brt[0:w, :], ALU.add))
                link(ve.max(top8[0:w, :], lg))
                signal(ve.tensor_scalar(cntf[0:w, j:j + 1], top8[0:w, 0:1], -1.0, None, ALU.mult), "lmax_ready")
                gt, eq, cum = rt[0:w, 0, :], rt[0:w, 1, :], rt[0:w, 2, :]
                link(ve.tensor_scalar(gt, lg, top8[0:w, 3:4], None, ALU.is_gt))
                link(ve.tensor_scalar(eq, lg, top8[0:w, 3:4], None, ALU.is_equal))
                link(ve.reduce_sum(cntf[0:w, 4:5], gt, AX))
                link(ve.tensor_scalar(cntf[0:w, 5:6], cntf[0:w, 4:5], -1.0, float(TOPK), ALU.mult, ALU.add))
                link(ve.tensor_tensor_scan(cum, ones[0:w, 0:NE], eq, 0.0, ALU.mult, ALU.add))
                link(ve.tensor_scalar(cum, cum, cntf[0:w, 5:6], None, ALU.is_le))
                link(ve.tensor_tensor(eq, eq, cum, ALU.mult))
                signal(ve.tensor_tensor(sel[0:w, j, :], gt, eq, ALU.add), "sel_ready")
                ve.wait_ge(S("sel_ready"), j + 1)
                ve.wait_ge(*after("pexp_ready", j + 1))
                link(ve.tensor_tensor(prob[0:w, j, :], prob[0:w, j, :], sel[0:w, j, :], ALU.mult))
                link(ve.reduce_sum(cntf[0:w, 6:7], prob[0:w, j, :], AX))
                link(ve.reciprocal(cntf[0:w, 7:8], cntf[0:w, 6:7]))
                signal(ve.tensor_scalar(prob[0:w, j, :], prob[0:w, j, :], cntf[0:w, 7:8], None, ALU.mult), "prob_ready")
            ve.wait_ge(*after("bgu_ps", 1))
            link(ve.tensor_copy(bguT, bank[5][:, :]))
            ve.wait_ge(*after("rank_ps", 1))
            for j, (c0, w) in enumerate(TOK):
                link(ve.tensor_scalar(slotcol[0:w, j, :], bank[6][0:w, j * NE:(j + 1) * NE], 1.0, None, ALU.add))
                link(ve.tensor_tensor(slotcol[0:w, j, :], slotcol[0:w, j, :], sel[0:w, j, :], ALU.mult))
                link(ve.tensor_scalar(slotcol[0:w, j, :], slotcol[0:w, j, :], -1.0, None, ALU.add))
            link(ve.reduce_max(cntf[0:1, 0:1], bank[6][0:1, 3 * NE:4 * NE], AX))
            for m in range(1, MAX_PASSES):
                link(ve.tensor_scalar(cntf[0:1, m:m + 1], cntf[0:1, 0:1], float(m * SLOTS), None, ALU.is_gt))
            link(ve.reduce_sum(cntf[0:1, 6:7], cntf[0:1, 1:MAX_PASSES], AX))
            signal(ve.tensor_scalar(npass[0:1, 0:1], cntf[0:1, 6:7], 1.0, None, ALU.add), "passes_known")
            ve.wait_ge(*after("probT_ps", 1))
            signal(ve.tensor_copy(probT[0:NE, :], bank[7][0:NE, 0:NT]), "probT_ready")
            i = 0
            for j, (c0, w) in enumerate(TOK):
                for hf in range(2):
                    ve.wait_ge(*after("bd_ps", i + 1))
                    signal(ve.tensor_tensor(acc[0:w, j, hf * 512:(hf + 1) * 512], acc[0:w, j, hf * 512:(hf + 1) * 512],
                                            bank[i % 2][0:w, :], ALU.add), "bd_added")
                    i += 1
            ve.wait_ge(*after("bd_added", 6))
            ve.wait_ge(*after("passes_known", 1))
            passes = ve.value_load(npass[0:1, 0:1], min_val=1, max_val=MAX_PASSES)
            ve.sem_inc(S("SwT_ready"), 1)
            ve.sem_inc(S("act_ready"), 1)
            ve.sem_inc(S("y_added"), 1)
            with ve.Fori(0, passes) as q:
                with ve.Fori(0, PAIRS) as p:
                    it = ve.snap(q * PAIRS + p)
                    ve.wait_ge(S("SwT_ps"), it + 1)
                    for j, w in ((slice(0, 2), P), (slice(2, 3), NS)):
                        nj = j.stop - j.start
                        for ee in range(2):
                            at = Z0 + 9024 + j.start * NE
                            sc = A[0:w, bass.DynSlice(p * 2 + (at + ee), 1 if nj == 1 else nj, 1 if nj == 1 else NE)]
                            ve.tensor_tensor(Sg[0:w, j, ee, :], iota_slot[0:w, :].unsqueeze(1).to_broadcast([w, nj, 64]),
                                             bc(sc.unsqueeze(2), w, nj, 64), ALU.is_equal).then_inc(S("Sg_step"), 1)
                    ve.wait_ge(S("Sg_step"), it * 4 + 4)
                    for j, w in ((slice(0, 2), P), (slice(2, 3), NS)):
                        nj = j.stop - j.start
                        for ee in range(2):
                            at = Z0 + 8832 + j.start * NE
                            pr = A[0:w, bass.DynSlice(p * 2 + (at + ee), 1 if nj == 1 else nj, 1 if nj == 1 else NE)]
                            ve.tensor_tensor(Sw[0:w, j, ee, :], Sg[0:w, j, ee, :], bc(pr.unsqueeze(2), w, nj, 64), ALU.mult)\
                                .then_inc(S("Sw_step"), 1)
                    ve.wait_ge(S("Sw_step"), it * 4 + 4)
                    ve.sem_inc(S("slots_built"), 1)
                    ve.wait_ge(S("SwT_ps"), it + 1 + 1)
                    ve.wait_ge(S("add_ps"), it * 6 + 1)
                    ve.tensor_copy(SwT, bank[5][:, 0:NT]).then_inc(S("SwT_ready"), 1)
                    for half in range(2):
                        eb = p * 32 + (Z0 + 7936 + 16 * half)
                        g_b = A[:, bass.DynSlice(eb, 8)]
                        u_b = A[:, bass.DynSlice(eb + 8, 8)]
                        ve.wait_ge(S("ring_free"), (it * 2 + half + 1) * CHUNKS + KD)
                        ve.tensor_tensor(gb, bank[2][:, :].rearrange("p (a b) -> p a b", a=8), bc(g_b.unsqueeze(2), P, 8, 64),
                                         ALU.add).then_inc(S("gb_step"), 1)
                        ve.wait_ge(S("gb_step"), (it * 2 + half) * 2 + 1)
                        ve.tensor_scalar(gb, gb, LIMIT, None, ALU.min).then_inc(S("gate_clipped"), 1)
                        ve.tensor_tensor(ub, bank[3][:, :].rearrange("p (a b) -> p a b", a=8), bc(u_b.unsqueeze(2), P, 8, 64),
                                         ALU.add).then_inc(S("ub_step"), 1)
                        ve.wait_ge(S("ub_step"), (it * 2 + half) * 2 + 1)
                        ve.tensor_scalar(ub, ub, LIMIT, -LIMIT, ALU.min, ALU.max).then_inc(S("ub_step"), 1)
                        ve.wait_ge(S("ub_step"), (it * 2 + half) * 2 + 2)
                        ve.wait_ge(S("moe_sig"), it * 2 + half + 1)
                        ve.scalar_tensor_tensor(out=gb, in0=ub, scalar=1.0, in1=gb, op0=ALU.add, op1=ALU.mult)\
                            .then_inc(S("gb_step"), 1)
                        ve.wait_ge(S("gb_step"), (it * 2 + half) * 2 + 2)
                        ve.tensor_tensor(actT, gb, sg, ALU.mult).then_inc(S("act_ready"), 1)
                        ve.wait_ge(S("act_ready"), it * 2 + half + 1 + 1)
                    i = 0
                    for j, (c0, w) in enumerate(TOK):
                        for hf in range(2):
                            ve.wait_ge(S("add_ps"), it * 6 + i + 1 + 1)
                            ve.tensor_tensor(acc[0:w, j, hf * 512:(hf + 1) * 512], acc[0:w, j, hf * 512:(hf + 1) * 512],
                                             bank[6 + i % 2][0:w, :], ALU.add).then_inc(S("y_added"), 1)
                            i += 1
                    ve.wait_ge(S("y_added"), it * 6 + 6 + 1)
                ve.tensor_scalar(slotcol[:, 0:2, :], slotcol[:, 0:2, :], -float(SLOTS), None, ALU.add).then_inc(S("next_pass"), 1)
                ve.tensor_scalar(slotcol[0:NS, 2, :], slotcol[0:NS, 2, :], -float(SLOTS), None, ALU.add).then_inc(S("next_pass"), 1)
                ve.wait_ge(S("next_pass"), q * 2 + 2)
            ve.sem_inc(S("acc_final"), 1)
            ve.wait_ge(S("gfin_loaded"), 16)
            for j, (c0, w) in enumerate(TOK):
                ve.wait_ge(*after("root3_ready", j + 1))
                link(ve.reciprocal(rinv[0:w, j:j + 1], rinv[0:w, j:j + 1]))
                signal(ve.scalar_tensor_tensor(out=acc[0:w, j, :], in0=acc[0:w, j, :], scalar=rinv[0:w, j:j + 1], in1=gfin[0:w, :],
                                               op0=ALU.mult, op1=ALU.mult), "y_ready")


_INS = ['x_prompt', 'x_sample', 'cache_k', 'cache_v', 'cache_k_idx', 'cache_mem_k', 'cache_mem_v', 'state_gdn', 'state_conv',
        'page_table', 'mem_prompt', 'norm_attn', 'w_in', 'conv_w', 'gdn_a_log', 'gdn_dt_bias', 'gdn_norm', 'norm_mem',
        'w_mem_kv', 'w_branch', 'w_out', 'norm_ffn', 'w_router', 'b_router', 'w_gate_up', 'b_gate_up', 'w_down', 'b_down',
        'norm_final']
_OUTS = [(1, 256, 1024), (8, 1, 1024), (1, 1, 256, 4, 64), (1, 1, 256, 4, 64), (1, 1, 256, 64), (1, 1, 256, 4, 128),
         (1, 1, 256, 4, 128), (1, 1, 8, 64, 64), (1, 1, 3, 1536), (1, 8, 1, 4, 64), (1, 8, 1, 4, 64), (1, 8, 1, 64),
         (1, 8, 8, 64, 64), (1, 8, 3, 1536)]


def kernel(**inputs):
    import numpy as _np
    import concourse.bacc as _bacc
    from concourse import mybir as _mybir
    from concourse.bass_utils import run_bass_kernel_spmd as _run

    nc = _bacc.Bacc("TRN2", target_bir_lowering=False, num_devices=1)
    arrays, args = {}, []
    for name in _INS:
        a = _np.ascontiguousarray(inputs[name])
        arrays[f"in_{name}_dram"] = a
        args.append(nc.dram_tensor(f"in_{name}_dram", a.shape, _mybir.dt.from_np(a.dtype), kind="ExternalInput").ap())
    for i, shape in enumerate(_OUTS):
        args.append(nc.dram_tensor(f"out_{i}_dram", shape, _mybir.dt.float32, kind="ExternalOutput").ap())
    program(nc, *args)
    r = _run(nc, [arrays], core_ids=[0])
    return tuple(r.results[0][f"out_{i}_dram"] for i in range(len(_OUTS)))
```

```python
from contextlib import ExitStack

import concourse.bass as bass
from concourse import mybir

F32 = mybir.dt.float32
I32 = mybir.dt.int32
ALU = mybir.AluOpType
ACT = mybir.ActivationFunctionType
AX = mybir.AxisListType.X

P = 128
D = 1024
KD = D // P
NP, NS = 256, 8
NT = NP + NS
TOK = [(0, P), (P, P), (NP, NS)]
PAST, PAGE, NPAGES, NPOOL = 1024, 128, 8, 80
L = PAST + 1
NEG = -1e30
TAKEN = -3e38
EPS = 1e-6
NE, TOPK, FF = 32, 4, 1024
SLOTS = 64
HALF = FF // 2
CHUNKS = 12
DN = CHUNKS - KD
LIMIT, ALPHA = 7.0, 1.702
TOP_PROMPT, TOP_SAMPLE = 64, 256
MERGE_ORDER = (2, 1, 0)
MAX_PASSES = -(-NT // SLOTS)

C_QKV, C_Z, C_B, C_A, C_DQ, C_DK, C_IQ, C_IK, C_IW, C_MQ, C_G = (
    0, 1536, 2048, 2056, 2064, 2576, 3088, 3344, 3408, 3412, 3924)

IQ, IK, IW, DK, DV, DQ, GQ, GK, GV, GZ, BE, AA, MQ = 0, 2, 3, 4, 6, 8, 12, 16, 20, 24, 28, 29, 30
NTILES = 34

SLOT_W = 528 * KD
RING_SLOTS = 4
KV0 = RING_SLOTS * SLOT_W
KT0 = KV0 + 3 * 2048
RING_END = CHUNKS * 2048
PT0 = RING_END
HT0 = PT0 + NTILES * NT
OT0 = HT0 + KD * NT
Z0 = OT0 + 12 * NT
ARENA = Z0 + 12064
PROB0 = Z0 + 7424
SCOL0 = PROB0 + 3 * (NE + 1)
assert KT0 + 1536 <= RING_END


ORDERS = {
    "te_steps": [
        ("sv_ps", 1), ("xT_ps", 8), ("memT_ps", 8), ("sidx_scores", 1), ("iw_ps", 1), ("sc8_ps", 1),
        ("iscore_ps", 2), ("mkT_ps", 4), ("tok_ps", 3), ("PTm_ps", 1),
        ("smv_step", 8), ("smvT_ps", 1), ("s64_ps", 1), ("PT64_ps", 1), ("sv_step", 8), ("svT_ps", 1), ("cstate_ps", 1), ("crow_ps", 1),
        ("qksum_ps", 8), ("bg_ps", 1), ("G_ps", 1), ("GT_ps", 1), ("EG_ps", 4), ("BEs_ps", 1),
        ("row_ps", 4), ("kk_ps", 2), ("kvtok_ps", 2), ("ksr_ps", 1), ("uw_ps", 2), ("kS_ps", 1),
        ("vnr_ps", 1), ("outer_ps", 4), ("so_ps", 1), ("osum_ps", 4), ("h2T_ps", 8),
        ("logit_ps", 3), ("rank_ps", 1), ("probT_ps", 1), ("bd_ps", 6),
    ],
    "act_steps": [
        ("root_ready", 1), ("relu32_ready", 3), ("mkT_ready", 4), ("tok_ready", 3),
        ("smk_ready", 16), ("sk_ready", 32), ("smv_out", 1), ("sa_exp", 1), ("sv_out", 8), ("csig_ready", 12),
        ("softplus_ready", 1), ("qksq_ready", 8), ("qkroot_ready", 8), ("eG_ready", 1),
        ("EG_ready", 4), ("gam_ready", 2), ("osq_ready", 4), ("oroot_ready", 4), ("root2_ready", 3),
        ("h2T_ready", 8), ("pexp_ready", 3), ("root3_ready", 3),
    ],
    "ve_steps": [
        ("sv_ready", 1), ("x_normed", 5), ("hT_ready", 8), ("memT_ready", 8), ("Qdi_ready", 8),
        ("kiT_ready", 8), ("wmix_ready", 1), ("iwtok_ready", 1), ("sc8_read", 3),
        ("ibias_ready", 2), ("Qm_ready", 1), ("QdT_ready", 1), ("sm_nmax", 1),
        ("sm_p", 1), ("PTm_ready", 1), ("bias8_ready", 1), ("sa_nmax", 1), ("sa_p", 1), ("PT64_ready", 2),
        ("conv_ready", 12), ("so_read", 3), ("crow_ready", 1), ("sconv_ready", 12), ("silu_ready", 12), ("dtx_ready", 1),
        ("gT_ready", 1), ("qk_ready", 8), ("bg_ready", 2), ("G_ready", 1), ("GL_ready", 1),
        ("GT_ready", 1), ("BEs_ready", 1), ("kk_read", 2), ("kv_tok", 8), ("uw_ready", 4), ("qg_ready", 4),
        ("state0", 1), ("o_read", 1), ("vnT_ready", 1), ("go_ready", 4), ("og_ready", 4), ("x1_ready", 6),
        ("h2_ready", 3), ("passes_known", 1), ("probT_ready", 1), ("bd_added", 6), ("acc_final", 1),
        ("y_ready", 3),
    ],
}
SHARED = {}
for _group, _names in ORDERS.items():
    _base = 0
    for _name, _count in _names:
        SHARED[_name] = (_group, _base)
        _base += _count


def program(nc, x_prompt, x_sample, cache_k, cache_v, cache_k_idx, cache_mem_k, cache_mem_v,
            state_gdn, state_conv, page_table, mem_prompt, norm_attn, w_in, conv_w, gdn_a_log,
            gdn_dt_bias, gdn_norm, norm_mem, w_mem_kv, w_branch, w_out, norm_ffn, w_router,
            b_router, w_gate_up, b_gate_up, w_down, b_down, norm_final,
            y_prompt, y_sample, k_prompt, v_prompt, kidx_prompt, memk_prompt, memv_prompt,
            ssm_prompt, conv_prompt, k_sample, v_sample, kidx_sample, ssm_sample, conv_sample):
    ctx = ExitStack()
    with ctx:
        A = ctx.enter_context(nc.sbuf_tensor("arena", [P, ARENA], F32))

        def sb(name, cols, dt=F32):
            return ctx.enter_context(nc.sbuf_tensor(name, [P, cols], dt))

        sems = {}

        def S(name):
            if name in SHARED:
                name = SHARED[name][0]
            if name not in sems:
                sems[name] = ctx.enter_context(nc.semaphore(name))
            return sems[name]

        def after(name, count):
            return S(name), SHARED[name][1] + count

        def area(at, *shape):
            n = 1
            for s in shape:
                n *= s
            v = A[:, at:at + n]
            if len(shape) == 2:
                v = v.rearrange("p (a b) -> p a b", a=shape[0])
            if len(shape) == 3:
                v = v.rearrange("p (a b c) -> p a b c", a=shape[0], b=shape[1])
            return v

        bank = [ctx.enter_context(nc.psum_tensor(f"bank{i}", [P, 512], F32)) for i in range(8)]

        ident = sb("ident", P)
        blockones = sb("blockones", P)
        ones = sb("ones", P)
        before = sb("before", P)
        cumul = sb("cumul", P)
        diag64 = sb("diag64", 64)
        incl = sb("incl", 64)
        strict = sb("strict", 64)
        level = sb("level", 6 * 64)
        headsel = sb("headsel", 512)
        seq64 = sb("seq64", 64)
        seq64t = sb("seq64t", 8)
        head32 = sb("head32", 32)
        seq32t = sb("seq32t", 8)
        iota_slot = sb("iota_slot", P)
        eps = sb("eps", 1)
        xc_i, ec_i, lv_i, slot_i = (area(KT0 + 128 + 64 * i, 64).bitcast(I32) for i in range(4))

        ptab = sb("ptab", 64, I32)
        svec = area(KT0, P)
        svT = sb("svT", 64)
        gnorm = sb("gnorm", 1)
        alog = sb("alog", 2)
        ssq = sb("ssq", 8)
        rinv = sb("rinv", 8)
        iwtok = sb("iwtok", 8)
        wmix = sb("wmix", 8)
        top8 = sb("top8", 8)
        mx = sb("mx", 2)
        nmx = sb("nmx", 2)
        sm = sb("sm", 2)
        rs = sb("rs", 2)
        mx1 = sb("mx1", 4)
        mx2 = area(Z0 + 6024, 4)
        becols = sb("becols", 16)
        gcols = sb("gcols", 16)
        Gcols = sb("Gcols", 16)
        eG = sb("eG", 16)
        eGl = sb("eGl", 16)
        beG = sb("beG", 16)

        slot = [area(s * SLOT_W, SLOT_W) for s in range(RING_SLOTS)]
        kvbuf = [area(KV0 + 2048 * i, 2048) for i in range(3)]
        ktbuf = [area(KT0 + 512 * i, 512) for i in range(3)]
        xraw = area(KV0, 3, 1024)
        memraw = area(KV0 + 3072, 2, 1024)
        sqs = area(KV0 + 5120, 1024)
        proj = area(PT0, NTILES, NT)
        hT = area(HT0, KD, NT)
        oT = area(OT0, 12, NT)

        memT = area(Z0, KD, NP)
        vtok = area(Z0, 3, 256)
        ktok = area(Z0 + 768, 3, 256)
        iktok = area(Z0 + 1536, 3, 64)
        idxc = area(Z0 + 2048, 32, 128)
        smx = area(Z0 + 2048, 2, 256)
        smt = smx[:, 0, :]
        pts = area(Z0 + 2560, 2, 256)
        QdT = area(Z0 + 3072, 16, 64)
        Qm = area(Z0 + 4096, 32, 32)
        S32 = area(Z0 + 5120, 256)
        PT64 = area(Z0 + 5376, 8, 64)
        PTz = area(Z0 + 4096, 16, 64)
        vout = area(Z0 + 2048, 512)
        pnew = area(Z0 + 5952, 8)
        pnewT = area(Z0 + 5960, 64)
        mk = area(Z0 + 6144, 2, 512)
        mv = area(Z0 + 7168, 2, 512)
        mkT = area(Z0 + 8192, 4, 256)
        Qdi = area(Z0 + 9216, 8, 32)
        relu32 = area(Z0 + 9472, L)
        S64 = area(Z0 + 9472, L)
        sc8 = area(Z0 + 10504, L)
        biasP = area(Z0 + 11536, 2, 256)

        conv = area(PT0, 12, NT)
        vb = area(Z0 + 1024, 2, 512)
        kbG = area(Z0 + 2048, 2, 512)
        kd = area(Z0 + 3072, 2, 512)
        gamT = area(Z0 + 4096, 2, 512)
        MT = area(Z0 + 5120, 2, 512)
        qkT = area(Z0 + 6144, 2, 512)
        X = area(Z0 + 7168, 2, 512)
        XT = area(Z0 + 8192, 2, 512)
        T1 = area(Z0 + 9216, 2, 512)
        EG = area(Z0 + 10240, 4, NT)
        St = area(Z0 + 11296, 4, 64)
        vn = area(Z0 + 11552, 512)
        usol = gamT
        dtx = area(Z0 + 7168, NT)
        dtn = area(Z0 + 7168 + NT, NT)
        wT = area(Z0 + 5120, 4, 256)
        nrm = area(PT0 + GQ * NT, 12, NT)
        sS = area(KV0, 8, 4, 64)
        ksr = area(KV0 + 2048, 512)
        Lm = area(KV0 + 2560, 2, 512)
        vnx = area(KV0 + 2560, 2, 8 * 64)
        vnT = area(KV0 + 3584, 4, 8)
        vnr = area(KV0 + 3616, 512)
        BEs = area(KV0 + 4128, 4, 8)
        srow = area(KV0 + 4160, 1536)
        xst = area(KT0, 12, 8, 4)
        dg = area(KT0 + 384, 512)
        conv_rows = area(KV0 + 4160, 1536)

        merged_at = [PT0 + (MQ + d) * NT for d in range(4)] + [Z0 + d * NT for d in range(3)] + [KV0 + 5696]
        mergedT = [area(at, NT) for at in merged_at]
        assert Z0 + 3 * NT <= Z0 + 1024 and KV0 + 5696 + NT <= KT0
        acc = area(Z0 + 2112, 3, 1024)
        sgate = area(KT0 + 896, 2, NT)
        assert KT0 + 896 + 2 * NT <= RING_END
        M0 = PT0
        h2 = area(M0, 3, 1024)
        h2T = area(M0 + 3072, KD, NT)
        xgT = area(M0 + 5184, 4, P)
        xgs = area(M0 + 5696, HALF)
        gate = area(M0 + 6208, HALF)
        up = area(M0 + 6720, HALF)
        sig = area(M0 + 7232, HALF)
        actT = area(M0 + 7744, 4, P)
        yx = area(M0 + 8256, HALF)
        Sg = area(M0 + 8768, 3, SLOTS)
        Sw = area(M0 + 8960, 3, P)
        SwT = area(M0 + 9344, 3 * P)
        brow = area(M0 + 9728, 2 * FF)
        gffn = area(Z0 + 10540, 1024)
        gfin = area(M0 + 12368, 1024)
        assert M0 + 13392 <= Z0, (M0 + 13392, Z0)
        bdn = area(Z0 + 6400, 1024)
        wr = area(Z0 + 8448, KD, NE)
        brt = area(Z0 + 8704, NE)
        logit = area(Z0 + 8736, 3, NE)
        prob = area(PROB0, 3, NE + 1)
        sel = area(Z0 + 8928, 3, NE)
        slotcol = area(SCOL0, 3, NE + 1)
        probT = area(Z0 + 9120, NT)
        rt = area(Z0 + 9384, 4, NE)
        sqs2 = area(Z0 + 9512, 1024)
        npass = sb("npass", 4, I32)
        cntf = sb("cntf", 8)

        ring = area(0, CHUNKS, 2048)
        block = ctx.enter_context(nc.Block())

        def w_cols(w, c0, n):
            return w.rearrange("(k p) n -> p k n", p=P)[:, :, c0:c0 + n]

        pieces = [("idx", w_cols(w_in[0], C_IQ, 324), 324), ("dkv", w_cols(w_in[0], C_DK, 512), 512),
                  ("dq", w_cols(w_in[0], C_DQ, 512), 512), ("mq", w_cols(w_in[0], C_MQ, 512), 512),
                  ("mkw", w_cols(w_mem_kv[0], 0, 512), 512), ("mvw", w_cols(w_mem_kv[0], 512, 512), 512),
                  ("q", w_cols(w_in[0], 0, 512), 512), ("k", w_cols(w_in[0], 512, 512), 512),
                  ("v", w_cols(w_in[0], 1024, 512), 512), ("z", w_cols(w_in[0], C_Z, 528), 528)]
        for n in MERGE_ORDER:
            gates = [(f"g{n}{hf}", w_cols(w_in[0], C_G + n * D + hf * 512, 512), 512) for hf in range(2)]
            pieces += [gates[0], (f"br{n}", None, None), gates[1]]
        pieces += [("wo0", w_cols(w_out[0], 0, 512), 512), ("wo1", w_cols(w_out[0], 512, 512), 512)]
        index = {name: i for i, (name, _, _) in enumerate(pieces)}

        def piece_view(name):
            i = index[name]
            w = pieces[i][2]
            if w is None:
                return slot[i % RING_SLOTS][:, 0:4096].rearrange("p (k n) -> p k n", k=4)
            return slot[i % RING_SLOTS][:, 0:KD * w].rearrange("p (k n) -> p k n", k=KD)

        def wait_piece(eng, name):
            i = index[name]
            eng.wait_ge(S(f"slot{i % RING_SLOTS}_loaded"), 16 * (i // RING_SLOTS + 1))

        units = [("mk", i) for i in range(4)] + [("k", b) for b in range(8)] + \
                [("mv", i) for i in range(4)] + [("v", b) for b in range(8)]

        def wait_unit_used(eng, u):
            kind, i = units[u]
            if kind == "mk":
                eng.wait_ge(S("smk_ps"), 4 * (i + 1))
            elif kind == "k":
                eng.wait_ge(S("sk_ps"), 4 * (i + 1))
            elif kind == "mv":
                eng.wait_ge(*after("smv_step", 2 * (i + 1)))
            else:
                eng.wait_ge(*after("sv_step", i + 1))

        def wait_unit(eng, n):
            per = 16 * NPAGES
            got = sum(32 if units[m][0][0] == "m" else per for m in range(n % 3, n + 1, 3))
            eng.wait_ge(S(f"kv{n % 3}_loaded"), got)

        tiles = [("idx", 0, 128, IQ), ("idx", 128, 128, IQ + 1), ("idx", 256, 64, IK), ("idx", 320, 4, IW),
                 ("dkv", 0, 128, DK), ("dkv", 128, 128, DK + 1), ("dkv", 256, 128, DV), ("dkv", 384, 128, DV + 1)]
        tiles += [("dq", 128 * i, 128, DQ) for i in range(4)]
        tiles += [("mq", 128 * i, 128, MQ + i) for i in range(4)]
        tiles += [("mkw", a, 0, None) for a in range(2)] + [("mvw", a, 0, None) for a in range(2)]
        tiles += [("q", 128 * i, 128, GQ + i) for i in range(4)]
        tiles += [("k", 128 * i, 128, GK + i) for i in range(4)]
        tiles += [("v", 128 * i, 128, GV + i) for i in range(4)]
        tiles += [("z", 128 * i, 128, GZ + i) for i in range(4)]
        tiles += [("z", 512, 8, BE), ("z", 520, 8, AA)]
        n_proj = {}
        for i, (nm, _, _, _) in enumerate(tiles):
            n_proj[nm] = i + 1
        NPROJ = 3

        heads_it = [("mem", a, h) for a in range(2) for h in range(4)] + \
                   [("dsa", a, h) for a in range(2) for h in range(8)]

        def width(it):
            return P if (it[0] == "dsa" and it[1] == 0) else NP

        def merge_banks(i):
            if i < 8:
                return bank[i % 2], bank[6 + i % 2]
            if 12 <= i < 16:
                return bank[4 + i % 2], bank[6 + i % 2]
            return bank[i % 2], bank[2 + i % 2]

        EARLY_ROUNDS = 20
        SM_IT = 8

        @block.sync
        def _(sp):
            sp.dma_start(xraw[:, 0:2, :], x_prompt[0].rearrange("(a p) d -> p a d", p=P)).then_inc(S("x_loaded"), 16)
            sp.dma_start(xraw[0:NS, 2, :], x_sample.rearrange("b o d -> (b o) d")).then_inc(S("x_loaded"), 16)
            sp.dma_start(memraw, mem_prompt[0].rearrange("(a p) d -> p a d", p=P)).then_inc(S("x_loaded"), 16)
            for i, (name, src, w) in enumerate(pieces):
                if i >= RING_SLOTS:
                    old = pieces[i - RING_SLOTS][0]
                    if old in n_proj:
                        sp.wait_ge(S("proj_done"), n_proj[old])
                    else:
                        first = old[0] == "g" and old[-1] == "0"
                        nth = MERGE_ORDER.index(int(old[1] if old[0] == "g" else old[2]))
                        sp.wait_ge(S("br_ps"), KD * nth + (4 if first else KD))
                done = S(f"slot{i % RING_SLOTS}_loaded")
                if name[0:2] == "br":
                    src = w_branch[0, int(name[2])]
                    if name != "br1":
                        sp.dma_start(piece_view(name), src.rearrange("(c p) n -> p c n", p=P)).then_inc(done, 16)
                    else:
                        rows = src.rearrange("(t u j d) n -> u d t j n", t=2, u=2, j=2)
                        for u in range(2):
                            for t in range(2):
                                ins = sp.dma_start(piece_view(name)[u * 64:u * 64 + 64, 2 * t:2 * t + 2, :], rows[u][:, t])
                                ins.then_inc(S("br1_part") if (u, t) != (1, 1) else done, 16)
                else:
                    sp.dma_start(piece_view(name), src).then_inc(done, 16)
            def load_gate_up(v, e):
                for j in range(KD):
                    sp.wait_ge(S("gu_free"), v * KD + (j + 1))
                    sp.dma_start(ring[:, j, :], w_gate_up[0, bass.DynSlice(e, 1), j * P:(j + 1) * P, :]
                                 .rearrange("o p n -> (o p) n")).then_inc(S(f"chunk{j}_loaded"), 16)
                sp.wait_ge(S("bias_ps"), v + 1)
                sp.dma_start(brow[0:1, :], b_gate_up[0, bass.DynSlice(e, 1)]).then_inc(S("brow_loaded"), 16)

            def load_down(v, e):
                for j in range(DN):
                    sp.wait_ge(S("dn_free"), v * DN + (j + 1))
                    r0 = j * 2 * P
                    sp.dma_start(ring[:, KD + j, :].rearrange("p (c n) -> p c n", c=2),
                                 w_down[0, bass.DynSlice(e, 1), r0:r0 + 2 * P, :]
                                 .rearrange("o (c p) n -> p (o c) n", p=P)).then_inc(S(f"chunk{KD + j}_loaded"), 16)

            sp.wait_ge(S("x1_ps"), 6)
            sp.sem_inc(S("gu_free"), KD)
            sp.sem_inc(S("dn_free"), DN)
            sp.sem_inc(S("bias_ps"), 1)
            sp.wait_ge(*after("passes_known", 1))
            passes = sp.value_load(npass[0:1, 0:1], min_val=1, max_val=MAX_PASSES)
            with sp.Fori(0, passes) as q:
                v0 = sp.snap(q * NE)
                load_gate_up(v0, 0)
                with sp.Fori(0, NE - 1) as e:
                    v = sp.snap(q * NE + e)
                    e1 = sp.snap(e + 1)
                    load_gate_up(v + 1, e1)
                    load_down(v, e)
                load_down(v0 + (NE - 1), NE - 1)
            sp.wait_ge(*after("y_ready", 3))
            sp.dma_start(y_prompt[0].rearrange("(a p) d -> p a d", p=P), acc[:, 0:2, :]).then_inc(S("out_written"), 16)
            sp.dma_start(y_sample.rearrange("b o d -> (b o) d"), acc[0:NS, 2, :]).then_inc(S("out_written"), 16)
            sp.wait_ge(S("out_written"), 32)

        @block.gpsimd
        def _(pool):
            n = [0]

            def link(ins):
                n[0] += 1
                ins.then_inc(S("pool_done"), 1)
                pool.wait_ge(S("pool_done"), n[0])

            pool.dma_start(ptab[0:1, :], page_table.rearrange("(o b) n -> o (b n)", o=1)).then_inc(S("ptab_loaded"), 16)
            pool.dma_start(svec[0:8, :], norm_attn.rearrange("o (r c) -> (o r) c", c=P)).then_inc(S("small_loaded"), 16)
            pool.dma_start(svec[8:16, :], norm_mem.rearrange("o (r c) -> (o r) c", c=P)).then_inc(S("small_loaded"), 16)
            pool.dma_start(svec[16:64, :], conv_w[0].rearrange("i (r c) -> (i r) c", c=P)).then_inc(S("small_loaded"), 16)
            pool.dma_start(gnorm[0:64, :], gdn_norm.rearrange("o v -> v o")).then_inc(S("small_loaded"), 16)
            pool.dma_start(gnorm[64:128, :], gdn_norm.rearrange("o v -> v o")).then_inc(S("small_loaded"), 16)
            pool.dma_start(alog[0:8, 0:1], gdn_a_log.rearrange("o v -> v o")).then_inc(S("small_loaded"), 16)
            pool.dma_start(alog[0:8, 1:2], gdn_dt_bias.rearrange("o v -> v o")).then_inc(S("small_loaded"), 16)

            def select(t, op, base, pattern, cm, fill):
                link(pool.affine_select(out=t, in_=t, compare_op=op, fill=fill, base=base, pattern=pattern,
                                        channel_multiplier=cm))

            link(pool.memset(ident[:, :], 0.0))
            select(ident[:, :], ALU.not_equal, 0, [[-1, P]], 1, 1.0)
            pool.wait_ge(S("pool_done"), n[0])
            link(pool.memset(eps[:, :], EPS))
            link(pool.memset(ones[:, :], 1.0))
            pool.sem_inc(S("ident_ready"), 1)
            pool.wait_ge(S("ptab_loaded"), 16)
            with pool.Fori(0, NS) as b:
                for j in range(NPAGES):
                    page = pool.value_load(ptab[0:1, bass.DynSlice(b * NPAGES + j, 1)], min_val=0, max_val=NPOOL - 1)
                    pos = (j % 4) * 2 + j // 4
                    pool.dma_start(A[:, bass.DynSlice(Z0 + 2048 + b * 512 + pos * 64, 64)],
                                   cache_k_idx[0, bass.DynSlice(page, 1)].rearrange("o p n -> (o p) n"))\
                        .then_inc(S("idx_loaded"), 16)
            link(pool.memset(before[:, :], 1.0))
            select(before[:, :], ALU.is_gt, 0, [[1, P]], -1, 0.0)
            link(pool.memset(blockones[:, :], 0.0))
            link(pool.memset(blockones[0:64, 0:64], 1.0))
            link(pool.memset(blockones[64:128, 64:128], 1.0))
            link(pool.tensor_copy(cumul[:, :], blockones[:, :]))
            select(cumul[:, :], ALU.is_ge, 0, [[1, P]], -1, 0.0)
            link(pool.tensor_copy(diag64[0:64, :], ident[0:64, 0:64]))
            link(pool.tensor_copy(diag64[64:128, :], ident[64:128, 64:128]))
            link(pool.memset(incl[:, :], 0.0))
            link(pool.memset(strict[:, :], 1.0))
            for h0 in (0, 64):
                select(incl[h0:h0 + 64, :], ALU.is_ge, 0, [[1, 64]], -1, NEG)
                select(strict[h0:h0 + 64, :], ALU.is_gt, 0, [[1, 64]], -1, 0.0)
            link(pool.memset(headsel[0:8, :], 0.0))
            select(headsel[0:8, :], ALU.not_equal, 0, [[-1, 8], [0, 64]], 1, 1.0)
            link(pool.memset(seq64[0:8, :], 0.0))
            select(seq64[0:8, :], ALU.not_equal, 0, [[-1, 8], [0, 8]], 1, 1.0)
            link(pool.memset(head32[0:4, :], 0.0))
            select(head32[0:4, :], ALU.not_equal, 0, [[0, 8], [-1, 4]], 1, 1.0)
            link(pool.memset(seq64t[0:64, :], 1.0))
            select(seq64t[0:64, :], ALU.is_ge, 0, [[-8, 8]], 1, 0.0)
            select(seq64t[0:64, :], ALU.is_ge, 7, [[8, 8]], -1, 0.0)
            link(pool.memset(seq32t[0:32, :], 1.0))
            select(seq32t[0:32, :], ALU.is_ge, 0, [[-4, 8]], 1, 0.0)
            select(seq32t[0:32, :], ALU.is_ge, 3, [[4, 8]], -1, 0.0)
            link(pool.iota(xc_i[:, :], pattern=[[1, 64]], base=0, channel_multiplier=0))
            link(pool.iota(slot_i[:, :], pattern=[[1, 64]], base=0, channel_multiplier=0))
            link(pool.iota(ec_i[:, :], pattern=[[0, 64]], base=0, channel_multiplier=1))
            pool.sem_inc(S("consts_ready"), 1)
            pool.wait_ge(*after("memT_ready", KD))
            for u, (kind, b) in enumerate(units):
                if u >= 3:
                    wait_unit_used(pool, u - 3)
                buf, done = kvbuf[u % 3], S(f"kv{u % 3}_loaded")
                if kind[0] == "m":
                    src = cache_mem_k if kind == "mk" else cache_mem_v
                    for i in range(2):
                        pool.dma_start(buf[:, i * 1024:(i + 1) * 1024].rearrange("p (a n) -> p a n", a=2),
                                       src[0, 2 * b + i].rearrange("(a p) h d -> p a (h d)", p=P)).then_inc(done, 16)
                else:
                    src = cache_k if kind == "k" else cache_v
                    for j in range(NPAGES):
                        page = pool.value_load(ptab[0:1, b * NPAGES + j:b * NPAGES + j + 1], min_val=0, max_val=NPOOL - 1)
                        pool.dma_start(buf[:, j * 256:(j + 1) * 256],
                                       src[0, bass.DynSlice(page, 1)]
                                       .rearrange("o p h d -> (o p) (h d)")).then_inc(done, 16)
                if u == 2:
                    for a in range(2):
                        pool.wait_ge(S("iscore_ready"), a + 1)
                        pool.affine_select(out=biasP[:, a, :], in_=biasP[:, a, :], compare_op=ALU.is_ge, fill=NEG,
                                           base=a * P, pattern=[[-1, 256]], channel_multiplier=1)\
                            .then_inc(S("iscore_masked"), 1)
                    for a in range(2):
                        pool.wait_ge(*after("ibias_ready", a + 1))
                        pool.affine_select(out=biasP[:, a, :], in_=biasP[:, a, :], compare_op=ALU.is_ge, fill=NEG,
                                           base=a * P, pattern=[[-1, 256]], channel_multiplier=1)\
                            .then_inc(S("ibias_masked"), 1)

            pool.wait_ge(*after("sv_step", NS))
            pool.dma_start(srow[0:24, :], state_conv[0].rearrange("b i c -> (b i) c")).then_inc(S("state_rows"), 16)
            for hh in range(2):
                pool.dma_start(sS[hh * 64:hh * 64 + 64, :, :, :].rearrange("p b h v -> p (b h) v"),
                               state_gdn[0].rearrange("b (h e) k v -> e k (b h) v", e=2)[hh]).then_inc(S("sstate_loaded"), 16)
            pool.dma_start(conv_sample[0, :, 0:2, :], state_conv[0, :, 1:3, :]).then_inc(S("pool_stored"), 16)
            pool.wait_ge(*after("crow_ready", 1))
            pool.dma_start(conv_prompt[0, 0], conv_rows[32:35, :]).then_inc(S("pool_stored"), 16)
            pool.dma_start(conv_sample[0, :, 2, :], conv_rows[35:43, :]).then_inc(S("pool_stored"), 16)
            pool.wait_ge(S("state_ready"), 4)
            for hh in range(2):
                pool.dma_start(ssm_prompt[0, 0].rearrange("(h e) k v -> e k h v", e=2)[hh], St[hh * 64:hh * 64 + 64, :, :])\
                    .then_inc(S("pool_stored"), 16)
            pool.wait_ge(S("sS_ready"), 4)
            for hh in range(2):
                pool.dma_start(ssm_sample[0].rearrange("b (h e) k v -> e k (b h) v", e=2)[hh],
                               sS[hh * 64:hh * 64 + 64, :, :, :].rearrange("p b h v -> p (b h) v")).then_inc(S("pool_stored"), 16)
            pool.wait_ge(*after("og_ready", 4))
            pool.wait_ge(S("pool_stored"), 16 * 7)
            pool.dma_start(acc[:, 0:2, :], x_prompt[0].rearrange("(a p) d -> p a d", p=P)).then_inc(S("xagain_loaded"), 16)
            pool.dma_start(acc[0:NS, 2, :], x_sample.rearrange("b o d -> (b o) d")).then_inc(S("xagain_loaded"), 16)
            pool.dma_start(gffn, norm_ffn[0].partition_broadcast(P)).then_inc(S("moe_small"), 16)
            pool.dma_start(brt, b_router[0].partition_broadcast(P)).then_inc(S("moe_small"), 16)
            pool.dma_start(wr, w_router[0].rearrange("(k p) n -> p k n", p=P)).then_inc(S("moe_small"), 16)
            pool.dma_start(bdn[0:NE, :], b_down[0]).then_inc(S("moe_small"), 16)
            pool.wait_ge(S("x1_ps"), 6)
            pool.dma_start(gfin, norm_final.partition_broadcast(P)).then_inc(S("gfin_loaded"), 16)

        @block.scalar
        def _(act):
            n = [0]

            def link(ins):
                n[0] += 1
                ins.then_inc(S("act_done"), 1)
                act.wait_ge(S("act_done"), n[0])

            def signal(ins, name):
                ins.then_inc(S(name), 1)

            act.wait_ge(S("x_loaded"), 48)
            act.wait_ge(S("ident_ready"), 1)
            for j, (t, m) in enumerate([(xraw[:, 0, :], P), (xraw[:, 1, :], P), (xraw[:, 2, :], NS),
                                        (memraw[:, 0, :], P), (memraw[:, 1, :], P)]):
                link(act.activation(sqs[0:m, :], t[0:m, :], ACT.Square, accum_out=ssq[0:m, j:j + 1]))
            for j, m in enumerate([P, P, NS, P, P]):
                link(act.activation(rinv[0:m, j:j + 1], ssq[0:m, j:j + 1], ACT.Sqrt, bias=eps[0:m, :], scale=1.0 / D))
            act.sem_inc(S("root_ready"), 1)

            def gate_sigmoid(i):
                act.wait_ge(S("gate_ps"), i + 1)
                if i >= 2:
                    act.wait_ge(S("merge_step"), i - 1)
                signal(act.activation(sgate[:, i % 2, :], merge_banks(i)[0][:, 0:NT], ACT.Sigmoid), "sgate_ready")

            def evac(i):
                nm, c, m, dst = tiles[i]
                b = bank[i % NPROJ]
                act.wait_ge(S("proj_done"), i + 1)
                if nm == "mkw" or nm == "mvw":
                    signal(act.activation((mk if nm == "mkw" else mv)[:, c, :], b[:, :], ACT.Copy), "proj_evac")
                elif nm == "idx" and dst == IK:
                    link(act.activation(proj[64:128, IK, :], b[0:64, 0:NT], ACT.Copy))
                    signal(act.activation(proj[0:64, IK, :], b[0:64, 0:NT], ACT.Copy), "proj_evac")
                elif nm == "dq":
                    kv = c // 128
                    t, u = kv // 2, kv % 2
                    link(act.activation(proj[u * 64:u * 64 + 64, DQ + 2 * t, :], b[0:64, 0:NT], ACT.Copy))
                    signal(act.activation(proj[u * 64:u * 64 + 64, DQ + 2 * t + 1, :], b[64:128, 0:NT], ACT.Copy), "proj_evac")
                else:
                    signal(act.activation(proj[0:m, dst, :], b[0:m, 0:NT], ACT.Copy), "proj_evac")

            for i in range(n_proj["dq"]):
                evac(i)
            act.wait_ge(*after("sidx_scores", 1))
            act.activation(relu32[0:32, 0:512], bank[6][0:32, :], ACT.Relu).then_inc(S("relu32_ready"), 1)
            act.activation(relu32[0:32, 512:1024], bank[7][0:32, :], ACT.Relu).then_inc(S("relu32_ready"), 1)
            act.activation(relu32[0:32, 1024:1025], bank[3][0:32, 0:1], ACT.Relu).then_inc(S("relu32_ready"), 1)
            for i in range(n_proj["dq"], n_proj["k"]):
                evac(i)
            act.wait_ge(S("proj_evac"), n_proj["mvw"])
            act.dma_start(memk_prompt[0, 0].rearrange("(a p) h d -> p a (h d)", p=P), mk).then_inc(S("act_stored"), 16)
            act.dma_start(memv_prompt[0, 0].rearrange("(a p) h d -> p a (h d)", p=P), mv).then_inc(S("act_stored"), 16)
            for h in range(4):
                act.wait_ge(*after("mkT_ps", h + 1))
                signal(act.activation(mkT[:, h, :], bank[h % 2][:, 0:256], ACT.Copy), "mkT_ready")
            for a, (c0, w) in enumerate(TOK):
                act.wait_ge(*after("tok_ps", a + 1))
                link(act.activation(ktok[0:w, a, :], bank[6][0:w, 0:256], ACT.Copy))
                link(act.activation(vtok[0:w, a, :], bank[6][0:w, 256:512], ACT.Copy))
                signal(act.activation(iktok[0:w, a, :], bank[7][0:w, 0:64], ACT.Copy), "tok_ready")
            act.wait_ge(*after("tok_ready", 3))
            for dst_p, dst_s, t in ((k_prompt, k_sample, ktok), (v_prompt, v_sample, vtok)):
                act.dma_start(dst_p[0, 0].rearrange("(a p) h d -> p a (h d)", p=P), t[:, 0:2, :]).then_inc(S("act_stored"), 16)
                act.dma_start(dst_s[0].rearrange("b o h d -> (b o) (h d)"), t[0:NS, 2, :]).then_inc(S("act_stored"), 16)
            act.dma_start(kidx_prompt[0, 0].rearrange("(a p) d -> p a d", p=P), iktok[:, 0:2, :]).then_inc(S("act_stored"), 16)
            act.dma_start(kidx_sample[0].rearrange("b o d -> (b o) d"), iktok[0:NS, 2, :]).then_inc(S("act_stored"), 16)

            def exp_it(i):
                act.wait_ge(S("att_nmax"), i + 1)
                w = width(heads_it[i])
                signal(act.activation(smx[:, i % 2, 0:w], smx[:, i % 2, 0:w], ACT.Exp, bias=nmx[:, i % 2:i % 2 + 1],
                                      accum_out=sm[:, i % 2:i % 2 + 1]), "att_exp")

            def out_it(i):
                kind, a, h = heads_it[i]
                act.wait_ge(S("att_o"), i + 1)
                ob = bank[2]
                if kind == "mem":
                    dst, src = oT[:, 8 + h, a * P:(a + 1) * P], ob[:, 0:P]
                else:
                    t, u, j = h // 4, (h // 2) % 2, h % 2
                    dst = oT[u * 64:u * 64 + 64, 4 + 2 * t + j, a * P:(a + 1) * P]
                    src = ob[u * 64:u * 64 + 64, 0:P]
                signal(act.activation(dst, src, ACT.Copy), "att_out")

            def keys_out(m):
                if m < 16:
                    act.wait_ge(S("smk_ps"), m + 1)
                    signal(act.activation(ktbuf[m % 3], bank[m % 2][:, :], ACT.Copy), "smk_ready")
                else:
                    act.wait_ge(S("sk_ps"), m - 15)
                    signal(act.activation(ktbuf[m % 3], bank[m % 2][:, :], ACT.Copy), "sk_ready")

            for i in range(len(heads_it)):
                keys_out(2 * i)
                exp_it(i)
                if i >= 1:
                    out_it(i - 1)
                keys_out(2 * i + 1)
                if i == SM_IT:
                    act.wait_ge(*after("sm_nmax", 1))
                    signal(act.activation(S32[0:32, :], S32[0:32, :], ACT.Exp, bias=mx2[0:32, 1:2], accum_out=mx2[0:32, 2:3]), "sm_exp")
            out_it(len(heads_it) - 1)
            for i in range(n_proj["k"], n_proj["z"]):
                evac(i)
            act.wait_ge(*after("smv_step", 8))
            signal(act.activation(vout, bank[5][:, :], ACT.Copy), "smv_out")
            act.wait_ge(*after("sa_nmax", 1))
            signal(act.activation(S64[0:64, :], S64[0:64, :], ACT.Exp, bias=mx1[0:64, 1:2], accum_out=mx1[0:64, 2:3]), "sa_exp")
            for b in range(NS):
                act.wait_ge(*after("sv_step", b + 1))
                signal(act.activation(vout[:, (b % 2) * 256:(b % 2) * 256 + 256], bank[2 + 2 * (b % 2)][:, 0:256], ACT.Copy), "sv_out")
                gate_sigmoid(b)

            for i in range(8, 11):
                gate_sigmoid(i)
            act.wait_ge(*after("sconv_ready", 12))
            for t in range(12):
                signal(act.activation(nrm[:, t, :], conv[:, t, :], ACT.Sigmoid), "csig_ready")
            gate_sigmoid(11)
            act.wait_ge(S("small_loaded"), 112)
            link(act.activation(proj[0:8, BE, :], proj[0:8, BE, :], ACT.Sigmoid))
            act.wait_ge(*after("dtx_ready", 1))
            link(act.activation(dtx[0:8, :], dtx[0:8, :], ACT.Exp, scale=-1.0))
            link(act.activation(dtx[0:8, :], dtx[0:8, :], ACT.Ln, bias=1.0))
            signal(act.activation(alog[0:8, 0:1], alog[0:8, 0:1], ACT.Exp), "softplus_ready")
            for t in range(8):
                act.wait_ge(*after("silu_ready", t + 1))
                signal(act.activation(nrm[:, t, :], conv[:, t, :], ACT.Square), "qksq_ready")
            for t in range(8):
                act.wait_ge(*after("qksum_ps", t + 1))
                signal(act.activation(nrm[:, t, :], bank[t % 4][:, 0:NT], ACT.Sqrt, bias=eps[:, :]), "qkroot_ready")
            for i in range(12, 16):
                gate_sigmoid(i)
            act.wait_ge(*after("G_ready", 1))
            act.wait_ge(*after("GL_ready", 1))
            link(act.activation(eG[:, :], Gcols[:, :], ACT.Exp))
            signal(act.activation(eGl[:, :], eGl[:, :], ACT.Exp), "eG_ready")
            for hp in range(4):
                act.wait_ge(*after("EG_ps", hp + 1))
                signal(act.activation(EG[:, hp, :], bank[4 + hp % 2][:, 0:NT], ACT.Exp), "EG_ready")
            for a in range(2):
                act.wait_ge(S("gdiff_ready"), a + 1)
                signal(act.activation(gamT[:, a, :], gamT[:, a, :], ACT.Exp), "gam_ready")
            for t in range(4):
                act.wait_ge(*after("go_ready", t + 1))
                link(act.activation(nrm[:, 8 + t, :], oT[:, t, :], ACT.Square))
                signal(act.activation(nrm[:, 4 + t, :], proj[:, GZ + t, :], ACT.Sigmoid), "osq_ready")
            for t in range(4):
                act.wait_ge(*after("osum_ps", t + 1))
                signal(act.activation(nrm[:, 8 + t, :], bank[t][:, 0:NT], ACT.Sqrt, bias=eps[:, :], scale=1.0 / 64), "oroot_ready")

            for i in range(16, 24):
                gate_sigmoid(i)

            for j, (c0, w) in enumerate(TOK):
                act.wait_ge(*after("x1_ready", 2 * (j + 1)))
                link(act.activation(sqs2[0:w, :], acc[0:w, j, :], ACT.Square, accum_out=ssq[0:w, j:j + 1]))
                signal(act.activation(rinv[0:w, j:j + 1], ssq[0:w, j:j + 1], ACT.Sqrt, bias=eps[0:w, :], scale=1.0 / D), "root2_ready")
            for k in range(KD):
                act.wait_ge(*after("h2T_ps", k + 1))
                signal(act.activation(h2T[:, k, :], bank[k % 4][:, 0:NT], ACT.Copy), "h2T_ready")
            for j, (c0, w) in enumerate(TOK):
                act.wait_ge(S("lmax_ready"), j + 1)
                signal(act.activation(prob[0:w, j, 0:NE], logit[0:w, j, :], ACT.Exp, bias=cntf[0:w, j:j + 1]), "pexp_ready")
            act.wait_ge(*after("passes_known", 1))
            passes = act.value_load(npass[0:1, 0:1], min_val=1, max_val=MAX_PASSES)
            act.sem_inc(S("xgT_ready"), 1)

            def rows_out(g):
                act.wait_ge(S("xg_ps"), g + 1)
                act.activation(xgs, bank[0][:, :], ACT.Copy).then_inc(S("xgs_ready"), 1)

            def columns_out(g):
                act.wait_ge(S("xgT_ps"), g + 1)
                act.activation(xgT, bank[1][:, :].rearrange("p (a b) -> p a b", a=4), ACT.Copy).then_inc(S("xgT_ready"), 1)

            def sigmoid(v):
                act.wait_ge(S("gate_clipped"), v + 1)
                act.activation(sig, gate, ACT.Sigmoid, scale=ALPHA).then_inc(S("moe_sig"), 1)

            def act_out(v):
                act.wait_ge(S("actT_ps"), v + 1)
                act.activation(actT, bank[5][:, :].rearrange("p (a b) -> p a b", a=4), ACT.Copy).then_inc(S("actT_ready"), 1)

            def y_out(v):
                act.wait_ge(S("dn_free"), v * DN + 2 * DN)
                act.activation(yx, bank[4][:, :], ACT.Copy).then_inc(S("yx_ready"), 1)

            with act.Fori(0, passes) as q:
                v0, g0 = act.snap(q * NE), act.snap(q * (NE + 1))
                rows_out(g0)
                columns_out(g0)
                rows_out(g0 + 1)
                sigmoid(v0)
                columns_out(g0 + 1)
                with act.Fori(0, NE - 1) as e:
                    v, g = act.snap(q * NE + e), act.snap(q * (NE + 1) + e)
                    act_out(v)
                    rows_out(g + 2)
                    sigmoid(v + 1)
                    columns_out(g + 2)
                    y_out(v)
                act_out(v0 + (NE - 1))
                y_out(v0 + (NE - 1))
            for j, (c0, w) in enumerate(TOK):
                act.wait_ge(*after("acc_final", 1))
                link(act.activation(sqs2[0:w, :], acc[0:w, j, :], ACT.Square, accum_out=ssq[0:w, j:j + 1]))
                signal(act.activation(rinv[0:w, j:j + 1], ssq[0:w, j:j + 1], ACT.Sqrt, bias=eps[0:w, :], scale=1.0 / D), "root3_ready")
            act.wait_ge(S("act_stored"), 16 * 8)

        @block.tensor
        def _(pe):
            def mm(out, lhsT, rhs, start=True, stop=True, **kw):
                return pe.matmul(out, lhsT, rhs, start=start, stop=stop, **kw)

            def tr(out, in_, m):
                return pe.transpose(out, in_, ident[0:m, 0:m])

            pe.wait_ge(S("ident_ready"), 1)
            pe.wait_ge(S("small_loaded"), 112)
            tr(bank[7][:, 0:64], svec[0:64, :], 64).then_inc(S("sv_ps"), 1)
            pe.wait_ge(*after("x_normed", 5))
            pe.wait_ge(*after("sv_ready", 1))
            for k in range(KD):
                for j, (c0, w) in enumerate(TOK):
                    last = tr(bank[k][:, c0:c0 + w], xraw[0:w, j, k * P:(k + 1) * P], w)
                last.then_inc(S("xT_ps"), 1)
            for k in range(KD):
                pe.wait_ge(*after("hT_ready", k + 1))
                for j in range(2):
                    last = tr(bank[k][:, j * P:(j + 1) * P], memraw[:, j, k * P:(k + 1) * P], P)
                last.then_inc(S("memT_ps"), 1)
            pe.wait_ge(*after("memT_ready", KD))

            def project(i):
                nm, c, m, dst = tiles[i]
                if i == 0 or tiles[i - 1][0] != nm:
                    wait_piece(pe, nm)
                if i >= NPROJ:
                    pe.wait_ge(S("proj_evac"), i - NPROJ + 1)
                w = piece_view(nm)
                for k in range(KD):
                    if nm in ("mkw", "mvw"):
                        last = mm(bank[i % NPROJ][:, :], memT[:, k, c * P:(c + 1) * P], w[:, k, :], k == 0, k == KD - 1)
                    else:
                        last = mm(bank[i % NPROJ][0:m, 0:NT], w[:, k, c:c + m], hT[:, k, :], k == 0, k == KD - 1)
                last.then_inc(S("proj_done"), 1)

            def merge(i):
                nb, d = MERGE_ORDER[i // KD], i % KD
                if d == 0:
                    wait_piece(pe, f"br{nb}")
                    if nb == 1:
                        pe.wait_ge(S("br1_part"), 48)
                if d % 4 == 0:
                    wait_piece(pe, f"g{nb}{d // 4}")
                wb, wg = piece_view(f"br{nb}"), piece_view(f"g{nb}{d // 4}")
                gate_bank, br_bank = merge_banks(i)
                if i >= 2:
                    pe.wait_ge(S("sgate_ready"), i - 1)
                for k in range(KD):
                    last = mm(gate_bank[:, 0:NT], wg[:, k, (d % 4) * P:(d % 4 + 1) * P], hT[:, k, :], k == 0, k == KD - 1)
                last.then_inc(S("gate_ps"), 1)
                if i >= 2:
                    pe.wait_ge(S("merge_step"), i - 1)
                for c in range(4):
                    last = mm(br_bank[:, 0:NT], wb[:, c, d * P:(d + 1) * P], oT[:, 4 * nb + c, :], c == 0, c == 3)
                last.then_inc(S("br_ps"), 1)

            for i in range(n_proj["dq"]):
                project(i)
            pe.wait_ge(*after("Qdi_ready", 8))
            pe.wait_ge(S("idx_loaded"), 16 * 64)
            pe.wait_ge(S("consts_ready"), 1)
            pe.wait_ge(S("proj_evac"), n_proj["idx"])
            for b in range(NS):
                if b >= 2:
                    pe.wait_ge(*after("kiT_ready", b - 1))
                for g in range(4):
                    last = tr(bank[4 + b % 2][:, g * P:(g + 1) * P], idxc[:, b * 4 + g, :], P)
                last.then_inc(S("kiT_ps"), 1)
                if b >= 1:
                    _score = b - 1
                    pe.wait_ge(*after("kiT_ready", b))
                    for h in range(2):
                        last = mm(bank[6 + h][0:32, :], Qdi[h * 64:h * 64 + 64, _score, :],
                                  ktbuf[_score % 2][h * 64:h * 64 + 64, :], _score == 0, False)
                    mm(bank[3][0:32, 0:1], Qdi[0:64, _score, :], proj[0:64, IK, NP + _score:NP + _score + 1],
                       _score == 0, False).then_inc(S("sidx_step"), 1)
            pe.wait_ge(*after("kiT_ready", 8))
            for h in range(2):
                mm(bank[6 + h][0:32, :], Qdi[h * 64:h * 64 + 64, 7, :], ktbuf[1][h * 64:h * 64 + 64, :], False, True)
            mm(bank[3][0:32, 0:1], Qdi[0:64, 7, :], proj[0:64, IK, NP + 7:NP + 8], False, True).then_inc(S("sidx_scores"), 1)
            mm(bank[4][0:32, 0:8], head32[0:4, :], proj[0:4, IW, NP:NT])
            for a in range(2):
                last = tr(bank[5][:, 4 * a:4 * a + 4], proj[0:4, IW, a * P:(a + 1) * P], 4)
            last.then_inc(S("iw_ps"), 1)
            pe.wait_ge(*after("relu32_ready", 3))
            pe.wait_ge(*after("iwtok_ready", 1))
            pe.wait_ge(*after("wmix_ready", 1))
            mm(bank[6][0:8, :], wmix[0:32, :], relu32[0:32, 0:512])
            mm(bank[7][0:8, :], wmix[0:32, :], relu32[0:32, 512:1024])
            mm(bank[3][0:8, 0:1], wmix[0:32, :], relu32[0:32, 1024:1025]).then_inc(S("sc8_ps"), 1)
            for a in range(2):
                if a:
                    pe.wait_ge(S("iscore_read"), a)
                for i in range(4):
                    h0 = (i % 2) * 64
                    last = mm(bank[4 + i % 2][:, (i // 2) * 256:(i // 2) * 256 + 256],
                              proj[h0:h0 + 64, IQ + i // 2, a * P:(a + 1) * P], proj[h0:h0 + 64, IK, 0:NP])
                last.then_inc(S("iscore_ps"), 1)
            for i in range(n_proj["dq"], n_proj["k"]):
                project(i)
            pe.wait_ge(S("proj_evac"), n_proj["k"])
            for h in range(4):
                if h >= 2:
                    pe.wait_ge(*after("mkT_ready", h - 1))
                for j in range(2):
                    last = tr(bank[h % 2][:, j * P:(j + 1) * P], mk[:, j, h * P:(h + 1) * P], P)
                last.then_inc(S("mkT_ps"), 1)
            pe.wait_ge(*after("sc8_read", 3))
            for a, (c0, w) in enumerate(TOK):
                if a:
                    pe.wait_ge(*after("tok_ready", a))
                for t in range(2):
                    tr(bank[6][0:w, t * P:(t + 1) * P], proj[:, DK + t, c0:c0 + w], P)
                    tr(bank[6][0:w, 256 + t * P:256 + (t + 1) * P], proj[:, DV + t, c0:c0 + w], P)
                tr(bank[7][0:w, 0:64], proj[0:64, IK, c0:c0 + w], 64).then_inc(S("tok_ps"), 1)

            def scores(i):
                kind, a, h = heads_it[i]
                if i >= 2:
                    pe.wait_ge(S("att_scaled"), i - 1)
                out = bank[4 + i % 2][:, 0:width(heads_it[i])]
                if kind == "mem":
                    m = mm(out, proj[:, MQ + h, a * P:(a + 1) * P], mkT[:, h, :])
                else:
                    t, u, j = h // 4, (h // 2) % 2, h % 2
                    r = slice(u * 64, u * 64 + 64)
                    m = mm(out, proj[r, DQ + 2 * t + j, a * P:(a + 1) * P], proj[r, DK + t, 0:width(heads_it[i])])
                m.then_inc(S("att_s"), 1)

            def mem_scores(m):
                pe.wait_ge(*after("smk_ready", m + 1))
                for j in range(2):
                    h = 2 * (m % 2) + j
                    r = (m // 2) * 4 + h
                    last = mm(bank[3][0:32, 0:256], Qm[:, r, :], ktbuf[m % 3][:, j * 256:(j + 1) * 256],
                              r == 0, r == 31)
                last.then_inc(S("smk_used"), 1)

            def key_scores(m):
                b, t, hf = m // 4, (m // 2) % 2, m % 2
                pe.wait_ge(*after("sk_ready", m + 1))
                if m == 0:
                    pe.wait_ge(S("sm_read"), 1)
                mm(bank[3 + 4 * hf][0:64, :], QdT[:, b * 2 + t, :], ktbuf[(16 + m) % 3], m < 2, False).then_inc(S("sk_used"), 1)

            def sample_step(m):
                if m < 16:
                    b = m // 2
                    if m % 4 == 0:
                        wait_unit(pe, m // 4)
                    if m >= 2:
                        pe.wait_ge(*after("smk_ready", m - 1))
                    src = kvbuf[(m // 4) % 3][:, (b % 2) * 1024:(b % 2) * 1024 + 1024]
                    for j in range(2):
                        h = 2 * (m % 2) + j
                        for c in range(2):
                            last = tr(bank[m % 2][:, j * 256 + c * P:j * 256 + (c + 1) * P],
                                      src[:, c * 512 + h * P:c * 512 + (h + 1) * P], P)
                    last.then_inc(S("smk_ps"), 1)
                else:
                    k = m - 16
                    b, t, hf = k // 4, (k // 2) % 2, k % 2
                    u = 4 + b
                    if k % 4 == 0:
                        wait_unit(pe, u)
                    if k >= 2:
                        pe.wait_ge(*after("sk_ready", k - 1))
                    else:
                        pe.wait_ge(*after("smk_ready", 15 + k))
                    for g in range(4):
                        pg = hf * 4 + g
                        last = tr(bank[k % 2][:, g * P:(g + 1) * P], kvbuf[u % 3][:, pg * 256 + t * P:pg * 256 + (t + 1) * P], P)
                    last.then_inc(S("sk_ps"), 1)
                if 1 <= m <= 16:
                    mem_scores(m - 1)
                elif m > 16:
                    key_scores(m - 17)

            pe.wait_ge(*after("mkT_ready", 4))
            pe.wait_ge(*after("tok_ready", 3))
            pe.wait_ge(S("iscore_read"), 2)
            pe.wait_ge(*after("Qm_ready", 1))
            pe.wait_ge(*after("QdT_ready", 1))
            scores(0)
            for i, (kind, a, h) in enumerate(heads_it):
                if i + 1 < len(heads_it):
                    scores(i + 1)
                sample_step(2 * i)
                nk = width(heads_it[i]) // P
                pe.wait_ge(S("att_p"), i + 1)
                for c in range(nk):
                    last = tr(bank[6][:, c * P:(c + 1) * P], smx[:, i % 2, c * P:(c + 1) * P], P)
                last.then_inc(S("att_pT_ps"), 1)
                sample_step(2 * i + 1)
                pe.wait_ge(S("att_pT"), i + 1)
                if i:
                    pe.wait_ge(S("att_out"), i)
                for c in range(nk):
                    if kind == "mem":
                        last = mm(bank[2][:, 0:P], mv[:, c, h * P:(h + 1) * P], pts[:, i % 2, c * P:(c + 1) * P],
                                  c == 0, c == nk - 1)
                    else:
                        u, kv = (h // 2) % 2, h // 2
                        last = mm(bank[2][u * 64:u * 64 + 64, 0:P], vtok[:, c, kv * 64:kv * 64 + 64],
                                  pts[:, i % 2, c * P:(c + 1) * P], c == 0, c == nk - 1)
                last.then_inc(S("att_o"), 1)
            key_scores(31)
            pe.wait_ge(S("att_out"), len(heads_it))

            pe.wait_ge(*after("sm_p", 1))
            for c in range(2):
                last = tr(bank[0][:, c * 32:(c + 1) * 32], S32[0:32, c * P:(c + 1) * P], 32)
            last.then_inc(S("PTm_ps"), 1)
            for b in range(NS):
                for t in range(2):
                    mm(bank[4][0:64, 0:1], QdT[:, b * 2 + t, :], proj[:, DK + t, NP + b:NP + b + 1], b + t == 0, False)
            pe.wait_ge(*after("PTm_ready", 1))
            late = list(range(n_proj["k"], n_proj["z"]))
            for b in range(NS):
                u = 12 + b // 2
                if b % 2 == 0:
                    wait_unit(pe, u)
                src = kvbuf[u % 3][:, (b % 2) * 1024:(b % 2) * 1024 + 1024]
                for c in range(2):
                    last = mm(bank[5][c * 64:c * 64 + 64, :], PTz[:, c * 8 + b, :], src[:, c * 512:(c + 1) * 512], b == 0, b == 7)
                last.then_inc(S("smv_step"), 1)
                if b % 2 == 1:
                    for i in late[(b // 2) * 3:(b // 2) * 3 + 3]:
                        project(i)
            pe.wait_ge(*after("smv_out", 1))
            for h in range(4):
                last = mm(bank[6][:, h * 32:(h + 1) * 32], vout[:, h * P:(h + 1) * P], diag64[:, 0:32])
            last.then_inc(S("smvT_ps"), 1)
            pe.wait_ge(*after("bias8_ready", 1))
            mm(bank[3][0:64, :], seq64[0:8, :], sc8[0:8, 0:512], False, True)
            mm(bank[7][0:64, :], seq64[0:8, :], sc8[0:8, 512:1024], False, True)
            mm(bank[4][0:64, 0:1], seq64[0:8, :], sc8[0:8, 1024:1025], False, True).then_inc(S("s64_ps"), 1)
            pe.wait_ge(S("proj_evac"), n_proj["z"])
            pe.wait_ge(*after("sa_p", 1))
            for g in range(8):
                tr(bank[0][:, g * 64:(g + 1) * 64], S64[0:64, g * P:(g + 1) * P], 64)
            tr(bank[1][0:8, 0:64], pnew[0:64, :], 64).then_inc(S("PT64_ps"), 1)
            pe.wait_ge(*after("PT64_ready", 2))
            for t in range(2):
                mm(bank[3][:, t * 64:(t + 1) * 64], vtok[0:8, 2, t * P:(t + 1) * P], pnewT[0:8, :], t == 0, False, skip_group_check=True)
            for b in range(NS):
                u = 16 + b
                wait_unit(pe, u)
                if b >= 2:
                    pe.wait_ge(*after("sv_out", b - 1))
                for pg in range(NPAGES):
                    r = slice((pg % 2) * 64, (pg % 2) * 64 + 64)
                    last = mm(bank[2 + 2 * (b % 2)][r, 0:256], PT64[:, pg, :], kvbuf[u % 3][:, pg * 256:(pg + 1) * 256],
                              pg < 2, pg >= NPAGES - 2)
                last.then_inc(S("sv_step"), 1)
                merge(b)
                pe.wait_ge(*after("sv_out", b + 1))
                for t in range(2):
                    last = mm(bank[3][:, t * 64 + b * 8:t * 64 + b * 8 + 8], vout[:, (b % 2) * 256 + t * P:(b % 2) * 256 + (t + 1) * P],
                              diag64[:, b * 8:b * 8 + 8], False, b == NS - 1, skip_group_check=True)
            last.then_inc(S("svT_ps"), 1)

            pe.wait_ge(*after("so_read", 3))
            pe.wait_ge(S("merge_step"), 8)
            pe.wait_ge(S("state_rows"), 16)
            for t in range(12):
                last = tr(bank[4][:, t * 24:(t + 1) * 24], srow[0:24, t * P:(t + 1) * P], 24)
            last.then_inc(S("cstate_ps"), 1)
            for t in range(12):
                last = tr(bank[5 + t // 4][0:11, (t % 4) * P:(t % 4 + 1) * P], proj[:, GQ + t, NP - 3:NT], P)
            last.then_inc(S("crow_ps"), 1)
            for i in range(8, 12):
                merge(i)
            pe.wait_ge(*after("crow_ready", 1))
            pe.wait_ge(S("merge_step"), 12)
            for t in range(8):
                pe.wait_ge(*after("qksq_ready", t + 1))
                if t >= 4:
                    pe.wait_ge(*after("qkroot_ready", t - 3))
                mm(bank[t % 4][:, 0:NT], blockones[:, :], nrm[:, t, :]).then_inc(S("qksum_ps"), 1)
            for i in range(12, 16):
                merge(i)
            pe.wait_ge(S("merge_step"), 16)
            pe.wait_ge(*after("gT_ready", 1))
            for a in range(2):
                tr(bank[4][:, 8 * a:8 * a + 8], proj[0:8, BE, a * P:(a + 1) * P], 8)
                last = tr(bank[4][:, 16 + 8 * a:24 + 8 * a], proj[0:8, AA, a * P:(a + 1) * P], 8)
            last.then_inc(S("bg_ps"), 1)
            pe.wait_ge(*after("bg_ready", 2))
            mm(bank[5][:, 0:16], cumul[:, :], gcols[:, :])
            mm(bank[5][:, 16:32], blockones[:, :], gcols[:, :]).then_inc(S("G_ps"), 1)
            pe.wait_ge(*after("G_ready", 1))
            for a in range(2):
                last = tr(bank[6][0:8, a * P:(a + 1) * P], Gcols[:, 8 * a:8 * a + 8], P)
            last.then_inc(S("GT_ps"), 1)
            pe.wait_ge(*after("GT_ready", 1))
            for hp in range(4):
                if hp >= 2:
                    pe.wait_ge(*after("EG_ready", hp - 1))
                mm(bank[4 + hp % 2][:, 0:NT], headsel[0:8, hp * P:(hp + 1) * P], proj[0:8, AA, :]).then_inc(S("EG_ps"), 1)
            for hp in range(4):
                last = mm(bank[7][:, hp * 8:hp * 8 + 8], headsel[0:8, hp * P:(hp + 1) * P], proj[0:8, BE, NP:NT])
            last.then_inc(S("BEs_ps"), 1)
            for a in range(2):
                for w, name in ((0, "G"), (1, "B")):
                    pe.wait_ge(S("diag_ready"), 2 * a + w + 1)
                    mm(bank[6][:, :], blockones[:, :], dg).then_inc(S("row_ps"), 1)
                    pe.wait_ge(S("row_read"), 2 * a + w + 1)
            pe.wait_ge(*after("EG_ready", 4))
            pe.wait_ge(*after("qk_ready", 8))
            for a in range(2):
                for h in range(8):
                    r = slice((h % 2) * 64, (h % 2) * 64 + 64)
                    for nn in range(2):
                        cs = slice(a * P + nn * 64, a * P + nn * 64 + 64)
                        o = slice(nn * 64, nn * 64 + 64)
                        half = slice((h // 2) * 64, (h // 2) * 64 + 64)
                        mm(bank[4 * a + h % 2][o, half], conv[r, 4 + h // 2, cs], conv[r, 4 + h // 2, cs])
                        last = mm(bank[4 * a + 2 + h % 2][o, half], conv[r, 4 + h // 2, cs], conv[r, h // 2, cs])
                last.then_inc(S("kk_ps"), 1)
            pe.wait_ge(*after("kk_read", 2))
            for a in range(2):
                if a:
                    pe.wait_ge(*after("kv_tok", 4 * a))
                for t in range(4):
                    tr(bank[4][:, t * P:(t + 1) * P], conv[:, 4 + t, a * P:(a + 1) * P], P)
                    last = tr(bank[5][:, t * P:(t + 1) * P], conv[:, 8 + t, a * P:(a + 1) * P], P)
                last.then_inc(S("kvtok_ps"), 1)
            pe.wait_ge(*after("BEs_ready", 1))
            for t in range(4):
                last = tr(bank[7][0:8, t * P:(t + 1) * P], conv[:, 4 + t, NP:NT], P)
            last.then_inc(S("ksr_ps"), 1)
            for l in range(6):
                for a in range(2):
                    pe.wait_ge(S("lvl_ready"), 2 * l + a + 1)
                    if l:
                        pe.wait_ge(S("XT_ready"), 2 * (l - 1) + a + 1)
                    else:
                        pe.wait_ge(*after("kv_tok", 8))
                    for h in range(8):
                        for nn in range(2):
                            o = slice(nn * 64, nn * 64 + 64)
                            hs = slice(h * 64, (h + 1) * 64)
                            last = mm(bank[4 + a][o, hs], Lm[o, a, hs], X[o, a, hs])
                    last.then_inc(S("T1_ps"), 1)
                for a in range(2):
                    pe.wait_ge(S("T1_ready"), 2 * l + a + 1)
                    for h in range(8):
                        for nn in range(2):
                            o = slice(nn * 64, nn * 64 + 64)
                            hs = slice(h * 64, (h + 1) * 64)
                            mm(bank[0 + a][o, hs], XT[o, a, hs], T1[o, a, hs])
                            last = mm(bank[2 + a][o, hs], T1[o, a, hs], XT[o, a, hs])
                    last.then_inc(S("T2_ps"), 1)
            pe.wait_ge(S("XT_ready"), 12)
            for a in range(2):
                for h in range(8):
                    for nn in range(2):
                        o = slice(nn * 64, nn * 64 + 64)
                        hs = slice(h * 64, (h + 1) * 64)
                        r = slice((h % 2) * 64, (h % 2) * 64 + 64)
                        mm(bank[4 + a][o, hs], XT[o, a, hs], vb[o, a, hs])
                        last = mm(bank[6 + nn][r, (h // 2) * P + a * 64:(h // 2) * P + a * 64 + 64], kbG[o, a, hs], XT[o, a, hs])
                last.then_inc(S("uw_ps"), 1)
            for c in range(4):
                a, nn = c // 2, c % 2
                o = slice(nn * 64, nn * 64 + 64)
                cs = slice(c * 64, c * 64 + 64)
                if c == 0:
                    pe.wait_ge(*after("uw_ready", 4))
                    pe.wait_ge(*after("qg_ready", 4))
                    pe.wait_ge(*after("state0", 1))
                else:
                    pe.wait_ge(S("state_ready"), c)
                for h in range(8):
                    r = slice((h % 2) * 64, (h % 2) * 64 + 64)
                    last = mm(bank[4 + h % 2][o, (h // 2) * 64:(h // 2) * 64 + 64], wT[r, h // 2, cs], St[r, h // 2, :])
                last.then_inc(S("wS_ps"), 1)
                pe.wait_ge(S("vn_ready"), 2 * c + 2)
                for h in range(8):
                    r = slice((h % 2) * 64, (h % 2) * 64 + 64)
                    hs = slice(h * 64, (h + 1) * 64)
                    oc = slice(((h // 2) % 2) * 256 + c * 64, ((h // 2) % 2) * 256 + c * 64 + 64)
                    mm(bank[h // 4][r, oc], St[r, h // 2, :], conv[r, h // 2, cs])
                    mm(bank[2 + h // 4][r, oc], vn[o, hs], qkT[o, a, hs])
                    last = mm(bank[6][r, (h // 2) * 64:(h // 2) * 64 + 64], kd[o, a, hs], vn[o, hs])
                last.then_inc(S("dS_ps"), 1)
            pe.wait_ge(*after("o_read", 1))
            pe.wait_ge(S("sstate_loaded"), 32)
            pe.wait_ge(*after("qk_ready", 8))
            for b in range(NS):
                for h in range(8):
                    r = slice((h % 2) * 64, (h % 2) * 64 + 64)
                    last = mm(bank[2][r, (h // 2) * 8 + b:(h // 2) * 8 + b + 1], sS[r, b, h // 2, :],
                              conv[r, 4 + h // 2, NP + b:NP + b + 1])
            last.then_inc(S("kS_ps"), 1)
            pe.wait_ge(*after("vnT_ready", 1))
            for t in range(4):
                last = tr(bank[3][0:8, t * P:(t + 1) * P], vnT[:, t, :], P)
            last.then_inc(S("vnr_ps"), 1)
            for hp in range(4):
                pe.wait_ge(S("vnx_ready"), hp + 1)
                for hh in range(2):
                    h = 2 * hp + hh
                    last = mm(bank[6 + hp % 2][hh * 64:hh * 64 + 64, :], ksr[0:8, h * 64:(h + 1) * 64], vnx[0:8, hh, :])
                last.then_inc(S("outer_ps"), 1)
                pe.wait_ge(S("sS_ready"), hp + 1)
            for b in range(NS):
                for h in range(8):
                    r = slice((h % 2) * 64, (h % 2) * 64 + 64)
                    last = mm(bank[2][r, (h // 2) * 8 + b:(h // 2) * 8 + b + 1], sS[r, b, h // 2, :],
                              conv[r, h // 2, NP + b:NP + b + 1])
            last.then_inc(S("so_ps"), 1)
            pe.wait_ge(*after("go_ready", 4))
            for t in range(4):
                pe.wait_ge(*after("osq_ready", t + 1))
                mm(bank[t][:, 0:NT], blockones[:, :], nrm[:, 8 + t, :]).then_inc(S("osum_ps"), 1)
            pe.wait_ge(*after("og_ready", 4))

            for i in range(16, 24):
                merge(i)
            pe.wait_ge(S("merge_step"), 24)
            for hf in range(2):
                wait_piece(pe, f"wo{hf}")
                w = piece_view(f"wo{hf}")
                for j, (c0, m) in enumerate(TOK):
                    for k in range(KD):
                        last = mm(bank[hf * 3 + j][0:m, :], mergedT[k][:, c0:c0 + m], w[:, k, :], k == 0, k == KD - 1)
                    last.then_inc(S("x1_ps"), 1)
            pe.wait_ge(*after("h2_ready", 3))
            pe.wait_ge(*after("x1_ready", 6))
            for k in range(KD):
                if k >= 4:
                    pe.wait_ge(*after("h2T_ready", k - 3))
                for j, (c0, w) in enumerate(TOK):
                    last = tr(bank[k % 4][:, c0:c0 + w], h2[0:w, j, k * P:(k + 1) * P], w)
                last.then_inc(S("h2T_ps"), 1)
            pe.wait_ge(*after("h2T_ready", KD))
            pe.wait_ge(S("moe_small"), 16 * 4)
            for j, (c0, w) in enumerate(TOK):
                for k in range(KD):
                    last = mm(bank[4][0:w, j * NE:(j + 1) * NE], h2T[:, k, c0:c0 + w], wr[:, k, :], k == 0, k == KD - 1)
                last.then_inc(S("logit_ps"), 1)
            pe.wait_ge(S("sel_ready"), 3)
            mm(bank[6][:, 0:NE], before[:, :], sel[:, 0, :])
            mm(bank[6][:, NE:2 * NE], before[:, :], sel[:, 1, :], True, False)
            mm(bank[6][:, NE:2 * NE], ones[:, :], sel[:, 0, :], False, True)
            mm(bank[6][0:NS, 2 * NE:3 * NE], before[0:NS, 0:NS], sel[0:NS, 2, :], True, False)
            mm(bank[6][0:NS, 2 * NE:3 * NE], ones[:, 0:NS], sel[:, 0, :], False, False)
            mm(bank[6][0:NS, 2 * NE:3 * NE], ones[:, 0:NS], sel[:, 1, :], False, True)
            mm(bank[6][0:1, 3 * NE:4 * NE], ones[:, 0:1], sel[:, 0, :], True, False)
            mm(bank[6][0:1, 3 * NE:4 * NE], ones[:, 0:1], sel[:, 1, :], False, False)
            mm(bank[6][0:1, 3 * NE:4 * NE], ones[0:NS, 0:1], sel[0:NS, 2, :], False, True).then_inc(S("rank_ps"), 1)
            pe.wait_ge(S("prob_ready"), 3)
            for j, (c0, w) in enumerate(TOK):
                last = tr(bank[7][0:NE, c0:c0 + w], prob[0:w, j, 0:NE], w)
            last.then_inc(S("probT_ps"), 1)
            pe.wait_ge(*after("probT_ready", 1))
            i = 0
            for j, (c0, w) in enumerate(TOK):
                for hf in range(2):
                    if i >= 2:
                        pe.wait_ge(*after("bd_added", i - 1))
                    mm(bank[i % 2][0:w, :], probT[0:NE, c0:c0 + w], bdn[0:NE, hf * 512:(hf + 1) * 512]).then_inc(S("bd_ps"), 1)
                    i += 1
            pe.wait_ge(*after("bd_added", 6))
            pe.wait_ge(*after("passes_known", 1))
            passes = pe.value_load(npass[0:1, 0:1], min_val=1, max_val=MAX_PASSES)
            pe.sem_inc(S("SwT_ps"), 1)

            half_rows = (slice(0, SLOTS), slice(SLOTS, P))

            def gather(g):
                pe.wait_ge(S("Sg_ready"), g + 1)
                for j, (c0, w) in enumerate(TOK):
                    for hf in range(2):
                        last = mm(bank[0][half_rows[hf], :], Sg[0:w, j, :], h2[0:w, j, hf * HALF:(hf + 1) * HALF], j == 0, j == 2)
                last.then_inc(S("xg_ps"), 1)

            def transpose_tokens(g):
                pe.wait_ge(S("xgs_ready"), g + 1)
                pe.wait_ge(S("xgT_ready"), g + 1)
                for j in range(4):
                    last = tr(bank[1][:, j * P:(j + 1) * P], xgs[:, j * P:(j + 1) * P], P)
                last.then_inc(S("xgT_ps"), 1)

            def gate_up(v, g, between):
                pe.wait_ge(S("xgT_ready"), g + 2)
                pe.wait_ge(S("brow_loaded"), (v + 1) * 16)
                quarters = [(m // 2, m % 2, m * HALF) for m in range(4)]
                for gu, hf, c0 in quarters:
                    last = mm(bank[2 + gu][half_rows[hf], :], ones[0:1, 0:SLOTS], brow[0:1, c0:c0 + HALF], True, False)
                last.then_inc(S("bias_ps"), 1)
                for k in range(KD):
                    pe.wait_ge(S(f"chunk{k}_loaded"), (v + 1) * 16)
                    for gu, hf, c0 in quarters:
                        last = mm(bank[2 + gu][half_rows[hf], :], xgT[:, k % 4, (k // 4) * SLOTS:(k // 4 + 1) * SLOTS],
                                  ring[:, k, c0:c0 + HALF], False, k == KD - 1)
                    last.then_inc(S("gu_free"), 1)
                    if k in between:
                        between[k]()

            def transpose_act(v):
                pe.wait_ge(S("act_ready"), v + 1)
                pe.wait_ge(S("SwT_ready"), v + 1)
                for j in range(4):
                    last = tr(bank[5][:, j * P:(j + 1) * P], gate[:, j * P:(j + 1) * P], P)
                last.then_inc(S("actT_ps"), 1)

            def transpose_choice(v):
                pe.wait_ge(S("Sw_ready"), v + 1)
                pe.wait_ge(S("actT_ready"), v + 1)
                for j, (c0, w) in enumerate(TOK):
                    last = tr(bank[5][:, c0:c0 + w], Sw[0:w, j, :], w)
                last.then_inc(S("SwT_ps"), 1)

            def down(v):
                pe.wait_ge(S("actT_ready"), v + 1)
                pe.wait_ge(S("yx_ready"), v + 1)
                for k in range(KD):
                    if k % 2 == 0:
                        pe.wait_ge(S(f"chunk{KD + k // 2}_loaded"), (v + 1) * 16)
                    for hf in range(2):
                        c0 = (k % 2) * D + hf * HALF
                        last = mm(bank[4][half_rows[hf], :], actT[:, k % 4, (k // 4) * SLOTS:(k // 4 + 1) * SLOTS],
                                  ring[:, KD + k // 2, c0:c0 + HALF], k == 0, k == KD - 1)
                    if k % 2 == 1:
                        last.then_inc(S("dn_free"), 1)

            def spread(v, j):
                c0 = TOK[j][0]
                if j == 0:
                    pe.wait_ge(S("yx_ready"), v + 1)
                    pe.wait_ge(S("SwT_ready"), v + 1)
                pe.wait_ge(S("y_added"), v * 6 + (2 * j + 1))
                for hf in range(2):
                    mm(bank[6 + hf][:, :], SwT[half_rows[hf], c0:c0 + P], yx[half_rows[hf], :]).then_inc(S("add_ps"), 1)

            with pe.Fori(0, passes) as q:
                v0, g0 = pe.snap(q * NE), pe.snap(q * (NE + 1))
                gather(g0)
                transpose_tokens(g0)
                gate_up(v0, g0, {6: lambda: gather(g0 + 1)})
                transpose_tokens(g0 + 1)
                with pe.Fori(0, NE - 1) as e:
                    v, g = pe.snap(q * NE + e), pe.snap(q * (NE + 1) + e)
                    transpose_act(v)
                    gate_up(v + 1, g + 1, {0: lambda: spread(v, 0), 1: lambda: spread(v, 1), 2: lambda: spread(v, 2),
                                           4: lambda: transpose_choice(v), 6: lambda: gather(g + 2)})
                    transpose_tokens(g + 2)
                    down(v)
                last_v = v0 + (NE - 1)
                transpose_act(last_v)
                for j in range(3):
                    spread(last_v, j)
                transpose_choice(last_v)
                down(last_v)
            last_v = pe.snap(passes * NE)
            for j in range(3):
                spread(last_v, j)

        @block.vector
        def _(ve):
            n = [0]

            def link(ins):
                n[0] += 1
                ins.then_inc(S("ve_done"), 1)
                ve.wait_ge(S("ve_done"), n[0])

            def signal(ins, name):
                ins.then_inc(S(name), 1)

            def bc(ap, *shape):
                return ap.to_broadcast(list(shape))

            def merge(i):
                at, product, g = mergedT[i % KD], merge_banks(i)[1][:, 0:NT], sgate[:, i % 2, :]
                ve.wait_ge(S("sgate_ready"), i + 1)
                ve.wait_ge(S("br_ps"), i + 1)
                if i < KD:
                    signal(ve.tensor_tensor(at, g, product, ALU.mult), "merge_step")
                else:
                    link(ve.tensor_tensor(g, g, product, ALU.mult))
                    signal(ve.tensor_tensor(at, at, g, ALU.add), "merge_step")

            ve.wait_ge(*after("sv_ps", 1))
            signal(ve.tensor_copy(svT[:, :], bank[7][:, 0:64]), "sv_ready")
            ve.wait_ge(*after("root_ready", 1))
            for j, m in enumerate([P, P, NS, P, P]):
                link(ve.reciprocal(rinv[0:m, j:j + 1], rinv[0:m, j:j + 1]))
            for j, (t, m) in enumerate([(xraw[:, 0, :], P), (xraw[:, 1, :], P), (xraw[:, 2, :], NS),
                                        (memraw[:, 0, :], P), (memraw[:, 1, :], P)]):
                signal(ve.tensor_scalar(t[0:m, :], t[0:m, :], rinv[0:m, j:j + 1], None, ALU.mult), "x_normed")
            ve.wait_ge(*after("sv_ready", 1))
            for k in range(KD):
                ve.wait_ge(*after("xT_ps", k + 1))
                signal(ve.tensor_scalar(hT[:, k, :], bank[k][:, 0:NT], svT[:, k:k + 1], None, ALU.mult), "hT_ready")
            for k in range(KD):
                ve.wait_ge(*after("memT_ps", k + 1))
                signal(ve.tensor_scalar(memT[:, k, :], bank[k][:, 0:NP], svT[:, 8 + k:9 + k], None, ALU.mult), "memT_ready")
            ve.wait_ge(S("consts_ready"), 1)
            link(ve.tensor_copy(iota_slot[:, 0:SLOTS], slot_i[:, :]))
            link(ve.tensor_copy(iota_slot[:, SLOTS:P], slot_i[:, :]))
            ve.wait_ge(S("consts_ready"), 1)
            link(ve.tensor_scalar(ec_i[:, :], ec_i[:, :], 63, None, ALU.bitwise_and))
            link(ve.tensor_tensor(xc_i[:, :], xc_i[:, :], ec_i[:, :], ALU.bitwise_xor))
            for l in range(6):
                link(ve.tensor_scalar(lv_i[:, :], xc_i[:, :], l, None, ALU.logical_shift_right))
                link(ve.tensor_scalar(level[:, l * 64:(l + 1) * 64], lv_i[:, :], 1, None, ALU.is_equal))
                link(ve.tensor_tensor(level[:, l * 64:(l + 1) * 64], level[:, l * 64:(l + 1) * 64], strict[:, :], ALU.mult))
            link(ve.memset(Qdi, 0.0))
            ve.wait_ge(S("proj_evac"), 2)
            for i in range(4):
                s0 = (i % 2) * 64
                for h in range(2):
                    at = Z0 + 9216 + i
                    dst = A[h * 64:h * 64 + 64, at:at + 7 * 36 + 1:36]
                    signal(ve.tensor_copy(dst, proj[s0:s0 + 64, IQ + i // 2, NP:NT]), "Qdi_ready")
            for b in range(NS):
                ve.wait_ge(S("kiT_ps"), b + 1)
                if b >= 2:
                    ve.wait_ge(S("sidx_step"), b - 1)
                signal(ve.tensor_copy(ktbuf[b % 2], bank[4 + b % 2][:, :]), "kiT_ready")
            ve.wait_ge(*after("iw_ps", 1))
            signal(ve.scalar_tensor_tensor(out=wmix[0:32, :], in0=bank[4][0:32, 0:8], scalar=0.0625,
                                           in1=seq32t[0:32, :], op0=ALU.mult, op1=ALU.mult), "wmix_ready")
            signal(ve.tensor_scalar(iwtok[:, :], bank[5][:, 0:8], 0.0625, None, ALU.mult), "iwtok_ready")
            ve.wait_ge(*after("sc8_ps", 1))
            signal(ve.tensor_scalar(sc8[0:8, 0:512], bank[6][0:8, :], 0.0, None, ALU.add), "sc8_read")
            signal(ve.tensor_scalar(sc8[0:8, 512:1024], bank[7][0:8, :], 0.0, None, ALU.add), "sc8_read")
            signal(ve.tensor_scalar(sc8[0:8, 1024:1025], bank[3][0:8, 0:1], 0.0, None, ALU.add), "sc8_read")
            for a in range(2):
                ve.wait_ge(*after("iscore_ps", a + 1))
                for i in range(4):
                    src = bank[4 + i % 2][:, (i // 2) * 256:(i // 2) * 256 + 256]
                    dst = biasP[:, a, :] if i == 0 else smt
                    link(ve.tensor_scalar(dst, src, 0.0, iwtok[:, 4 * a + i:4 * a + i + 1], ALU.max, ALU.mult))
                    if i in (1, 2):
                        link(ve.tensor_tensor(biasP[:, a, :], biasP[:, a, :], smt, ALU.add))
                    if i == 3:
                        ve.sem_inc(S("iscore_read"), 1)
                        link(ve.tensor_tensor(biasP[:, a, :], biasP[:, a, :], smt, ALU.add))
                        signal(ve.tensor_scalar(biasP[:, a, :], biasP[:, a, :], 0.0, None, ALU.add), "iscore_ready")
            for a in range(2):
                ve.wait_ge(S("iscore_masked"), a + 1)
                for r in range(TOP_PROMPT // 8):
                    link(ve.max(top8[:, :], biasP[:, a, :]))
                    link(ve.match_replace(biasP[:, a, :], top8[:, :], biasP[:, a, :], TAKEN))
                signal(ve.tensor_scalar(biasP[:, a, :], biasP[:, a, :], -2.9e38, NEG, ALU.is_gt, ALU.mult), "ibias_ready")
            ve.wait_ge(*after("sc8_read", 3))

            def take_eight(rounds):
                for r in range(rounds):
                    link(ve.max(top8[0:8, :], sc8[0:8, :]))
                    link(ve.match_replace(sc8[0:8, :], top8[0:8, :], sc8[0:8, :], TAKEN))

            take_eight(EARLY_ROUNDS)

            ve.wait_ge(S("proj_evac"), n_proj["mq"])
            link(ve.memset(Qm, 0.0))
            for h in range(4):
                at = Z0 + 4096 + h * 33
                ins = ve.tensor_copy(A[:, at:at + 7 * 132 + 1:132], proj[:, MQ + h, NP:NT])
                if h < 3:
                    link(ins)
                else:
                    signal(ins, "Qm_ready")
            link(ve.memset(QdT, 0.0))
            for t in range(2):
                for u in range(2):
                    for j in range(2):
                        at = Z0 + 3072 + t * 64 + 4 * t + 2 * u + j
                        ins = ve.tensor_copy(A[u * 64:u * 64 + 64, at:at + 7 * 136 + 1:136],
                                             proj[u * 64:u * 64 + 64, DQ + 2 * t + j, NP:NT])
                        if (t, u, j) == (1, 1, 1):
                            signal(ins, "QdT_ready")
                        else:
                            link(ins)

            ve.wait_ge(S("ibias_masked"), 2)

            def scale(i):
                kind, a, h = heads_it[i]
                w = width(heads_it[i])
                ve.wait_ge(S("att_s"), i + 1)
                if i >= 2:
                    ve.wait_ge(S("att_pT_ps"), i - 1)
                src = bank[4 + i % 2][:, 0:w]
                if kind == "mem":
                    signal(ve.tensor_scalar(smx[:, i % 2, :], src, P ** -0.5, None, ALU.mult), "att_scaled")
                else:
                    signal(ve.scalar_tensor_tensor(out=smx[:, i % 2, 0:w], in0=src, scalar=64 ** -0.5, in1=biasP[:, a, 0:w],
                                                   op0=ALU.mult, op1=ALU.add), "att_scaled")
                ve.wait_ge(S("att_scaled"), i + 1)
                link(ve.reduce_max(mx[:, i % 2:i % 2 + 1], smx[:, i % 2, 0:w], AX))
                signal(ve.tensor_scalar(nmx[:, i % 2:i % 2 + 1], mx[:, i % 2:i % 2 + 1], -1.0, None, ALU.mult), "att_nmax")

            def norm(i):
                w = width(heads_it[i])
                ve.wait_ge(S("att_exp"), i + 1)
                link(ve.reciprocal(rs[:, i % 2:i % 2 + 1], sm[:, i % 2:i % 2 + 1]))
                signal(ve.tensor_scalar(smx[:, i % 2, 0:w], smx[:, i % 2, 0:w], rs[:, i % 2:i % 2 + 1], None, ALU.mult), "att_p")

            def ptout(i):
                w = width(heads_it[i])
                ve.wait_ge(S("att_pT_ps"), i + 1)
                if i >= 2:
                    ve.wait_ge(S("att_o"), i - 1)
                signal(ve.tensor_copy(pts[:, i % 2, 0:w], bank[6][:, 0:w]), "att_pT")

            scale(0)
            for i in range(len(heads_it)):
                if i + 1 < len(heads_it):
                    scale(i + 1)
                if i == SM_IT:
                    ve.wait_ge(S("smk_used"), 16)
                    ve.tensor_scalar(S32[0:32, :], bank[3][0:32, 0:256], P ** -0.5, None, ALU.mult).then_inc(S("sm_read"), 1)
                    ve.wait_ge(S("sm_read"), 1)
                    link(ve.reduce_max(mx2[0:32, 0:1], S32[0:32, :], AX))
                    signal(ve.tensor_scalar(mx2[0:32, 1:2], mx2[0:32, 0:1], -1.0, None, ALU.mult), "sm_nmax")
                if i == SM_IT + 1:
                    link(ve.memset(PTz, 0.0))
                if i == SM_IT + 2:
                    ve.wait_ge(S("sm_exp"), 1)
                    link(ve.reciprocal(mx2[0:32, 3:4], mx2[0:32, 2:3]))
                    signal(ve.tensor_scalar(S32[0:32, :], S32[0:32, :], mx2[0:32, 3:4], None, ALU.mult), "sm_p")
                norm(i)
                ptout(i)

            ve.wait_ge(*after("PTm_ps", 1))
            for c in range(2):
                at = Z0 + 4096 + c * 512
                ins = ve.tensor_copy(A[:, at:at + 8 * 68].rearrange("p (b x) -> p b x", x=68)[:, :, 0:4],
                                     bank[0][:, c * 32:(c + 1) * 32].rearrange("p (b h) -> p b h", h=4))
                if c:
                    signal(ins, "PTm_ready")
                else:
                    link(ins)
            take_eight(TOP_SAMPLE // 8 - EARLY_ROUNDS)
            signal(ve.tensor_scalar(sc8[0:8, :], sc8[0:8, :], -2.9e38, NEG, ALU.is_gt, ALU.mult), "bias8_ready")
            ve.wait_ge(*after("smvT_ps", 1))
            for h in range(4):
                link(ve.tensor_copy(oT[:, 8 + h, NP:NT], bank[6][:, h * 33:h * 33 + 29:4]))
            ve.wait_ge(*after("s64_ps", 1))
            link(ve.tensor_scalar(S64[0:64, 0:512], bank[3][0:64, :], 0.125, None, ALU.mult))
            link(ve.tensor_scalar(S64[0:64, 512:1024], bank[7][0:64, :], 0.125, None, ALU.mult))
            link(ve.tensor_scalar(S64[0:64, 1024:1025], bank[4][0:64, 0:1], 0.125, None, ALU.mult))
            link(ve.reduce_max(mx1[0:64, 0:1], S64[0:64, :], AX))
            signal(ve.tensor_scalar(mx1[0:64, 1:2], mx1[0:64, 0:1], -1.0, None, ALU.mult), "sa_nmax")
            ve.wait_ge(*after("sa_exp", 1))
            link(ve.reciprocal(mx1[0:64, 3:4], mx1[0:64, 2:3]))
            link(ve.tensor_scalar(S64[0:64, :], S64[0:64, :], mx1[0:64, 3:4], None, ALU.mult))
            signal(ve.tensor_scalar(pnew[0:64, :], seq64t[0:64, :], S64[0:64, 1024:1025], None, ALU.mult), "sa_p")
            ve.wait_ge(*after("PT64_ps", 1))
            signal(ve.tensor_copy(PT64, bank[0][:, :].rearrange("p (a b) -> p a b", a=8)), "PT64_ready")
            signal(ve.tensor_copy(pnewT[0:8, :], bank[1][0:8, 0:64]), "PT64_ready")
            ve.wait_ge(S("proj_evac"), n_proj["z"])
            ve.wait_ge(S("act_stored"), 16 * 8)
            for t in range(12):
                if t % 3 > 0:
                    merge(t // 3 * 2 + t % 3 - 1)
                w = [svT[:, 16 + i * 12 + t:17 + i * 12 + t] for i in range(4)]
                x = proj[:, GQ + t, 0:NP]
                y = conv[:, t, 0:NP]
                link(ve.tensor_scalar(y, x, w[3], None, ALU.mult))
                for i in range(3):
                    s = 3 - i
                    ins = ve.scalar_tensor_tensor(out=y[:, s:NP], in0=x[:, 0:NP - s], scalar=w[i], in1=y[:, s:NP],
                                                  op0=ALU.mult, op1=ALU.add)
                    if i < 2:
                        link(ins)
                    else:
                        signal(ins, "conv_ready")
            ve.wait_ge(*after("svT_ps", 1))
            for t in range(2):
                for u in range(2):
                    r = slice(u * 64, u * 64 + 64)
                    for j in range(2):
                        c0 = t * 64 + 4 * t + 2 * u + j
                        link(ve.tensor_copy(oT[r, 4 + 2 * t + j, NP:NT], bank[3][r, c0:c0 + 57:8]))
            ve.sem_inc(S("so_read"), 3)

            ve.wait_ge(S("act_stored"), 16 * 8)
            ve.wait_ge(*after("cstate_ps", 1))
            link(ve.tensor_copy(xst[:, :, :, 0:3], bank[4][:, 0:288].rearrange("p (t b i) -> p t b i", t=12, b=8)))
            for t in range(12):
                link(ve.tensor_copy(xst[:, t, :, 3], proj[:, GQ + t, NP:NT]))
            ve.wait_ge(*after("crow_ps", 1))
            for g in range(3):
                link(ve.tensor_copy(conv_rows[32:43, g * 512:(g + 1) * 512], bank[5 + g][0:11, :]))
            ve.sem_inc(S("crow_ready"), 1)
            for t in range(12):
                w = [svT[:, 16 + i * 12 + t:17 + i * 12 + t] for i in range(4)]
                ys = conv[:, t, NP:NT]
                link(ve.tensor_scalar(ys, xst[:, t, :, 3], w[3], None, ALU.mult))
                for i in range(3):
                    ins = ve.scalar_tensor_tensor(out=ys, in0=xst[:, t, :, i], scalar=w[i], in1=ys, op0=ALU.mult, op1=ALU.add)
                    if i < 2:
                        link(ins)
                    else:
                        signal(ins, "sconv_ready")
                if t % 4 == 3:
                    merge(8 + t // 4)
            ve.wait_ge(*after("sconv_ready", 12))
            for t in range(12):
                ve.wait_ge(*after("csig_ready", t + 1))
                signal(ve.tensor_tensor(conv[:, t, :], conv[:, t, :], nrm[:, t, :], ALU.mult), "silu_ready")
            merge(11)
            ve.wait_ge(S("small_loaded"), 112)
            link(ve.tensor_scalar(proj[0:8, AA, :], proj[0:8, AA, :], alog[0:8, 1:2], None, ALU.add))
            link(ve.tensor_scalar(dtn[0:8, :], proj[0:8, AA, :], -1.0, None, ALU.mult))
            signal(ve.tensor_tensor(dtx[0:8, :], dtn[0:8, :], proj[0:8, AA, :], ALU.max), "dtx_ready")
            link(ve.tensor_scalar(proj[0:8, AA, :], proj[0:8, AA, :], 0.0, None, ALU.max))
            ve.wait_ge(*after("softplus_ready", 1))
            link(ve.tensor_tensor(proj[0:8, AA, :], proj[0:8, AA, :], dtx[0:8, :], ALU.add))
            signal(ve.tensor_scalar(proj[0:8, AA, :], proj[0:8, AA, :], alog[0:8, 0:1], -1.0, ALU.mult, ALU.mult), "gT_ready")
            for t in range(8):
                ve.wait_ge(*after("qkroot_ready", t + 1))
                link(ve.reciprocal(nrm[:, t, :], nrm[:, t, :]))
                signal(ve.scalar_tensor_tensor(out=conv[:, t, :], in0=conv[:, t, :], scalar=0.125 if t < 4 else 1.0,
                                               in1=nrm[:, t, :], op0=ALU.mult, op1=ALU.mult), "qk_ready")
                if t in (3, 5, 7):
                    merge(12 + (t - 3) // 2)
            merge(15)
            ve.wait_ge(*after("bg_ps", 1))
            signal(ve.tensor_copy(becols[:, :], bank[4][:, 0:16]), "bg_ready")
            signal(ve.tensor_copy(gcols[:, :], bank[4][:, 16:32]), "bg_ready")
            ve.wait_ge(*after("G_ps", 1))
            signal(ve.tensor_copy(Gcols[:, :], bank[5][:, 0:16]), "G_ready")
            ve.wait_ge(*after("G_ready", 1))
            signal(ve.tensor_tensor(eGl[:, :], bank[5][:, 16:32], Gcols[:, :], ALU.subtract), "GL_ready")
            ve.wait_ge(*after("GT_ps", 1))
            signal(ve.tensor_copy(proj[0:8, AA, 0:NP], bank[6][0:8, 0:NP]), "GT_ready")
            ve.wait_ge(*after("BEs_ps", 1))
            signal(ve.tensor_copy(BEs, bank[7][:, 0:32].rearrange("p (a b) -> p a b", a=4)), "BEs_ready")
            dg3 = dg.rearrange("p (h c) -> p h c", h=8)
            d64 = diag64[:, :].unsqueeze(1).to_broadcast([P, 8, 64])
            for a in range(2):
                for w, cols in ((0, Gcols), (1, becols)):
                    if a or w:
                        ve.wait_ge(*after("row_ps", 2 * a + w))
                    signal(ve.tensor_tensor(dg3, d64, bc(cols[:, 8 * a:8 * a + 8].unsqueeze(2), P, 8, 64), ALU.mult), "diag_ready")
                    ve.wait_ge(*after("row_ps", 2 * a + w + 1))
                    if w == 0:
                        g3 = gamT[:, a, :].rearrange("p (h c) -> p h c", h=8)
                        link(ve.tensor_tensor(g3, bank[6][:, :].rearrange("p (h c) -> p h c", h=8),
                                              bc(Gcols[:, 8 * a:8 * a + 8].unsqueeze(2), P, 8, 64), ALU.subtract))
                        ve.sem_inc(S("row_read"), 1)
                        signal(ve.tensor_tensor(g3, g3, incl[:, :].unsqueeze(1).to_broadcast([P, 8, 64]), ALU.add), "gdiff_ready")
                    else:
                        m3 = MT[:, a, :].rearrange("p (h c) -> p h c", h=8)
                        link(ve.tensor_tensor(m3, bank[6][:, :].rearrange("p (h c) -> p h c", h=8),
                                              strict[:, :].unsqueeze(1).to_broadcast([P, 8, 64]), ALU.mult))
                        ve.sem_inc(S("row_read"), 1)
            ve.wait_ge(*after("eG_ready", 1))
            link(ve.tensor_tensor(beG[:, :], becols[:, :], eG[:, :], ALU.mult))
            for a in range(2):
                ve.wait_ge(*after("kk_ps", a + 1))
                ve.wait_ge(*after("gam_ready", a + 1))
                link(ve.tensor_tensor(MT[:, a, :], MT[:, a, :], gamT[:, a, :], ALU.mult))
                for e in range(2):
                    mt, qk, gm = (x[:, a, :].rearrange("p (h e c) -> p h e c", h=4, e=2)[:, :, e, :] for x in (MT, qkT, gamT))
                    kkb, qkb = (bank[4 * a + 2 * m + e][:, 0:256].rearrange("p (h c) -> p h c", h=4) for m in range(2))
                    link(ve.tensor_tensor(mt, mt, kkb, ALU.mult))
                    ins = ve.tensor_tensor(qk, gm, qkb, ALU.mult)
                    if e == 0:
                        link(ins)
                    else:
                        signal(ins, "kk_read")
            for a in range(2):
                ve.wait_ge(*after("kvtok_ps", a + 1))
                k3, v3 = (b[:, :].rearrange("p (h c) -> p h c", h=8) for b in (bank[4], bank[5]))
                for dst, src, cols in ((kbG, k3, beG), (kd, k3, eGl), (vb, v3, becols)):
                    signal(ve.tensor_tensor(dst[:, a, :].rearrange("p (h c) -> p h c", h=8), src,
                                            bc(cols[:, 8 * a:8 * a + 8].unsqueeze(2), P, 8, 64), ALU.mult), "kv_tok")
                signal(ve.tensor_copy(X[:, a, :].rearrange("p (h c) -> p h c", h=8), d64), "kv_tok")
                link(ve.tensor_copy(XT[:, a, :].rearrange("p (h c) -> p h c", h=8), d64))
            ve.wait_ge(*after("ksr_ps", 1))
            link(ve.tensor_copy(ksr[0:8, :], bank[7][0:8, :]))
            for l in range(6):
                for a in range(2):
                    if l:
                        ve.wait_ge(S("T1_ps"), 2 * (l - 1) + a + 1)
                    signal(ve.tensor_tensor(Lm[:, a, :].rearrange("p (h c) -> p h c", h=8), MT[:, a, :].rearrange("p (h c) -> p h c", h=8),
                                            level[:, l * 64:(l + 1) * 64].unsqueeze(1).to_broadcast([P, 8, 64]), ALU.mult), "lvl_ready")
                for a in range(2):
                    ve.wait_ge(S("T1_ps"), 2 * l + a + 1)
                    if l:
                        ve.wait_ge(S("T2_ps"), 2 * (l - 1) + a + 1)
                    signal(ve.tensor_copy(T1[:, a, :], bank[4 + a][:, :]), "T1_ready")
                for a in range(2):
                    ve.wait_ge(S("T2_ps"), 2 * l + a + 1)
                    link(ve.tensor_tensor(X[:, a, :], X[:, a, :], bank[0 + a][:, :], ALU.subtract))
                    signal(ve.tensor_tensor(XT[:, a, :], XT[:, a, :], bank[2 + a][:, :], ALU.subtract), "XT_ready")
            for a in range(2):
                ve.wait_ge(*after("uw_ps", a + 1))
                signal(ve.tensor_copy(usol[:, a, :], bank[4 + a][:, :]), "uw_ready")
            for nn in range(2):
                signal(ve.tensor_copy(wT.rearrange("p h (a n c) -> p h a n c", a=2, n=2)[:, :, :, nn, :],
                                      bank[6 + nn][:, :].rearrange("p (h a c) -> p h a c", h=4, a=2)), "uw_ready")
            ve.wait_ge(*after("EG_ready", 4))
            ve.wait_ge(*after("kk_ps", 2))
            for t in range(4):
                signal(ve.tensor_tensor(conv[:, t, 0:NP], conv[:, t, 0:NP], EG[:, t, 0:NP], ALU.mult), "qg_ready")
            signal(ve.memset(St, 0.0), "state0")
            for c in range(4):
                a, nn = c // 2, c % 2
                o = slice(nn * 64, nn * 64 + 64)
                ve.wait_ge(S("wS_ps"), c + 1)
                if c:
                    ve.wait_ge(S("dS_ps"), c)
                for e in range(2):
                    v3, u3 = (x.rearrange("p (h e c) -> p h e c", h=4, e=2)[o, :, e, :] for x in (vn, usol[:, a, :]))
                    signal(ve.tensor_tensor(v3, u3, bank[4 + e][o, 0:256].rearrange("p (h c) -> p h c", h=4), ALU.subtract), "vn_ready")
                ve.wait_ge(S("dS_ps"), c + 1)
                link(ve.tensor_tensor(St, St, bc(EG[:, :, c * 64 + 63:c * 64 + 64], P, 4, 64), ALU.mult))
                signal(ve.tensor_tensor(St, St, bank[6][:, 0:256].rearrange("p (a b) -> p a b", a=4), ALU.add), "state_ready")
            for t in range(4):
                cs = slice((t % 2) * 256, (t % 2) * 256 + 256)
                link(ve.tensor_copy(oT[:, t, 0:NP], bank[t // 2][:, cs]))
                ins = ve.tensor_tensor(oT[:, t, 0:NP], oT[:, t, 0:NP], bank[2 + t // 2][:, cs], ALU.add)
                if t < 3:
                    link(ins)
                else:
                    signal(ins, "o_read")
            ve.wait_ge(*after("kS_ps", 1))
            link(ve.tensor_tensor(vnT, bank[2][:, 0:32].rearrange("p (a b) -> p a b", a=4), EG[:, :, NP:NT], ALU.mult))
            link(ve.tensor_tensor(vnT, conv[:, 8:12, NP:NT], vnT, ALU.subtract))
            signal(ve.tensor_tensor(vnT, vnT, BEs, ALU.mult), "vnT_ready")
            ve.wait_ge(*after("vnr_ps", 1))
            link(ve.tensor_copy(vnr[0:8, :], bank[3][0:8, :]))
            for hp in range(4):
                if hp:
                    ve.wait_ge(*after("outer_ps", hp))
                for hh in range(2):
                    h = 2 * hp + hh
                    ins = ve.tensor_tensor(vnx[0:8, hh, :].rearrange("p (b v) -> p b v", b=8),
                                           bc(ident[0:8, 0:8].unsqueeze(2), 8, 8, 64),
                                           bc(vnr[0:8, h * 64:(h + 1) * 64].unsqueeze(1), 8, 8, 64), ALU.mult)
                    if hh:
                        signal(ins, "vnx_ready")
                    else:
                        link(ins)
                link(ve.tensor_tensor(sS[:, :, hp, :], sS[:, :, hp, :], bc(EG[:, hp, NP:NT].unsqueeze(2), P, 8, 64), ALU.mult))
                ve.wait_ge(*after("outer_ps", hp + 1))
                signal(ve.tensor_tensor(sS[:, :, hp, :], sS[:, :, hp, :], bank[6 + hp % 2][:, :].rearrange("p (b v) -> p b v", b=8), ALU.add), "sS_ready")
            ve.wait_ge(*after("so_ps", 1))
            for t in range(4):
                signal(ve.tensor_copy(oT[:, t, NP:NT], bank[2][:, t * 8:t * 8 + 8]), "go_ready")
            for t in range(4):
                ve.wait_ge(*after("oroot_ready", t + 1))
                link(ve.reciprocal(nrm[:, 8 + t, :], nrm[:, 8 + t, :]))
                link(ve.tensor_tensor(proj[:, GZ + t, :], proj[:, GZ + t, :], nrm[:, 4 + t, :], ALU.mult))
                link(ve.scalar_tensor_tensor(out=oT[:, t, :], in0=oT[:, t, :], scalar=gnorm[:, 0:1], in1=nrm[:, 8 + t, :],
                                             op0=ALU.mult, op1=ALU.mult))
                signal(ve.tensor_tensor(oT[:, t, :], oT[:, t, :], proj[:, GZ + t, :], ALU.mult), "og_ready")

            for i in range(16, 24):
                merge(i)
            ve.wait_ge(S("xagain_loaded"), 32)
            for hf in range(2):
                for j, (c0, w) in enumerate(TOK):
                    ve.wait_ge(S("x1_ps"), hf * 3 + j + 1)
                    link(ve.tensor_tensor(acc[0:w, j, hf * 512:(hf + 1) * 512], acc[0:w, j, hf * 512:(hf + 1) * 512],
                                          bank[hf * 3 + j][0:w, :], ALU.add))
            ve.sem_inc(S("x1_ready"), 6)
            for j, (c0, w) in enumerate(TOK):
                ve.wait_ge(*after("root2_ready", j + 1))
                link(ve.reciprocal(rinv[0:w, j:j + 1], rinv[0:w, j:j + 1]))
                ve.wait_ge(S("moe_small"), 16 * 4)
                signal(ve.scalar_tensor_tensor(out=h2[0:w, j, :], in0=acc[0:w, j, :], scalar=rinv[0:w, j:j + 1], in1=gffn[0:w, :],
                                               op0=ALU.mult, op1=ALU.mult), "h2_ready")
            for j, (c0, w) in enumerate(TOK):
                ve.wait_ge(*after("logit_ps", 3))
                lg = logit[0:w, j, :]
                link(ve.tensor_tensor(lg, bank[4][0:w, j * NE:(j + 1) * NE], brt[0:w, :], ALU.add))
                link(ve.max(top8[0:w, :], lg))
                signal(ve.tensor_scalar(cntf[0:w, j:j + 1], top8[0:w, 0:1], -1.0, None, ALU.mult), "lmax_ready")
                gt, eq, cum = rt[0:w, 0, :], rt[0:w, 1, :], rt[0:w, 2, :]
                link(ve.tensor_scalar(gt, lg, top8[0:w, 3:4], None, ALU.is_gt))
                link(ve.tensor_scalar(eq, lg, top8[0:w, 3:4], None, ALU.is_equal))
                link(ve.reduce_sum(cntf[0:w, 4:5], gt, AX))
                link(ve.tensor_scalar(cntf[0:w, 5:6], cntf[0:w, 4:5], -1.0, float(TOPK), ALU.mult, ALU.add))
                link(ve.tensor_tensor_scan(cum, ones[0:w, 0:NE], eq, 0.0, ALU.mult, ALU.add))
                link(ve.tensor_scalar(cum, cum, cntf[0:w, 5:6], None, ALU.is_le))
                link(ve.tensor_tensor(eq, eq, cum, ALU.mult))
                signal(ve.tensor_tensor(sel[0:w, j, :], gt, eq, ALU.add), "sel_ready")
                ve.wait_ge(S("sel_ready"), j + 1)
                ve.wait_ge(*after("pexp_ready", j + 1))
                link(ve.tensor_tensor(prob[0:w, j, 0:NE], prob[0:w, j, 0:NE], sel[0:w, j, :], ALU.mult))
                link(ve.reduce_sum(cntf[0:w, 6:7], prob[0:w, j, 0:NE], AX))
                link(ve.reciprocal(cntf[0:w, 7:8], cntf[0:w, 6:7]))
                signal(ve.tensor_scalar(prob[0:w, j, 0:NE], prob[0:w, j, 0:NE], cntf[0:w, 7:8], None, ALU.mult), "prob_ready")
            ve.wait_ge(*after("rank_ps", 1))
            for j, (c0, w) in enumerate(TOK):
                link(ve.tensor_scalar(slotcol[0:w, j, 0:NE], bank[6][0:w, j * NE:(j + 1) * NE], 1.0, None, ALU.add))
                link(ve.tensor_tensor(slotcol[0:w, j, 0:NE], slotcol[0:w, j, 0:NE], sel[0:w, j, :], ALU.mult))
                link(ve.tensor_scalar(slotcol[0:w, j, 0:NE], slotcol[0:w, j, 0:NE], -1.0, None, ALU.add))
            link(ve.reduce_max(cntf[0:1, 0:1], bank[6][0:1, 3 * NE:4 * NE], AX))
            for m in range(1, MAX_PASSES):
                link(ve.tensor_scalar(cntf[0:1, m:m + 1], cntf[0:1, 0:1], float(m * SLOTS), None, ALU.is_gt))
            link(ve.reduce_sum(cntf[0:1, 6:7], cntf[0:1, 1:MAX_PASSES], AX))
            signal(ve.tensor_scalar(npass[0:1, 0:1], cntf[0:1, 6:7], 1.0, None, ALU.add), "passes_known")
            ve.wait_ge(*after("probT_ps", 1))
            signal(ve.tensor_copy(probT[0:NE, :], bank[7][0:NE, 0:NT]), "probT_ready")
            i = 0
            for j, (c0, w) in enumerate(TOK):
                for hf in range(2):
                    ve.wait_ge(*after("bd_ps", i + 1))
                    signal(ve.tensor_tensor(acc[0:w, j, hf * 512:(hf + 1) * 512], acc[0:w, j, hf * 512:(hf + 1) * 512],
                                            bank[i % 2][0:w, :], ALU.add), "bd_added")
                    i += 1
            ve.wait_ge(*after("bd_added", 6))
            ve.wait_ge(*after("passes_known", 1))
            passes = ve.value_load(npass[0:1, 0:1], min_val=1, max_val=MAX_PASSES)
            link(ve.memset(prob[:, :, NE:NE + 1], 0.0))
            link(ve.memset(slotcol[:, :, NE:NE + 1], -1.0))
            link(ve.memset(yx, 0.0))
            ve.memset(SwT, 0.0).then_inc(S("SwT_ready"), 1)
            ve.sem_inc(S("yx_ready"), 1)
            ve.sem_inc(S("y_added"), 1)
            tiles_of = ((slice(0, 2), P), (slice(2, 3), NS))

            def column(at, j, w, e):
                nj = j.stop - j.start
                return A[0:w, bass.DynSlice(e + (at + j.start * (NE + 1)), nj, NE + 1 if nj > 1 else 1)]

            def choice(e):
                for j, w in tiles_of:
                    nj = j.stop - j.start
                    ve.tensor_tensor(Sg[0:w, j, :], iota_slot[0:w, 0:SLOTS].unsqueeze(1).to_broadcast([w, nj, SLOTS]),
                                     bc(column(SCOL0, j, w, e).unsqueeze(2), w, nj, SLOTS), ALU.is_equal).then_inc(S("Sg_step"), 1)

            def choice_ready(g):
                ve.wait_ge(S("Sg_step"), g * 2 + 2)
                ve.sem_inc(S("Sg_ready"), 1)

            def weighted_choice(v, e):
                ve.wait_ge(S("SwT_ps"), v + 1)
                for j, w in tiles_of:
                    nj = j.stop - j.start
                    ve.tensor_tensor(Sw[0:w, j, :], iota_slot[0:w, :].unsqueeze(1).to_broadcast([w, nj, P]),
                                     bc(column(SCOL0, j, w, e).unsqueeze(2), w, nj, P), ALU.is_equal).then_inc(S("Sw_step"), 1)
                ve.wait_ge(S("Sw_step"), v * 4 + 2)
                for j, w in tiles_of:
                    nj = j.stop - j.start
                    ve.tensor_tensor(Sw[0:w, j, :], Sw[0:w, j, :], bc(column(PROB0, j, w, e).unsqueeze(2), w, nj, P), ALU.mult)\
                        .then_inc(S("Sw_step"), 1)
                ve.wait_ge(S("Sw_step"), v * 4 + 4)
                ve.sem_inc(S("Sw_ready"), 1)

            def SwT_out(v):
                ve.wait_ge(S("SwT_ps"), v + 2)
                ve.tensor_copy(SwT[:, 0:NT], bank[5][:, 0:NT]).then_inc(S("SwT_ready"), 1)

            def activation(v):
                ve.wait_ge(S("gu_free"), v * KD + 2 * KD)
                ve.tensor_scalar(gate, bank[2][:, :], LIMIT, None, ALU.min).then_inc(S("gate_clipped"), 1)
                ve.tensor_scalar(up, bank[3][:, :], LIMIT, -LIMIT, ALU.min, ALU.max).then_inc(S("up_clipped"), 1)
                ve.wait_ge(S("up_clipped"), v + 1)
                ve.wait_ge(S("moe_sig"), v + 1)
                ve.scalar_tensor_tensor(out=gate, in0=up, scalar=1.0, in1=gate, op0=ALU.add, op1=ALU.mult)\
                    .then_inc(S("gated"), 1)
                ve.wait_ge(S("gated"), v + 1)
                ve.tensor_tensor(gate, gate, sig, ALU.mult).then_inc(S("act_ready"), 1)

            def add_outputs(v):
                for j, (c0, w) in enumerate(TOK):
                    for hf in range(2):
                        at = acc[0:w, j, hf * HALF:(hf + 1) * HALF]
                        ve.wait_ge(S("add_ps"), v * 6 + (2 * j + hf + 1))
                        ve.tensor_tensor(at, at, bank[6 + hf][0:w, :], ALU.add).then_inc(S("y_added"), 1)

            with ve.Fori(0, passes) as q:
                v0, g0 = ve.snap(q * NE), ve.snap(q * (NE + 1))
                choice(0)
                choice_ready(g0)
                ve.wait_ge(S("xg_ps"), g0 + 1)
                choice(1)
                choice_ready(g0 + 1)
                activation(v0)
                with ve.Fori(0, NE - 1) as e:
                    v, g = ve.snap(q * NE + e), ve.snap(q * (NE + 1) + e)
                    add_outputs(v)
                    weighted_choice(v, e)
                    ve.wait_ge(S("xg_ps"), g + 2)
                    choice(e + 2)
                    choice_ready(g + 2)
                    SwT_out(v)
                    activation(v + 1)
                last_v = v0 + (NE - 1)
                add_outputs(last_v)
                weighted_choice(last_v, NE - 1)
                SwT_out(last_v)
                ve.wait_ge(S("SwT_ready"), last_v + 2)
                ve.tensor_scalar(slotcol[:, 0:2, :], slotcol[:, 0:2, :], -float(SLOTS), None, ALU.add).then_inc(S("next_pass"), 1)
                ve.tensor_scalar(slotcol[0:NS, 2, :], slotcol[0:NS, 2, :], -float(SLOTS), None, ALU.add).then_inc(S("next_pass"), 1)
                ve.wait_ge(S("next_pass"), q * 2 + 2)
            last_v = ve.snap(passes * NE)
            add_outputs(last_v)
            ve.wait_ge(S("y_added"), last_v * 6 + 7)
            ve.sem_inc(S("acc_final"), 1)
            ve.wait_ge(S("gfin_loaded"), 16)
            for j, (c0, w) in enumerate(TOK):
                ve.wait_ge(*after("root3_ready", j + 1))
                link(ve.reciprocal(rinv[0:w, j:j + 1], rinv[0:w, j:j + 1]))
                signal(ve.scalar_tensor_tensor(out=acc[0:w, j, :], in0=acc[0:w, j, :], scalar=rinv[0:w, j:j + 1], in1=gfin[0:w, :],
                                               op0=ALU.mult, op1=ALU.mult), "y_ready")


_INS = ['x_prompt', 'x_sample', 'cache_k', 'cache_v', 'cache_k_idx', 'cache_mem_k', 'cache_mem_v', 'state_gdn', 'state_conv',
        'page_table', 'mem_prompt', 'norm_attn', 'w_in', 'conv_w', 'gdn_a_log', 'gdn_dt_bias', 'gdn_norm', 'norm_mem',
        'w_mem_kv', 'w_branch', 'w_out', 'norm_ffn', 'w_router', 'b_router', 'w_gate_up', 'b_gate_up', 'w_down', 'b_down',
        'norm_final']
_OUTS = [(1, 256, 1024), (8, 1, 1024), (1, 1, 256, 4, 64), (1, 1, 256, 4, 64), (1, 1, 256, 64), (1, 1, 256, 4, 128),
         (1, 1, 256, 4, 128), (1, 1, 8, 64, 64), (1, 1, 3, 1536), (1, 8, 1, 4, 64), (1, 8, 1, 4, 64), (1, 8, 1, 64),
         (1, 8, 8, 64, 64), (1, 8, 3, 1536)]


def kernel(**inputs):
    import numpy as _np
    import concourse.bacc as _bacc
    from concourse import mybir as _mybir
    from concourse.bass_utils import run_bass_kernel_spmd as _run

    nc = _bacc.Bacc("TRN2", target_bir_lowering=False, num_devices=1)
    arrays, args = {}, []
    for name in _INS:
        a = _np.ascontiguousarray(inputs[name])
        arrays[f"in_{name}_dram"] = a
        args.append(nc.dram_tensor(f"in_{name}_dram", a.shape, _mybir.dt.from_np(a.dtype), kind="ExternalInput").ap())
    for i, shape in enumerate(_OUTS):
        args.append(nc.dram_tensor(f"out_{i}_dram", shape, _mybir.dt.float32, kind="ExternalOutput").ap())
    program(nc, *args)
    r = _run(nc, [arrays], core_ids=[0])
    return tuple(r.results[0][f"out_{i}_dram"] for i in range(len(_OUTS)))
```
